# Optimizing a Trainium2 kernel written in Bass

```python
import jax, jax.numpy as jnp
from jax import lax
import numpy as np

D_MODEL = 1024
BATCH = 1
SEQ = 512
DEPTH = 1

CHUNK = 64
NORM_EPS = 1e-6

GDN_HEADS = 8
GDN_DK = 64
GDN_DV = 64
GDN_QK_W = GDN_HEADS * GDN_DK
GDN_V_W = GDN_HEADS * GDN_DV
GDN_QKV_W = 2 * GDN_QK_W + GDN_V_W
CONV_K = 4

MLA_HEADS = 8
MLA_NOPE = 64
MLA_ROPE = 32
MLA_QK = MLA_NOPE + MLA_ROPE
MLA_V = 64
MLA_V_W = MLA_HEADS * MLA_V
Q_LORA = 384
KV_LORA = 256
ROPE_THETA = 10000.0
Q_BLOCK = 128
MAX_POS_OFFSET = 4096

PEER_HEADS = 8
PEER_DKEY = 256
N_KEYS = 128
N_EXPERTS = N_KEYS * N_KEYS
PEER_TOPK = 16
PEER_TOKEN_BLOCK = 128

IN_SPLITS = (GDN_QKV_W, GDN_V_W, GDN_HEADS, GDN_HEADS, Q_LORA, KV_LORA, MLA_ROPE, 2 * D_MODEL)
IN_TOTAL = sum(IN_SPLITS)

kernel_name = "chunk_causal_gdn_mla_peer_block"

def rms_norm(x, g):
    xf = x.astype(jnp.float32)
    y = xf * lax.rsqrt(jnp.mean(xf * xf, axis=-1, keepdims=True) + NORM_EPS)
    return (y * g.astype(jnp.float32)).astype(x.dtype)

def l2_norm(x):
    xf = x.astype(jnp.float32)
    return xf * lax.rsqrt(jnp.sum(xf * xf, axis=-1, keepdims=True) + NORM_EPS)

def causal_depthwise_conv(x, w):
    c = x.shape[-1]
    return lax.conv_general_dilated(
        x, w[:, None, :].astype(x.dtype), window_strides=(1,), padding=[(CONV_K - 1, 0)],
        dimension_numbers=("NWC", "WIO", "NWC"), feature_group_count=c)

def rope(x, pos):
    half = MLA_ROPE // 2
    inv = jnp.power(ROPE_THETA, -jnp.arange(half, dtype=jnp.float32) / half)
    ang = pos.astype(jnp.float32)[:, :, None, None] * inv
    cos, sin = jnp.cos(ang), jnp.sin(ang)
    xf = x.astype(jnp.float32)
    x1, x2 = xf[..., :half], xf[..., half:]
    return jnp.concatenate([x1 * cos - x2 * sin, x2 * cos + x1 * sin], axis=-1).astype(x.dtype)

def gated_delta_rule(q, k, v, g, beta):
    b, s, h, dk = q.shape
    dv = v.shape[-1]
    nc = s // CHUNK
    f32 = jnp.float32

    def to_chunks(t):
        return t.astype(f32).reshape(b, nc, CHUNK, h, -1).transpose(0, 3, 1, 2, 4)

    q, k, v = to_chunks(q), to_chunks(k), to_chunks(v)
    g = g.astype(f32).reshape(b, nc, CHUNK, h).transpose(0, 3, 1, 2)
    beta = beta.astype(f32).reshape(b, nc, CHUNK, h).transpose(0, 3, 1, 2)
    gc = jnp.cumsum(g, axis=-1)
    idx = jnp.arange(CHUNK)
    strict = idx[:, None] > idx[None, :]
    causal = idx[:, None] >= idx[None, :]
    decay = jnp.exp(jnp.where(causal, gc[..., :, None] - gc[..., None, :], -jnp.inf))

    kb = k * beta[..., None]
    lower = jnp.where(strict, jnp.einsum("bhncd,bhnsd->bhncs", kb, k) * decay, 0.0)
    eye = jnp.eye(CHUNK, dtype=f32)
    t_inv = lax.linalg.triangular_solve(eye + lower, jnp.broadcast_to(eye, lower.shape),
                                        left_side=True, lower=True)
    u = jnp.einsum("bhncs,bhnsd->bhncd", t_inv, v * beta[..., None])
    w = jnp.einsum("bhncs,bhnsd->bhncd", t_inv, kb * jnp.exp(gc)[..., None])
    attn = jnp.einsum("bhncd,bhnsd->bhncs", q, k) * decay
    qg = q * jnp.exp(gc)[..., None]
    kdec = k * jnp.exp(gc[..., -1:] - gc)[..., None]
    glast = jnp.exp(gc[..., -1])

    def step(state, xs):
        u_c, w_c, a_c, qg_c, kd_c, gl_c = xs
        v_new = u_c - jnp.einsum("bhcd,bhde->bhce", w_c, state)
        o = jnp.einsum("bhcd,bhde->bhce", qg_c, state) + jnp.einsum("bhcs,bhse->bhce", a_c, v_new)
        state = state * gl_c[..., None, None] + jnp.einsum("bhcd,bhce->bhde", kd_c, v_new)
        return state, o

    xs = tuple(jnp.moveaxis(t, 2, 0) for t in (u, w, attn, qg, kdec, glast))
    _, o = lax.scan(step, jnp.zeros((b, h, dk, dv), f32), xs)
    return o.transpose(1, 0, 3, 2, 4).reshape(b, s, h, dv)

def chunk_causal_attention(q, k, v):
    b, s, h, dqk = q.shape
    dv = v.shape[-1]
    nqb = s // Q_BLOCK
    scale = dqk ** -0.5
    qb = q.astype(jnp.float32).reshape(b, nqb, Q_BLOCK, h, dqk).transpose(1, 0, 3, 2, 4)
    kh = k.astype(jnp.float32).transpose(0, 2, 1, 3)
    vh = v.astype(jnp.float32).transpose(0, 2, 1, 3)
    key_chunk = jnp.arange(s) // CHUNK

    def one_block(args):
        q_blk, start = args
        sc = jnp.einsum("bhqd,bhkd->bhqk", q_blk, kh) * scale
        q_chunk = (start + jnp.arange(Q_BLOCK)) // CHUNK
        sc = jnp.where(key_chunk[None, :] <= q_chunk[:, None], sc, -jnp.inf)
        p = jax.nn.softmax(sc, axis=-1)
        return jnp.einsum("bhqk,bhkd->bhqd", p, vh)

    o = lax.map(one_block, (qb, jnp.arange(nqb) * Q_BLOCK))
    return o.transpose(1, 0, 3, 2, 4).reshape(b, s, h * dv).astype(q.dtype)

def peer_ffn(h, w_pq, sub_keys, u_tab, v_tab):
    b, s, d = h.shape
    q = (h @ w_pq).reshape(b, s, PEER_HEADS, 2, PEER_DKEY // 2)
    scores = jnp.einsum("bshpd,hpnd->bshpn", q.astype(jnp.float32), sub_keys.astype(jnp.float32))
    top_s, top_i = lax.top_k(scores, PEER_TOPK)
    cand_s = (top_s[..., 0, :, None] + top_s[..., 1, None, :]).reshape(b, s, PEER_HEADS, PEER_TOPK * PEER_TOPK)
    cand_i = (top_i[..., 0, :, None] * N_KEYS + top_i[..., 1, None, :]).reshape(b, s, PEER_HEADS, PEER_TOPK * PEER_TOPK)
    best_s, best_pos = lax.top_k(cand_s, PEER_TOPK)
    expert_idx = jnp.take_along_axis(cand_i, best_pos, axis=-1)
    gate = jax.nn.softmax(best_s, axis=-1)

    nb = (b * s) // PEER_TOKEN_BLOCK
    hb = h.reshape(nb, PEER_TOKEN_BLOCK, d)
    ib = expert_idx.reshape(nb, PEER_TOKEN_BLOCK, PEER_HEADS, PEER_TOPK)
    gb = gate.reshape(nb, PEER_TOKEN_BLOCK, PEER_HEADS, PEER_TOPK)

    def block(args):
        h_blk, i_blk, g_blk = args
        u = u_tab[i_blk]
        act = jax.nn.gelu(jnp.einsum("td,thkd->thk", h_blk, u).astype(jnp.float32), approximate=False)
        vv = v_tab[i_blk]
        return jnp.einsum("thk,thkd->td", (g_blk * act).astype(vv.dtype), vv)

    y = lax.map(block, (hb, ib, gb))
    return y.reshape(b, s, d).astype(h.dtype)

def setup_inputs(seed: int = 0) -> dict:
    key = jax.random.key(seed)
    ks = jax.random.split(key, 24)
    f32 = jnp.float32
    L = DEPTH

    def nrm(k, shape, scale):
        return jax.random.normal(k, shape, f32) * scale

    def gain(k, n):
        return 1.0 + 0.02 * jax.random.normal(k, (L, n), f32)

    x = jax.random.normal(ks[0], (BATCH, SEQ, D_MODEL), f32)
    offset = jax.random.randint(ks[1], (BATCH, 1), 0, MAX_POS_OFFSET // CHUNK) * CHUNK
    positions = (offset + jnp.arange(SEQ, dtype=jnp.int32)[None, :]).astype(jnp.int32)
    a_log = jnp.log(jax.random.uniform(ks[5], (L, GDN_HEADS), f32, 1.0, 16.0))
    dt = jnp.exp(jax.random.uniform(ks[6], (L, GDN_HEADS), f32, np.log(1e-3), np.log(1e-1)))
    dt_bias = dt + jnp.log(-jnp.expm1(-dt))
    return {
        "x": x,
        "positions": positions,
        "norm1_g": gain(ks[2], D_MODEL),
        "w_in": nrm(ks[3], (L, D_MODEL, IN_TOTAL), D_MODEL ** -0.5),
        "conv_w": nrm(ks[4], (L, CONV_K, GDN_QKV_W), CONV_K ** -0.5),
        "a_log": a_log,
        "dt_bias": dt_bias,
        "gdn_norm_g": gain(ks[7], GDN_DV),
        "w_gdn_out": nrm(ks[8], (L, GDN_V_W, D_MODEL), GDN_V_W ** -0.5),
        "cq_norm_g": gain(ks[9], Q_LORA),
        "w_uq": nrm(ks[10], (L, Q_LORA, MLA_HEADS * MLA_QK), Q_LORA ** -0.5),
        "ckv_norm_g": gain(ks[11], KV_LORA),
        "w_ukv": nrm(ks[12], (L, KV_LORA, MLA_HEADS * (MLA_NOPE + MLA_V)), KV_LORA ** -0.5),
        "q_norm_g": gain(ks[13], MLA_QK),
        "k_norm_g": gain(ks[14], MLA_QK),
        "w_mla_out": nrm(ks[15], (L, MLA_V_W, D_MODEL), MLA_V_W ** -0.5),
        "w_o": nrm(ks[16], (L, D_MODEL, D_MODEL), D_MODEL ** -0.5),
        "norm2_g": gain(ks[17], D_MODEL),
        "w_pq": nrm(ks[18], (L, D_MODEL, PEER_HEADS * PEER_DKEY), D_MODEL ** -0.5),
        "sub_keys": nrm(ks[19], (L, PEER_HEADS, 2, N_KEYS, PEER_DKEY // 2), (PEER_DKEY // 2) ** -0.5),
        "u_tab": nrm(ks[20], (L, N_EXPERTS, D_MODEL), D_MODEL ** -0.5),
        "v_tab": nrm(ks[21], (L, N_EXPERTS, D_MODEL), 0.5),
    }

def reference(x, positions, norm1_g, w_in, conv_w, a_log, dt_bias, gdn_norm_g, w_gdn_out,
              cq_norm_g, w_uq, ckv_norm_g, w_ukv, q_norm_g, k_norm_g, w_mla_out,
              w_o, norm2_g, w_pq, sub_keys, u_tab, v_tab):
    b, s, d = x.shape
    split_points = np.cumsum(IN_SPLITS)[:-1].tolist()
    for l in range(DEPTH):
        h = rms_norm(x, norm1_g[l])
        proj = h @ w_in[l]
        qkv, z, b_raw, a_raw, cq, ckv, k_rot, gates = jnp.split(proj, split_points, axis=-1)

        qkv = jax.nn.silu(causal_depthwise_conv(qkv, conv_w[l]))
        gq, gk, gv = jnp.split(qkv, [GDN_QK_W, 2 * GDN_QK_W], axis=-1)
        gq = l2_norm(gq.reshape(b, s, GDN_HEADS, GDN_DK)) * (GDN_DK ** -0.5)
        gk = l2_norm(gk.reshape(b, s, GDN_HEADS, GDN_DK))
        gv = gv.reshape(b, s, GDN_HEADS, GDN_DV)
        beta = jax.nn.sigmoid(b_raw.astype(jnp.float32))
        log_decay = -jnp.exp(a_log[l].astype(jnp.float32)) * jax.nn.softplus(
            a_raw.astype(jnp.float32) + dt_bias[l].astype(jnp.float32))
        o_a = gated_delta_rule(gq, gk, gv, log_decay, beta).astype(x.dtype)
        o_a = rms_norm(o_a, gdn_norm_g[l]) * jax.nn.silu(z.reshape(b, s, GDN_HEADS, GDN_DV))
        y_a = o_a.reshape(b, s, GDN_V_W) @ w_gdn_out[l]

        mq = (rms_norm(cq, cq_norm_g[l]) @ w_uq[l]).reshape(b, s, MLA_HEADS, MLA_QK)
        kv = (rms_norm(ckv, ckv_norm_g[l]) @ w_ukv[l]).reshape(b, s, MLA_HEADS, MLA_NOPE + MLA_V)
        k_nope, mv = kv[..., :MLA_NOPE], kv[..., MLA_NOPE:]
        k_rot_h = jnp.broadcast_to(k_rot[:, :, None, :], (b, s, MLA_HEADS, MLA_ROPE))
        mk = jnp.concatenate([k_nope, k_rot_h], axis=-1)
        mq = rms_norm(mq, q_norm_g[l])
        mk = rms_norm(mk, k_norm_g[l])
        mq = jnp.concatenate([mq[..., :MLA_NOPE], rope(mq[..., MLA_NOPE:], positions)], axis=-1)
        mk = jnp.concatenate([mk[..., :MLA_NOPE], rope(mk[..., MLA_NOPE:], positions)], axis=-1)
        y_b = chunk_causal_attention(mq, mk, mv) @ w_mla_out[l]

        g_a, g_b = jnp.split(gates, 2, axis=-1)
        merged = jax.nn.sigmoid(g_a) * y_a + jax.nn.sigmoid(g_b) * y_b
        x = x + merged @ w_o[l]

        h2 = rms_norm(x, norm2_g[l])
        x = x + peer_ffn(h2, w_pq[l], sub_keys[l], u_tab[l], v_tab[l])
    return x


_drawn_inputs = setup_inputs


def setup_inputs(seed=0):
    import zlib

    import numpy as np

    out = dict(_drawn_inputs(seed))
    spreads = {}
    factors = {'cq_norm_g': 5.981,
     'ckv_norm_g': 4.893,
     'q_norm_g': 6.051,
     'k_norm_g': 6.196,
     'gdn_norm_g': 8.0,
     'norm2_g': 4.176}
    for name, (base, spread) in spreads.items():
        noise = np.random.default_rng([zlib.crc32(name.encode()), seed]).standard_normal(out[name].shape)
        drawn = base * np.exp(spread * noise) if base else spread * noise
        out[name] = __import__('jax').numpy.asarray(drawn.astype(out[name].dtype))
    for name, factor in factors.items():
        out[name] = (out[name] * factor).astype(out[name].dtype)
    return out
```

```python
from contextlib import ExitStack

import numpy as np
import concourse.bass as bass
from concourse import mybir

F32 = mybir.dt.float32
F32R = mybir.dt.float32r
I32 = mybir.dt.int32
U32 = mybir.dt.uint32
ALU = mybir.AluOpType
ACT = mybir.ActivationFunctionType
AX = mybir.AxisListType

P = 128
S = 512
D = 1024
TT = S // P
KD = D // P
CH = 64
EPS = 1e-6
H = 8
HP = H // 2
DK = 64
QKV = 3 * H * DK
CONV = 4
NOPE, ROPE = 64, 32
QK = NOPE + ROPE
QL, KVL = 384, 256
THETA = 10000.0
PK = 16
NK = 128
SETS = 2 * H
NE = NK * NK
HALF = NK // 2
GT = 8
BIG = 3.0e38
NEG = -1.0e30
OFF_Z = QKV
OFF_BA = OFF_Z + 512
OFF_CKV = OFF_BA + 16 + QL
OFF_GATES = OFF_CKV + KVL + ROPE
NW = 2


def build(nc, x, positions, norm1_g, w_in, conv_w, a_log, dt_bias, gdn_norm_g, w_gdn_out,
          cq_norm_g, w_uq, ckv_norm_g, w_ukv, q_norm_g, k_norm_g, w_mla_out,
          w_o, norm2_g, w_pq, sub_keys, u_tab, v_tab, out, dump=None, upto=99):
    x_d = x.rearrange("a (t p) d -> p (a t) d", p=P)
    out_d = out.rearrange("a (t p) d -> p (a t) d", p=P)
    w_in_d = w_in.rearrange("l (k p) n -> p (l k) n", p=P)
    w_uq_d = w_uq.rearrange("l (k p) n -> p (l k) n", p=P)
    w_ukv_d = w_ukv.rearrange("l (k p) n -> p (l k) n", p=P)
    w_gdn_d = w_gdn_out.rearrange("l (k p) n -> p (l k) n", p=P)
    w_mla_d = w_mla_out.rearrange("l (k p) n -> p (l k) n", p=P)
    w_o_d = w_o.rearrange("l (k p) n -> p (l k) n", p=P)
    w_pq_d = w_pq.rearrange("l (k p) n -> p (l k) n", p=P)
    sk_d = sub_keys.rearrange("l h s n d -> n (l h s) d")
    u_d = u_tab.rearrange("l e d -> (l e) d")
    v_d = v_tab.rearrange("l e d -> (l e) d")
    yt_d = nc.dram_tensor("y_first_half", [P, KD, S], F32).ap()

    ctx = ExitStack()

    def sb(name, shape, dt=F32, stack=ctx):
        return stack.enter_context(nc.sbuf_tensor(name, shape, dt))

    def sem(name):
        return ctx.enter_context(nc.semaphore(name))

    with ctx:
        ident = sb("ident", [P, P])
        iota = sb("iota", [P, P])
        jT = sb("jT", [P, S])
        iT = sb("iT", [P, S])
        gateT = sb("gateT", [P, S])
        lent = ExitStack()
        tposed = sb("tposed", [P, 4, HP, P], stack=lent)
        decay = sb("decay", [P, 2, HP, P], stack=lent)
        upper = sb("upper", [P, 2, HP, P], stack=lent)
        attnT = sb("attnT", [P, 2, HP, P], stack=lent)
        inv = sb("inv", [P, 2, HP, P], stack=lent)
        invT = sb("invT", [P, 2, HP, P], stack=lent)
        offd = sb("offd", [P, 2, HP, P], stack=lent)
        lent.close()
        h2hi = sb("h2hi", [P, KD, S], F32R)
        h2lo = sb("h2lo", [P, KD, S], F32R)

        early = ExitStack()

        def eb(name, shape, dt=F32, stack=early):
            return sb(name, shape, dt, stack)

        wring = eb("wring", [P, NW, KD * 512])
        hT = eb("hT", [P, KD, S])
        ones = eb("ones", [P, P])
        same = {b: eb(f"same{b}", [P, P]) for b in (2, 4, 8, 16, 32, 64)}
        level = {b: eb(f"level{b}", [P, P]) for b in (1, 2, 4, 8, 16, 32)}
        causal = eb("causal", [P, P])
        strict = eb("strict", [P, P])
        negmask = eb("negmask", [P, P])
        chunk_ones = eb("chunk_ones", [P, 2, P])
        iota_i = eb("iota_i", [P, P], I32)
        half_neg = eb("half_neg", [P, 2 * H])
        g1 = eb("g1", [P, KD])
        g2 = eb("g2", [P, KD])
        gcq = eb("gcq", [P, 3])
        gckv = eb("gckv", [P, 2])
        cw = eb("cw", [P, QKV // P, CONV])
        alog = eb("alog", [P, H])
        dtb = eb("dtb", [P, H])
        ggdn = eb("ggdn", [P, DK])
        gqk = eb("gqk", [P, 2, QK])
        pos_i = eb("pos_i", [P, TT], I32)
        oaT = eb("oaT", [P, HP, S])
        obT = eb("obT", [P, HP, S])
        ss = eb("ss", [P, TT])
        rs = eb("rs", [P, TT])
        ptok = eb("ptok", [P, TT, 16 + QL + KVL + ROPE])
        cos = eb("cos", [P, TT, ROPE // 2])
        sin = eb("sin", [P, TT, ROPE // 2])

        gdn = ExitStack()
        qkv = eb("qkv", [P, TT, QKV], stack=gdn)
        zs = eb("zs", [P, TT, 512], stack=gdn)
        beta = eb("beta", [P, TT, H], stack=gdn)
        gdec = eb("gdec", [P, TT, H], stack=gdn)
        gtmp = [eb(f"gtmp{i}", [P, TT, H], stack=gdn) for i in range(6)]
        ealog = eb("ealog", [P, H], stack=gdn)
        gsum = eb("gsum", [P, 4, TT * H], stack=gdn)
        eg = eb("eg", [P, TT, H], stack=gdn)
        ekd = eb("ekd", [P, TT, H], stack=gdn)
        egl = eb("egl", [P, 2, TT, H], stack=gdn)
        egp = eb("egp", [P, 2, TT, HP], stack=gdn)
        state = eb("state", [P, HP, 2, DK], stack=gdn)
        s1 = ExitStack()
        xt = eb("xt", [P, TT, D], stack=s1)
        xjunk = eb("xjunk", [P, D], stack=s1)
        cin = eb("cin", [P, 2, S + 3], stack=s1)
        cacc = eb("cacc", [P, 2, S], stack=s1)
        csil = eb("csil", [P, 2, S], stack=s1)
        s1.close()
        s2 = ExitStack()
        sq = eb("sq", [P, 2 * H, DK], stack=s2)
        ms = eb("ms", [P, 2 * H], stack=s2)
        rn = eb("rn", [P, 2 * H], stack=s2)
        kb = eb("kb", [P, 512], stack=s2)
        kbg = eb("kbg", [P, 512], stack=s2)
        kd = eb("kd", [P, 512], stack=s2)
        qg = eb("qg", [P, 512], stack=s2)
        gm = eb("gm", [P, 2, HP, P], stack=s2)
        ysb = eb("ysb", [P, 2, HP, P], stack=s2)
        usb = eb("usb", [P, 512], stack=s2)
        wT = eb("wT", [P, HP, P], stack=s2)
        vn = eb("vn", [P, 512], stack=s2)
        otok = eb("otok", [P, 512], stack=s2)
        onrm = eb("onrm", [P, 512], stack=s2)
        s2.close()
        gdn.close()

        mla = ExitStack()
        cqT = eb("cqT", [P, 3, S], stack=mla)
        ckvT = eb("ckvT", [P, 2, S], stack=mla)
        rss = eb("rss", [P, 2, TT], stack=mla)
        rrs = eb("rrs", [P, 2, TT], stack=mla)
        qk = eb("qk", [P, 2 * H, QK], stack=mla)
        qsq = eb("qsq", [P, 2 * H, QK], stack=mla)
        qms = eb("qms", [P, 2 * H], stack=mla)
        qrn = eb("qrn", [P, 2 * H], stack=mla)
        ang = [eb(f"ang{i}", [P, TT, ROPE // 2], stack=mla) for i in range(6)]
        invf = eb("invf", [P, ROPE // 2], stack=mla)
        posf = eb("posf", [P, TT], stack=mla)
        rt = [eb(f"rt{i}", [P, 2 * H, ROPE // 2], stack=mla) for i in range(4)]
        qkT = eb("qkT", [QK, 2 * H, S], stack=mla)
        vtok = eb("vtok", [P, TT, H, DK], stack=mla)
        prob = eb("prob", [P, 2, S], stack=mla)
        pT = eb("pT", [P, 2, TT, P], stack=mla)
        mx = eb("mx", [P, 2 * TT * H], stack=mla)
        nmx = eb("nmx", [P, TT * H], stack=mla)
        rsum = eb("rsum", [P, TT * H], stack=mla)
        rinv = eb("rinv", [P, TT * H], stack=mla)
        mla.close()

        mrg = ExitStack()
        siga = eb("siga", [P, TT, 512], stack=mrg)
        sigb = eb("sigb", [P, TT, 512], stack=mrg)
        mergedT = eb("mergedT", [P, KD, S], stack=mrg)
        x2 = eb("x2", [P, TT, D], stack=mrg)
        junk2 = eb("junk2", [P, D], stack=mrg)
        mrg.close()
        pk = ExitStack()
        h2T = hT
        skT = eb("skT", [P, SETS, NK], stack=pk)
        qTm = eb("qTm", [P, 2, S], stack=pk)
        sc = eb("sc", [P, TT, SETS, NK], stack=pk)
        sc2 = eb("sc2", [P, TT, NK], stack=pk)
        tops = eb("tops", [P, TT, SETS, PK], stack=pk)
        topi = eb("topi", [P, TT, SETS, PK], U32, stack=pk)
        topf = eb("topf", [P, TT, SETS, PK], stack=pk)
        cand = eb("cand", [P, H, PK, PK], stack=pk)
        cand2 = eb("cand2", [P, H, PK, PK], stack=pk)
        best = eb("best", [P, H, PK], stack=pk)
        bpos = eb("bpos", [P, H, PK], U32, stack=pk)
        apos = eb("apos", [P, 2, H, PK], U32, stack=pk)
        afl = eb("afl", [P, 2, H, PK], stack=pk)
        sel = eb("sel", [P, 3, H, PK], stack=pk)
        gsm = eb("gsm", [P, 2, H], stack=pk)
        pk.close()
        early.close()

        act = sb("act", [P, HALF, S])
        raw = sb("raw", [P, 2, D])
        opr_hi = sb("opr_hi", [P, 2, D], F32R)
        opr_lo = sb("opr_lo", [P, 2, D], F32R)
        w_hi = sb("w_hi", [P, 2, S], F32R)
        w_lo = sb("w_lo", [P, 2, S], F32R)
        selA = sb("selA", [P, 2, GT, HALF])
        selB = raw[:, :, :].rearrange("p s (t j) -> p s t j", t=GT)

        ps = ctx.enter_context(nc.psum_tensor("ps", [P, 8, 512], F32))

        tiles = {k: v[:] for k, v in locals().items() if k in (
            "hT", "qkv", "zs", "ptok", "beta", "gdec", "oaT", "cos", "sin", "obT", "x2", "sc", "jT", "iT", "gateT", "h2T")}
        ystage = lambda k: selA[:, k % 2, :, :].rearrange("p t i -> p (t i)")
        y0T = act[:, 0:KD, :]
        ysum = act[:, KD:2 * KD, :]
        xb = act[:, 2 * KD:3 * KD, :].rearrange("p (t a) n -> p t (a n)", t=TT)

        names = """consts_ready small_loaded mask_step
            sumsq_ready meansq_ready rstd_ready xn_ready xT_mm hT_ready
            qkv_mm conv_in conv_out silu_ready qkvT_mm qkv_tok
            tok_mm tok_taken dve_step act_step pool_step
            gates_in gates_exp gates_ready gsum_mm gsum_exp
            gms_ready grn_ready gderived gT_mm gT_taken gmask_ready grow_mm gexp_in gexp_ready gdecay_done
            gkk_mm gkk_taken goffd_ready gy_mm gy_taken glev_mm glev_done guw_mm guw_taken
            gws_mm gvn_ready go_mm go_taken gup_mm gstate_ready onsq_ready onrs_ready onorm_ready oT_mm oT_taken gdn_over
            msq_ready mms_ready mrs_ready mcn_ready mcT_mm mcT_taken ang_ready trig_ready
            mproj_mm mproj_taken mqms_ready mqrs_ready mrope_ready mqT_mm mqT_taken
            score_mm negmax_ready prob_ready probn_ready pT_mm pT_taken av_mm av_taken mla_over
            ga_mm ga_sig gb_mm gb_sig y_mm merged_ready mT_mm mT_taken xo_mm x2_ready ss2_ready ms2_ready rs2_ready
            h2n_ready h2T_mm h2T_taken h2_hi h2_lo sk_mm sk_taken pq_mm pq_taken sc_mm sc_taken topk_ready
            best_ready gexp2_ready sel_ready selT_mm selT_taken early_over
            u_tmm u_hi u_lo u_mm act_ready onehot_ready spread_mm spread_taken
            v_hi v_lo w_hi_ready w_ready v_mm y_copied yT_mm y_added""".split()
        s = {n: sem(n) for n in names}
        w_loaded = [sem(f"w_loaded{i}") for i in range(NW)]
        w_used = sem("w_used")
        x_loaded = [sem(f"x_loaded{t}") for t in range(TT)]
        raw_loaded = [sem(f"raw_loaded{i}") for i in range(2)]
        y_stored = [sem(f"y_stored{i}") for i in range(2)]
        x2_stored = sem("x2_stored")
        y_loaded = sem("y_loaded")
        out_stored = sem("out_stored")
        dumped = sem("dumped")

        panels = []
        for n in range(3):
            panels.append(("qkv_mm", 4 * (n + 1), [(w_in_d[:, :, n * 512:(n + 1) * 512], 0, KD, 512)]))
        PAN_TOK = len(panels)
        TOK = [(OFF_Z, 512), (OFF_BA, 16 + QL), (OFF_CKV, KVL + ROPE)]
        for n, (at, w) in enumerate(TOK):
            panels.append(("tok_mm", TT * (n + 1), [(w_in_d[:, :, at:at + w], 0, KD, w)]))
        PAN_UQ = len(panels)
        panels.append(("mproj_mm", TT, [(w_uq_d, 0, 3, H * QK)]))
        PAN_UKV = len(panels)
        panels.append(("mproj_mm", TT, [(w_ukv_d, 0, 2, H * 2 * DK)]))
        PAN_MERGE = len(panels)
        for n in range(2):
            for g, name in enumerate(("ga_mm", "gb_mm")):
                at = OFF_GATES + g * D + n * 512
                panels.append((name, TT * (n + 1), [(w_in_d[:, :, at:at + 512], 0, KD, 512)]))
            panels.append(("y_mm", TT * (n + 1), [(w_gdn_d[:, :, n * 512:(n + 1) * 512], 0, HP, 512),
                                                  (w_mla_d[:, :, n * 512:(n + 1) * 512], HP * 512, HP, 512)]))
        PAN_O = len(panels)
        for n in range(2):
            panels.append(("xo_mm", TT * (n + 1), [(w_o_d[:, :, n * 512:(n + 1) * 512], 0, KD, 512)]))
        PAN_SK = len(panels)
        panels.append(("sk_mm", SETS // 4, [(sk_d, 0, SETS, NK)]))
        PAN_PQ = len(panels)
        for n in range(4):
            panels.append(("pq_mm", 4 * (n + 1), [(w_pq_d[:, :, n * 512:(n + 1) * 512], 0, KD, 512)]))

        def panel(n, k, w, at=0):
            return wring[:, n % NW, at:at + k * w].rearrange("p (k w) -> p k w", k=k)

        def loads_by(n):
            return sum(16 * len(panels[m][2]) for m in range(n % NW, n + 1, NW))

        def linker(eng, step):
            count = [0]

            def link(ins):
                count[0] += 1
                ins.then_inc(step, 1)
                eng.wait_ge(step, count[0])
            return link

        block = ctx.enter_context(nc.Block())
        bc = lambda ap, n, at: ap.unsqueeze(at).to_broadcast(list(ap.shape[:at]) + [n] + list(ap.shape[at:]))

        def stop(eng, stage):
            return upto < stage

        @block.sync
        def _(sp):
            for t in range(TT):
                sp.dma_start(xt[:, t, :], x_d[:, t, :]).then_inc(x_loaded[t], 16)
            for n, (_, _, parts) in enumerate(panels):
                if dump is not None and n >= {1: 3, 2: 6, 3: 8, 4: 8, 5: PAN_SK}.get(upto, 99):
                    break
                if n == PAN_PQ + 1:
                    sp.wait_ge(s["x2_ready"], 2 * TT)
                    sp.dma_start(out_d, x2[:, :, :]).then_inc(x2_stored, 16)
                if n >= NW:
                    sp.wait_ge(s[panels[n - NW][0]], panels[n - NW][1])
                if n == PAN_MERGE:
                    sp.wait_ge(s["mla_over"], 4)
                    sp.dma_start(x2[:, :, :], x_d).then_inc(x_loaded[0], 16)
                for src, at, k, w in parts:
                    sp.dma_start(panel(n, k, w, at), src).then_inc(w_loaded[n % NW], 16)
            if dump is not None:
                waits, outs = dump
                for name, v in waits:
                    sp.wait_ge(s[name], v)
                for i, (tile, dst) in enumerate(outs):
                    sp.dma_start(dst, tiles[tile]).then_inc(dumped, 16)
                    sp.wait_ge(dumped, 16 * (i + 1))
            if upto < 6:
                return
            sp.wait_ge(x2_stored, 16)
            if upto < 7:
                return
            sp.wait_ge(s["early_over"], 4)
            for half in range(2):
                base = half * HALF
                for table, used in ((u_d, "u_tmm"), (v_d, "v_lo")):
                    if table is u_d and half:
                        sp.wait_ge(s["v_lo"], HALF)
                    if table is v_d:
                        sp.wait_ge(s["spread_mm"], (half + 1) * (S // GT))
                    for sl in range(2):
                        sp.dma_start(raw[:, sl, :], table[(base + sl) * P:(base + sl + 1) * P, :])\
                          .then_inc(raw_loaded[sl], 16)
                    with sp.Fori(1, HALF // 2) as it:
                        for sl in range(2):
                            sp.wait_ge(s[used], 2 * it + (base - 1 + sl))
                            sp.dma_start(raw[:, sl, :], table[bass.ds((2 * it + (base + sl)) * P, P), :])\
                              .then_inc(raw_loaded[sl], 16)
                if not half:
                    for k in range(KD):
                        sp.wait_ge(s["y_copied"], k + 1)
                        sp.dma_start(yt_d[:, k, :], ystage(k)).then_inc(y_stored[k % 2], 16)
            for sl in range(2):
                sp.wait_ge(y_stored[sl], 16 * KD // 2)
            sp.wait_ge(s["w_ready"], NK)
            sp.dma_start(y0T, yt_d).then_inc(y_loaded, 16)
            sp.dma_start(xb, out_d).then_inc(y_loaded, 16)
            for t in range(TT):
                sp.wait_ge(s["y_added"], 2 * (t + 1))
                sp.dma_start(out_d[:, t, :], xb[:, t, :]).then_inc(out_stored, 16)
            sp.wait_ge(out_stored, 16 * TT)

        @block.tensor
        def _(pe):
            def take_panel(n, *shape):
                pe.wait_ge(w_loaded[n % NW], loads_by(n))
                return panel(n, *shape)

            pe.wait_ge(s["consts_ready"], 1)
            for u in range(2 * TT):
                t, hf = divmod(u, 2)
                if not hf:
                    pe.wait_ge(s["xn_ready"], t + 1)
                if u >= 2:
                    pe.wait_ge(s["hT_ready"], u - 1)
                for b in range(4):
                    last = pe.transpose(ps[:, u % 2, b * P:(b + 1) * P], xt[:, t, (4 * hf + b) * P:(4 * hf + b + 1) * P], ident[:, :])
                last.then_inc(s["xT_mm"], 1)
            pe.wait_ge(s["hT_ready"], 2 * TT)

            NB = QKV // P
            for m in range(NB + 2):
                if m < NB:
                    if m % 4 == 0:
                        wp = take_panel(m // 4, KD, 512)
                    if m >= 2:
                        pe.wait_ge(s["conv_in"], m - 1)
                    for k in range(KD):
                        last = pe.matmul(ps[:, 2 + m % 2, :], wp[:, k, (m % 4) * P:(m % 4 + 1) * P], hT[:, k, :],
                                         start=k == 0, stop=k == KD - 1)
                    last.then_inc(s["qkv_mm"], 1)
                if m >= 2:
                    j = m - 2
                    pe.wait_ge(s["silu_ready"], j + 1)
                    if j >= 2:
                        pe.wait_ge(s["qkv_tok"], j - 1)
                    for t in range(TT):
                        last = pe.transpose(ps[:, 4 + j % 2, t * P:(t + 1) * P], csil[:, j % 2, t * P:(t + 1) * P], ident[:, :])
                    last.then_inc(s["qkvT_mm"], 1)
            if stop(pe, 2):
                return
            for n, (_, w) in enumerate(TOK):
                wp = take_panel(PAN_TOK + n, KD, w)
                for t in range(TT):
                    u = n * TT + t
                    if u >= 2:
                        pe.wait_ge(s["tok_taken"], u - 1)
                    for k in range(KD):
                        last = pe.matmul(ps[:, 6 + u % 2, 0:w], hT[:, k, t * P:(t + 1) * P], wp[:, k, :],
                                         start=k == 0, stop=k == KD - 1)
                    last.then_inc(s["tok_mm"], 1)
            if stop(pe, 3):
                return

            pe.wait_ge(s["consts_ready"], 2)
            pe.wait_ge(s["gates_ready"], 1)
            gflat = gdec[:, :, :].rearrange("p t h -> p (t h)")
            for i, m in enumerate((causal[:, :], same[64][:, :], chunk_ones[:, 0, :], chunk_ones[:, 1, :])):
                last = pe.matmul(ps[:, 0, i * 32:(i + 1) * 32], m, gflat, start=True, stop=True)
            last.then_inc(s["gsum_mm"], 1)
            pe.wait_ge(s["gsum_exp"], 1)
            pe.wait_ge(s["conv_in"], NB)
            pe.wait_ge(s["qkv_tok"], NB)
            pe.wait_ge(s["tok_taken"], 3 * TT)
            for t in range(TT):
                pe.wait_ge(s["gderived"], t + 1)
                if t:
                    pe.wait_ge(s["gkk_taken"], 2 * t)
                srcs = (qkv[:, t, 512:1024], kb[:, :], qkv[:, t, 0:512], qg[:, :])
                for i, src in enumerate(srcs):
                    for hp in range(HP):
                        last = pe.transpose(ps[:, i, hp * P:(hp + 1) * P], src[:, hp * P:(hp + 1) * P], ident[:, :])
                    last.then_inc(s["gT_mm"], 1)
                pe.wait_ge(s["gmask_ready"], t + 1)
                if t:
                    pe.wait_ge(s["go_taken"], 2 * t)
                for par in range(2):
                    last = pe.matmul(ps[:, 4 + par, :], ones[:, :], gm[:, par, :, :].rearrange("p a b -> p (a b)"),
                                     start=True, stop=True)
                last.then_inc(s["grow_mm"], 1)
                pe.wait_ge(s["gT_taken"], 4 * (t + 1))
                if t:
                    pe.wait_ge(s["oT_taken"], t)
                    pe.wait_ge(s["gstate_ready"], 2 * t + 1)
                for i, (bank, b) in enumerate(((6, 1), (0, 2))):
                    for hp in range(HP):
                        for par in range(2):
                            r = slice(par * DK, (par + 1) * DK)
                            last = pe.matmul(ps[:, bank + par, hp * P:(hp + 1) * P], tposed[r, 0, hp, :], tposed[r, b, hp, :],
                                             start=True, stop=True)
                    last.then_inc(s["gkk_mm"], 1)
                for lv in range(6):
                    n = 6 * t + lv
                    pe.wait_ge(s["goffd_ready"], n + 1)
                    if lv:
                        pe.wait_ge(s["glev_done"], n)
                    for par in range(2):
                        for hp in range(HP):
                            last = pe.matmul(ps[:, 2 + par, hp * P:(hp + 1) * P], offd[:, par, hp, :],
                                             inv[:, par, hp, :] if lv else ident[:, :], start=True, stop=True)
                    last.then_inc(s["gy_mm"], 1)
                    if not lv:
                        continue
                    pe.wait_ge(s["gy_taken"], 5 * t + lv)
                    if lv < 5:
                        for par in range(2):
                            for hp in range(HP):
                                last = pe.matmul(ps[:, 4 + par, hp * P:(hp + 1) * P], invT[:, par, hp, :], ysb[:, par, hp, :],
                                                 start=True, stop=True)
                    for par in range(2):
                        for hp in range(HP):
                            last = pe.matmul(ps[:, 6 + par, hp * P:(hp + 1) * P], ysb[:, par, hp, :], invT[:, par, hp, :],
                                             start=True, stop=True)
                    last.then_inc(s["glev_mm"], 1)
                pe.wait_ge(s["glev_done"], 6 * (t + 1))
                for hp in range(HP):
                    for par in range(2):
                        h = 2 * hp + par
                        pe.matmul(ps[:, 2, h * DK:(h + 1) * DK], invT[:, par, hp, :], qkv[:, t, 1024 + h * DK:1024 + (h + 1) * DK],
                                  start=True, stop=True)
                        last = pe.matmul(ps[par * DK:(par + 1) * DK, 3, hp * P:(hp + 1) * P], kbg[:, h * DK:(h + 1) * DK],
                                         invT[:, par, hp, :], start=True, stop=True)
                last.then_inc(s["guw_mm"], 1)
                pe.wait_ge(s["guw_taken"], 2 * (t + 1))
                for c in range(2):
                    n = 2 * t + c
                    r = slice(c * CH, (c + 1) * CH)
                    pe.wait_ge(s["gstate_ready"], n + 1)
                    for hp in range(HP):
                        last = pe.matmul(ps[r, 4, hp * P:(hp + 1) * P], wT[:, hp, r],
                                         state[:, hp, :, :].rearrange("p a d -> p (a d)"), start=True, stop=True)
                    last.then_inc(s["gws_mm"], 1)
                    pe.wait_ge(s["gvn_ready"], n + 1)
                    for hp in range(HP):
                        last = pe.matmul(ps[:, 6, hp * P:(hp + 1) * P], kd[r, hp * P:(hp + 1) * P], vn[r, hp * P:(hp + 1) * P],
                                         start=True, stop=True)
                    last.then_inc(s["gup_mm"], 1)
                    for hp in range(HP):
                        pe.matmul(ps[r, 5, hp * P:(hp + 1) * P], tposed[:, 3, hp, r],
                                  state[:, hp, :, :].rearrange("p a d -> p (a d)"), start=True, stop=False)
                        for par in range(2):
                            h = 2 * hp + par
                            last = pe.matmul(ps[r, 5, h * DK:(h + 1) * DK], attnT[:, par, hp, r], vn[:, h * DK:(h + 1) * DK],
                                             start=False, stop=par == 1)
                    last.then_inc(s["go_mm"], 1)
                pe.wait_ge(s["onorm_ready"], t + 1)
                for hp in range(HP):
                    last = pe.transpose(ps[:, 7, hp * P:(hp + 1) * P], onrm[:, hp * P:(hp + 1) * P], ident[:, :])
                last.then_inc(s["oT_mm"], 1)
            if stop(pe, 4):
                return

            pe.drain().then_inc(s["gdn_over"], 1)
            pe.wait_ge(s["gdn_over"], 4)
            for t in range(TT):
                pe.wait_ge(s["mcn_ready"], t + 1)
                if t >= 2:
                    pe.wait_ge(s["mcT_taken"], t - 1)
                a = 2 * (t % 2)
                for b in range(3):
                    pe.transpose(ps[:, a, b * P:(b + 1) * P], ptok[:, t, 16 + b * P:16 + (b + 1) * P], ident[:, :])
                for b in range(2):
                    last = pe.transpose(ps[:, a + 1, b * P:(b + 1) * P],
                                        ptok[:, t, 16 + QL + b * P:16 + QL + (b + 1) * P], ident[:, :])
                last.then_inc(s["mcT_mm"], 1)
            pe.wait_ge(s["mcT_taken"], TT)
            wq = take_panel(PAN_UQ, 3, H * QK)
            wkv = take_panel(PAN_UKV, 2, H * 2 * DK)
            for t in range(TT + 1):
                if t < TT:
                    if t:
                        pe.wait_ge(s["mproj_taken"], 4 * t)
                    for bank, w, src, n0, n1 in ((4, wq, cqT, 0, 512), (5, wq, cqT, 512, 768),
                                                 (6, wkv, ckvT, 0, 512), (7, wkv, ckvT, 512, 1024)):
                        nk = src.shape[1]
                        for k in range(nk):
                            last = pe.matmul(ps[:, bank, 0:n1 - n0], src[:, k, t * P:(t + 1) * P], w[:, k, n0:n1],
                                             start=k == 0, stop=k == nk - 1)
                    last.then_inc(s["mproj_mm"], 1)
                if t:
                    j = t - 1
                    pe.wait_ge(s["mrope_ready"], j + 1)
                    if j:
                        pe.wait_ge(s["mqT_taken"], 4 * j)
                    for b in range(4):
                        for i in range(4):
                            last = pe.transpose(ps[0:QK, b, i * P:(i + 1) * P], qk[:, 4 * b + i, :], ident[:, :])
                        last.then_inc(s["mqT_mm"], 1)
            pe.wait_ge(s["mqT_taken"], 4 * TT)
            NU = TT * H
            for i in range(NU + 2):
                if i < NU:
                    t, h = divmod(i, H)
                    if i >= 2:
                        pe.wait_ge(s["prob_ready"], i - 1)
                    pe.matmul(ps[:, 4 + i % 2, 0:(t + 1) * P], qkT[:, h, t * P:(t + 1) * P], qkT[:, H + h, 0:(t + 1) * P],
                              start=True, stop=True).then_inc(s["score_mm"], 1)
                if 1 <= i <= NU:
                    j = i - 1
                    t = j // H
                    pe.wait_ge(s["probn_ready"], j + 1)
                    if j >= 2:
                        pe.wait_ge(s["pT_taken"], j - 1)
                    for k in range(t + 1):
                        last = pe.transpose(ps[:, 6 + j % 2, k * P:(k + 1) * P], prob[:, j % 2, k * P:(k + 1) * P], ident[:, :])
                    last.then_inc(s["pT_mm"], 1)
                if i >= 2:
                    j = i - 2
                    t, h = divmod(j, H)
                    hp, par = divmod(h, 2)
                    pe.wait_ge(s["pT_taken"], j + 1)
                    if h == 0 and t >= 2:
                        pe.wait_ge(s["av_taken"], t - 1)
                    for k in range(t + 1):
                        last = pe.matmul(ps[par * DK:(par + 1) * DK, t % 2, hp * P:(hp + 1) * P], vtok[:, k, h, :],
                                         pT[:, j % 2, k, :], start=k == 0, stop=k == t)
                    last.then_inc(s["av_mm"], 1)
            if stop(pe, 5):
                return
            pe.drain().then_inc(s["mla_over"], 1)
            pe.wait_ge(s["mla_over"], 4)
            for n in range(2):
                for g, (name, taken) in enumerate((("ga_mm", "ga_sig"), ("gb_mm", "gb_sig"))):
                    wp = take_panel(PAN_MERGE + 3 * n + g, KD, 512)
                    for t in range(TT):
                        u = n * TT + t
                        if u >= 2:
                            pe.wait_ge(s[taken], u - 1)
                        for k in range(KD):
                            last = pe.matmul(ps[:, 2 * g + u % 2, :], hT[:, k, t * P:(t + 1) * P], wp[:, k, :],
                                             start=k == 0, stop=k == KD - 1)
                        last.then_inc(s[name], 1)
                wp = take_panel(PAN_MERGE + 3 * n + 2, KD, 512)
                for t in range(TT + 1):
                    if t < TT:
                        u = n * TT + t
                        if u:
                            pe.wait_ge(s["merged_ready"], u)
                        for b, src in enumerate((oaT, obT)):
                            for k in range(HP):
                                last = pe.matmul(ps[:, 4 + b, :], src[:, k, t * P:(t + 1) * P], wp[:, b * HP + k, :],
                                                 start=k == 0, stop=k == HP - 1)
                        last.then_inc(s["y_mm"], 1)
                    if t:
                        u = n * TT + t - 1
                        pe.wait_ge(s["merged_ready"], u + 1)
                        if u >= 2:
                            pe.wait_ge(s["mT_taken"], u - 1)
                        for b in range(4):
                            last = pe.transpose(ps[:, 6 + u % 2, b * P:(b + 1) * P], siga[:, t - 1, b * P:(b + 1) * P], ident[:, :])
                        last.then_inc(s["mT_mm"], 1)
            pe.wait_ge(s["mT_taken"], 2 * TT)
            for n in range(2):
                wp = take_panel(PAN_O + n, KD, 512)
                for t in range(TT):
                    u = n * TT + t
                    if u >= 2:
                        pe.wait_ge(s["x2_ready"], u - 1)
                    for k in range(KD):
                        last = pe.matmul(ps[:, u % 2, :], mergedT[:, k, t * P:(t + 1) * P], wp[:, k, :],
                                         start=k == 0, stop=k == KD - 1)
                    last.then_inc(s["xo_mm"], 1)
            if stop(pe, 6):
                return
            wp = take_panel(PAN_SK, SETS, NK)
            for u in range(SETS // 4):
                if u >= 2:
                    pe.wait_ge(s["sk_taken"], u - 1)
                for b in range(4):
                    last = pe.transpose(ps[:, 2 + u % 2, b * P:(b + 1) * P], wp[:, 4 * u + b, :], ident[:, :])
                last.then_inc(s["sk_mm"], 1)
            pe.wait_ge(s["x2_ready"], 2 * TT)
            for u in range(2 * TT):
                t, hf = divmod(u, 2)
                pe.wait_ge(s["h2n_ready"], t + 1)
                if u >= 2:
                    pe.wait_ge(s["h2T_taken"], u - 1)
                for b in range(4):
                    last = pe.transpose(ps[:, u % 2, b * P:(b + 1) * P], x2[:, t, (4 * hf + b) * P:(4 * hf + b + 1) * P], ident[:, :])
                last.then_inc(s["h2T_mm"], 1)
            pe.wait_ge(s["h2T_taken"], 2 * TT)
            pe.wait_ge(s["sk_taken"], SETS // 4)
            for m in range(SETS + 1):
                if m < SETS:
                    if m % 4 == 0:
                        wp = take_panel(PAN_PQ + m // 4, KD, 512)
                    if m >= 2:
                        pe.wait_ge(s["pq_taken"], m - 1)
                    for k in range(KD):
                        last = pe.matmul(ps[:, 4 + m % 2, :], wp[:, k, (m % 4) * P:(m % 4 + 1) * P], h2T[:, k, :],
                                         start=k == 0, stop=k == KD - 1)
                    last.then_inc(s["pq_mm"], 1)
                if m:
                    j = m - 1
                    pe.wait_ge(s["pq_taken"], j + 1)
                    if j >= 2:
                        pe.wait_ge(s["sc_taken"], j - 1)
                    for t in range(TT):
                        last = pe.matmul(ps[:, 6 + j % 2, t * P:(t + 1) * P], qTm[:, j % 2, t * P:(t + 1) * P], skT[:, j, :],
                                         start=True, stop=True)
                    last.then_inc(s["sc_mm"], 1)
            for t in range(TT):
                pe.wait_ge(s["sel_ready"], t + 1)
                if t >= 2:
                    pe.wait_ge(s["selT_taken"], t - 1)
                for i in range(3):
                    last = pe.transpose(ps[:, t % 2, i * P:(i + 1) * P], sel[:, i, :, :].rearrange("p h k -> p (h k)"), ident[:, :])
                last.then_inc(s["selT_mm"], 1)
            pe.drain().then_inc(s["early_over"], 1)
            pe.wait_ge(s["early_over"], 4)
            if stop(pe, 7):
                return

            def u_transposes(sl, use):
                pe.wait_ge(raw_loaded[sl], use)
                for k in range(KD):
                    last = pe.transpose(ps[:, 2 * sl + k // 4, (k % 4) * P:(k % 4 + 1) * P], raw[:, sl, k * P:(k + 1) * P], ident[:, :])
                last.then_inc(s["u_tmm"], 1)

            def u_products(sl, n):
                pe.wait_ge(s["u_lo"], n)
                for k in range(KD):
                    c = slice(k * P, (k + 1) * P)
                    pe.matmul(ps[:, 4 + sl, :], opr_hi[:, sl, c], h2hi[:, k, :], start=k == 0, stop=False)
                    pe.matmul(ps[:, 4 + sl, :], opr_hi[:, sl, c], h2lo[:, k, :], start=False, stop=False)
                    last = pe.matmul(ps[:, 4 + sl, :], opr_lo[:, sl, c], h2hi[:, k, :], start=False, stop=k == KD - 1)
                last.then_inc(s["u_mm"], 1)

            def v_products(sl, n, first, final):
                pe.wait_ge(s["v_lo"], n)
                pe.wait_ge(s["w_ready"], n)
                for k in range(KD):
                    c = slice(k * P, (k + 1) * P)
                    pe.matmul(ps[:, k, :], opr_hi[:, sl, c], w_hi[:, sl, :], start=first, stop=False)
                    pe.matmul(ps[:, k, :], opr_hi[:, sl, c], w_lo[:, sl, :], start=False, stop=False)
                    last = pe.matmul(ps[:, k, :], opr_lo[:, sl, c], w_hi[:, sl, :], start=False, stop=final)
                last.then_inc(s["v_mm"], 1)

            for half in range(2):
                base = half * HALF
                rb = 2 * half * HALF // 2
                if half:
                    pe.wait_ge(s["y_copied"], KD)
                u_transposes(0, 16 * (rb + 1))
                with pe.Fori(0, HALF // 2 - 1) as it:
                    u_transposes(1, 16 * it + 16 * (rb + 1))
                    u_products(0, 2 * it + base + 1)
                    u_transposes(0, 16 * it + 16 * (rb + 2))
                    u_products(1, 2 * it + base + 2)
                u_transposes(1, 16 * (rb + HALF // 2))
                u_products(0, base + HALF - 1)
                u_products(1, base + HALF)
                gb = half * (S // GT)
                with pe.Fori(0, S // GT // 2) as it:
                    for sl in range(2):
                        pe.wait_ge(s["onehot_ready"], 2 * it + (gb + 1 + sl))
                        for g in range(GT):
                            last = pe.matmul(ps[:, sl, g * HALF:(g + 1) * HALF], selB[:, sl, g, :], selA[:, sl, g, :],
                                             start=True, stop=True)
                        last.then_inc(s["spread_mm"], 1)
                pe.wait_ge(s["spread_taken"], gb + S // GT)
                pe.wait_ge(s["act_ready"], base + HALF)
                v_products(0, base + 1, True, False)
                v_products(1, base + 2, False, False)
                with pe.Fori(1, HALF // 2 - 1) as it:
                    v_products(0, 2 * it + base + 1, False, False)
                    v_products(1, 2 * it + base + 2, False, False)
                v_products(0, base + HALF - 1, False, False)
                v_products(1, base + HALF, False, True)
            pe.wait_ge(s["y_copied"], 2 * KD)
            for u in range(2 * TT):
                t, hf = divmod(u, 2)
                if u >= 2:
                    pe.wait_ge(s["y_added"], u - 1)
                for b in range(4):
                    last = pe.transpose(ps[:, u % 2, b * P:(b + 1) * P], ysum[:, 4 * hf + b, t * P:(t + 1) * P], ident[:, :])
                last.then_inc(s["yT_mm"], 1)

        @block.scalar
        def _(act_e):
            link = linker(act_e, s["act_step"])
            A = nc.scalar.activation
            with nc.allow_non_contiguous_dma(reason="small vectors onto partitions"):
                col = lambda v: v.rearrange("l (k p) -> p (l k)", p=P)
                row = lambda v, n: v.to_broadcast([P, n])
                loads = [(g1[:, :], col(norm1_g)), (g2[:, :], col(norm2_g)), (gcq[:, :], col(cq_norm_g)),
                         (gckv[:, :], col(ckv_norm_g)),
                         (alog[:, :], row(a_log, H)), (dtb[:, :], row(dt_bias, H)), (ggdn[:, :], row(gdn_norm_g, DK)),
                         (gqk[:, 0, :], row(q_norm_g, QK)), (gqk[:, 1, :], row(k_norm_g, QK)),
                         (pos_i[:, :], positions.rearrange("b (t p) -> p (b t)", p=P))]
                loads += [(cw[:, :, j], conv_w[:, j, :].rearrange("l (m p) -> p (l m)", p=P)) for j in range(CONV)]
                for dst, src in loads:
                    act_e.dma_start(dst, src).then_inc(s["small_loaded"], 16)
            small = 16 * len(loads)
            for t in range(TT):
                act_e.wait_ge(x_loaded[t], 16)
                link(A(xjunk[:, :], xt[:, t, :], ACT.Square, accum_out=ss[:, t:t + 1]))
                act_e.nop().then_inc(s["sumsq_ready"], 1)
            NB = QKV // P
            for m in range(NB + 1):
                if m < NB:
                    act_e.wait_ge(s["qkv_mm"], m + 1)
                    if m >= 2:
                        act_e.wait_ge(s["conv_out"], m - 1)
                    A(cin[:, m % 2, 3:], ps[:, 2 + m % 2, :], ACT.Copy).then_inc(s["conv_in"], 1)
                if m:
                    j = m - 1
                    act_e.wait_ge(s["conv_out"], j + 1)
                    if j >= 2:
                        act_e.wait_ge(s["qkvT_mm"], j - 1)
                    A(csil[:, j % 2, :], cacc[:, j % 2, :], ACT.Silu).then_inc(s["silu_ready"], 1)
            if stop(act_e, 2):
                return
            for n, (_, w) in enumerate(TOK):
                for t in range(TT):
                    u = n * TT + t
                    act_e.wait_ge(s["tok_mm"], u + 1)
                    src = ps[:, 6 + u % 2, 0:w]
                    if n == 0:
                        ins = A(zs[:, t, :], src, ACT.Silu)
                    elif n == 1:
                        ins = A(ptok[:, t, 0:w], src, ACT.Copy)
                    else:
                        ins = A(ptok[:, t, 16 + QL:16 + QL + w], src, ACT.Copy)
                    ins.then_inc(s["tok_taken"], 1)
            if stop(act_e, 3):
                return
            act_e.wait_ge(s["tok_taken"], 3 * TT)
            act_e.wait_ge(s["small_loaded"], small)
            link(A(beta[:, :, :], ptok[:, :, 0:H], ACT.Sigmoid))
            link(A(ealog[:, :], alog[:, :], ACT.Exp))
            act_e.wait_ge(s["gates_in"], 1)
            link(A(gtmp[2][:, :, :], gtmp[1][:, :, :], ACT.Exp))
            act_e.nop().then_inc(s["gates_exp"], 1)
            act_e.wait_ge(s["gates_in"], 2)
            link(A(gtmp[4][:, :, :], gtmp[3][:, :, :], ACT.Ln))
            act_e.nop().then_inc(s["gates_exp"], 1)
            act_e.wait_ge(s["gsum_mm"], 1)
            link(A(gsum[:, :, :], ps[:, 0, 0:P].rearrange("p (a b) -> p a b", a=4), ACT.Copy))
            link(A(eg[:, :, :].rearrange("p t h -> p (t h)"), gsum[:, 0, :], ACT.Exp))
            link(A(egl[:, :, :, :].rearrange("p c t h -> p (c t h)"), gsum[:, 2:4, :].rearrange("p a b -> p (a b)"), ACT.Exp))
            act_e.nop().then_inc(s["gsum_exp"], 1)
            act_e.wait_ge(s["gates_in"], 3)
            link(A(ekd[:, :, :], gtmp[5][:, :, :], ACT.Exp))
            act_e.nop().then_inc(s["gsum_exp"], 1)
            for t in range(TT):
                for i in range(4):
                    act_e.wait_ge(s["gT_mm"], 4 * t + i + 1)
                    if not i and t:
                        act_e.wait_ge(s["go_mm"], 2 * t)
                    A(tposed[:, i, :, :], ps[:, i, :].rearrange("p (a b) -> p a b", a=HP), ACT.Copy).then_inc(s["gT_taken"], 1)
                act_e.wait_ge(s["gexp_in"], t + 1)
                A(decay[:, :, :, :], decay[:, :, :, :], ACT.Exp).then_inc(s["gexp_ready"], 1)
                for lv in range(1, 6):
                    act_e.wait_ge(s["gy_mm"], 6 * t + lv + 1)
                    if lv > 1:
                        act_e.wait_ge(s["glev_mm"], 5 * t + lv - 1)
                    A(ysb[:, :, :, :], ps[:, 2:4, :].rearrange("p a (b c) -> p a b c", b=HP), ACT.Copy).then_inc(s["gy_taken"], 1)
                act_e.wait_ge(s["guw_mm"], t + 1)
                if t:
                    act_e.wait_ge(s["go_taken"], 2 * t)
                A(usb[:, :], ps[:, 2, :], ACT.Copy).then_inc(s["guw_taken"], 1)
                A(wT[:, :, :], ps[:, 3, :].rearrange("p (a b) -> p a b", a=HP), ACT.Copy).then_inc(s["guw_taken"], 1)
                for c in range(2):
                    r = slice(c * CH, (c + 1) * CH)
                    act_e.wait_ge(s["go_mm"], 2 * t + c + 1)
                    if t:
                        act_e.wait_ge(s["onorm_ready"], t)
                    A(otok[r, :], ps[r, 5, :], ACT.Copy).then_inc(s["go_taken"], 1)
                act_e.wait_ge(s["oT_mm"], t + 1)
                A(oaT[:, :, t * P:(t + 1) * P], ps[:, 7, :].rearrange("p (a b) -> p a b", a=HP), ACT.Copy).then_inc(s["oT_taken"], 1)
            if stop(act_e, 4):
                return
            act_e.drain().then_inc(s["gdn_over"], 1)
            act_e.wait_ge(s["gdn_over"], 4)
            qf = qsq[:, :, :].rearrange("p a b -> p (a b)")
            for t in range(TT):
                link(A(qf[:, 0:QL], ptok[:, t, 16:16 + QL], ACT.Square, accum_out=rss[:, 0, t:t + 1]))
                link(A(qf[:, 0:KVL], ptok[:, t, 16 + QL:16 + QL + KVL], ACT.Square, accum_out=rss[:, 1, t:t + 1]))
            act_e.nop().then_inc(s["msq_ready"], 1)
            act_e.wait_ge(s["ang_ready"], 1)
            A(sin[:, :, :], ang[2][:, :, :], ACT.Sin).then_inc(s["trig_ready"], 1)
            A(cos[:, :, :], ang[5][:, :, :], ACT.Sin).then_inc(s["trig_ready"], 1)
            for t in range(TT):
                act_e.wait_ge(s["mproj_mm"], t + 1)
                if t:
                    act_e.wait_ge(s["mqT_mm"], 4 * t)
                A(qk[:, 0:H, :].rearrange("p a b -> p (a b)"), ps[:, 4:6, :].rearrange("p a b -> p (a b)")[:, 0:H * QK], ACT.Copy)\
                    .then_inc(s["mproj_taken"], 1)
                kv = ps[:, 6:8, :].rearrange("p a (h c) -> p (a h) c", c=2 * DK)
                A(qk[:, H:, 0:NOPE], kv[:, :, 0:NOPE], ACT.Copy).then_inc(s["mproj_taken"], 1)
                A(vtok[:, t, :, :], kv[:, :, NOPE:], ACT.Copy).then_inc(s["mproj_taken"], 1)
                A(qk[:, H:, NOPE:], bc(ptok[:, t, 16 + QL + KVL:], H, 1), ACT.Copy).then_inc(s["mproj_taken"], 1)
                for b in range(4):
                    act_e.wait_ge(s["mqT_mm"], 4 * t + b + 1)
                    A(qkT[:, 4 * b:4 * b + 4, t * P:(t + 1) * P], ps[0:QK, b, :].rearrange("p (a b) -> p a b", a=4), ACT.Copy)\
                        .then_inc(s["mqT_taken"], 1)
            NU = TT * H
            for i in range(NU + 1):
                if i < NU:
                    t = i // H
                    act_e.wait_ge(s["negmax_ready"], i + 1)
                    if i >= 2:
                        act_e.wait_ge(s["pT_mm"], i - 1)
                    A(prob[:, i % 2, 0:(t + 1) * P], ps[:, 4 + i % 2, 0:(t + 1) * P], ACT.Exp, bias=nmx[:, i:i + 1],
                      scale=QK ** -0.5, accum_out=rsum[:, i:i + 1]).then_inc(s["prob_ready"], 1)
                if i:
                    j = i - 1
                    t, h = divmod(j, H)
                    act_e.wait_ge(s["pT_mm"], j + 1)
                    if j >= 2:
                        act_e.wait_ge(s["av_mm"], j - 1)
                    A(pT[:, j % 2, 0:t + 1, :], ps[:, 6 + j % 2, 0:(t + 1) * P].rearrange("p (a b) -> p a b", b=P), ACT.Copy)\
                        .then_inc(s["pT_taken"], 1)
                    if h == 1 and t:
                        act_e.wait_ge(s["av_mm"], t * H)
                        A(obT[:, :, (t - 1) * P:t * P], ps[:, (t - 1) % 2, :].rearrange("p (a b) -> p a b", a=HP), ACT.Copy)\
                            .then_inc(s["av_taken"], 1)
            act_e.wait_ge(s["av_mm"], NU)
            A(obT[:, :, (TT - 1) * P:], ps[:, (TT - 1) % 2, :].rearrange("p (a b) -> p a b", a=HP), ACT.Copy)\
                .then_inc(s["av_taken"], 1)
            if stop(act_e, 5):
                return
            act_e.drain().then_inc(s["mla_over"], 1)
            act_e.wait_ge(s["mla_over"], 4)
            for n in range(2):
                for g, (name, taken, dst) in enumerate((("ga_mm", "ga_sig", siga), ("gb_mm", "gb_sig", sigb))):
                    if n:
                        act_e.wait_ge(s["mT_mm"], TT)
                    for t in range(TT):
                        u = n * TT + t
                        act_e.wait_ge(s[name], u + 1)
                        A(dst[:, t, :], ps[:, 2 * g + u % 2, :], ACT.Sigmoid).then_inc(s[taken], 1)
                for t in range(TT):
                    u = n * TT + t
                    act_e.wait_ge(s["mT_mm"], u + 1)
                    A(mergedT[:, 4 * n:4 * n + 4, t * P:(t + 1) * P], ps[:, 6 + u % 2, :].rearrange("p (a b) -> p a b", a=4), ACT.Copy)\
                        .then_inc(s["mT_taken"], 1)
            if stop(act_e, 6):
                return
            for t in range(TT):
                act_e.wait_ge(s["x2_ready"], TT + t + 1)
                link(A(junk2[:, :], x2[:, t, :], ACT.Square, accum_out=ss[:, t:t + 1]))
                act_e.nop().then_inc(s["ss2_ready"], 1)
            for u in range(SETS // 4):
                act_e.wait_ge(s["sk_mm"], u + 1)
                A(skT[:, 4 * u:4 * u + 4, :], ps[:, 2 + u % 2, :].rearrange("p (a b) -> p a b", a=4), ACT.Copy).then_inc(s["sk_taken"], 1)
            for u in range(2 * TT):
                t, hf = divmod(u, 2)
                act_e.wait_ge(s["h2T_taken"], u + 1)
                b = (slice(None), slice(4 * hf, 4 * hf + 4), slice(t * P, (t + 1) * P))
                A(h2hi[b], h2T[b], ACT.Copy).then_inc(s["h2_hi"], 1)
            for m in range(SETS + 1):
                if m < SETS:
                    act_e.wait_ge(s["pq_mm"], m + 1)
                    if m >= 2:
                        act_e.wait_ge(s["sc_mm"], m - 1)
                    A(qTm[:, m % 2, :], ps[:, 4 + m % 2, :], ACT.Copy).then_inc(s["pq_taken"], 1)
                if m:
                    j = m - 1
                    act_e.wait_ge(s["sc_mm"], j + 1)
                    A(sc[:, :, j, :], ps[:, 6 + j % 2, :].rearrange("p (t n) -> p t n", t=TT), ACT.Copy).then_inc(s["sc_taken"], 1)
            for t in range(TT):
                act_e.wait_ge(s["best_ready"], t + 1)
                A(best[:, :, :], best[:, :, :], ACT.Exp).then_inc(s["gexp2_ready"], 1)
            act_e.drain().then_inc(s["early_over"], 1)
            act_e.wait_ge(s["early_over"], 4)
            if stop(act_e, 7):
                return
            wide = lambda sl: ps[:, 2 * sl:2 * sl + 2, :].rearrange("p a b -> p (a b)")

            def u_hi(sl, n):
                act_e.wait_ge(s["u_tmm"], n)
                A(opr_hi[:, sl, :], wide(sl), ACT.Copy).then_inc(s["u_hi"], 1)

            def u_act(sl, n, at):
                act_e.wait_ge(s["u_mm"], n)
                A(act[:, at, :] if isinstance(at, int) else act[:, bass.ds(at, 1), :].rearrange("p a b -> p (a b)"),
                  ps[:, 4 + sl, :], ACT.Gelu).then_inc(s["act_ready"], 1)

            def v_hi(sl, n, use):
                act_e.wait_ge(raw_loaded[sl], use)
                A(opr_hi[:, sl, :], raw[:, sl, :], ACT.Copy).then_inc(s["v_hi"], 1)

            for half in range(2):
                base = half * HALF
                if half:
                    act_e.wait_ge(s["v_mm"], base)
                u_hi(0, base + 1)
                u_hi(1, base + 2)
                with act_e.Fori(0, HALF // 2 - 1) as it:
                    for sl in range(2):
                        u_act(sl, 2 * it + (base + 1 + sl), 2 * it + sl)
                        u_hi(sl, 2 * it + (base + 3 + sl))
                for sl in range(2):
                    u_act(sl, base + HALF - 1 + sl, HALF - 2 + sl)
                rb = half * HALF + HALF // 2
                for sl in range(2):
                    v_hi(sl, base + 1 + sl, 16 * (rb + 1))
                with act_e.Fori(1, HALF // 2) as it:
                    for sl in range(2):
                        act_e.wait_ge(s["v_mm"], 2 * it + (base - 1 + sl))
                        v_hi(sl, None, 16 * it + 16 * (rb + 1))
                act_e.wait_ge(s["v_mm"], base + HALF)
                if not half:
                    for k in range(KD):
                        if k >= 2:
                            act_e.wait_ge(y_stored[k % 2], 16 * (k // 2))
                        A(ystage(k), ps[:, k, :], ACT.Copy).then_inc(s["y_copied"], 1)

        @block.vector
        def _(dve):
            link = linker(dve, s["dve_step"])
            V = nc.vector
            tt, ts, stt = V.tensor_tensor, V.tensor_scalar, V.scalar_tensor_tensor
            for t in range(TT):
                dve.wait_ge(s["sumsq_ready"], t + 1)
                ts(ss[:, t:t + 1], ss[:, t:t + 1], 1.0 / D, EPS, ALU.mult, ALU.add).then_inc(s["meansq_ready"], 1)
            for sl in range(2):
                link(V.memset(cin[:, sl, 0:3], 0.0))
            for t in range(TT):
                dve.wait_ge(s["rstd_ready"], t + 1)
                ts(xt[:, t, :], xt[:, t, :], rs[:, t:t + 1], None, ALU.mult).then_inc(s["xn_ready"], 1)
            dve.wait_ge(s["small_loaded"], 16 * 14)
            for u in range(2 * TT):
                t, hf = divmod(u, 2)
                dve.wait_ge(s["xT_mm"], u + 1)
                tt(hT[:, 4 * hf:4 * hf + 4, t * P:(t + 1) * P], ps[:, u % 2, :].rearrange("p (a b) -> p a b", a=4),
                   bc(g1[:, 4 * hf:4 * hf + 4], P, 2), ALU.mult).then_inc(s["hT_ready"], 1)
            NB = QKV // P
            for m in range(NB + 2):
                if m < NB:
                    dve.wait_ge(s["conv_in"], m + 1)
                    if m >= 2:
                        dve.wait_ge(s["silu_ready"], m - 1)
                    x0, acc = cin[:, m % 2, :], cacc[:, m % 2, :]
                    link(ts(acc, x0[:, 0:S], cw[:, m, 0:1], None, ALU.mult))
                    for j in (1, 2):
                        link(stt(acc, x0[:, j:j + S], cw[:, m, j:j + 1], acc, ALU.mult, ALU.add))
                    stt(acc, x0[:, 3:3 + S], cw[:, m, 3:4], acc, ALU.mult, ALU.add).then_inc(s["conv_out"], 1)
                if m >= 2:
                    j = m - 2
                    dve.wait_ge(s["qkvT_mm"], j + 1)
                    V.tensor_copy(qkv[:, :, j * P:(j + 1) * P], ps[:, 4 + j % 2, :].rearrange("p (t c) -> p t c", t=TT))\
                        .then_inc(s["qkv_tok"], 1)
            if stop(dve, 3):
                return
            dve.wait_ge(s["tok_taken"], 3 * TT)
            araw = ptok[:, :, H:2 * H]
            link(tt(gtmp[0][:, :, :], araw, bc(dtb[:, :], TT, 1), ALU.add))
            link(ts(gtmp[1][:, :, :], gtmp[0][:, :, :], -1.0, None, ALU.mult))
            tt(gtmp[1][:, :, :], gtmp[0][:, :, :], gtmp[1][:, :, :], ALU.min).then_inc(s["gates_in"], 1)
            dve.wait_ge(s["gates_exp"], 1)
            ts(gtmp[3][:, :, :], gtmp[2][:, :, :], 1.0, None, ALU.add).then_inc(s["gates_in"], 1)
            dve.wait_ge(s["gates_in"], 2)
            link(ts(gtmp[5][:, :, :], gtmp[3][:, :, :], 1.0, 1e-30, ALU.subtract, ALU.max))
            link(V.reciprocal(gtmp[5][:, :, :], gtmp[5][:, :, :]))
            link(tt(gtmp[5][:, :, :], gtmp[5][:, :, :], gtmp[2][:, :, :], ALU.mult))
            dve.wait_ge(s["gates_exp"], 2)
            link(tt(gtmp[5][:, :, :], gtmp[5][:, :, :], gtmp[4][:, :, :], ALU.mult))
            link(ts(gtmp[0][:, :, :], gtmp[0][:, :, :], 0.0, None, ALU.max))
            link(tt(gtmp[5][:, :, :], gtmp[5][:, :, :], gtmp[0][:, :, :], ALU.add))
            link(tt(gtmp[5][:, :, :], gtmp[5][:, :, :], bc(ealog[:, :], TT, 1), ALU.mult))
            ts(gdec[:, :, :], gtmp[5][:, :, :], -1.0, None, ALU.mult).then_inc(s["gates_ready"], 1)
            dve.wait_ge(s["gsum_exp"], 1)
            fl = lambda ap: ap.rearrange("p t h -> p (t h)")
            tt(fl(gtmp[5][:, :, :]), gsum[:, 1, :], gsum[:, 0, :], ALU.subtract).then_inc(s["gates_in"], 1)
            for par in range(2):
                r = slice(par * DK, (par + 1) * DK)
                link(V.tensor_copy(egp[r, :, :, :], egl[r, :, :, :].rearrange("p c t (a b) -> p c t a b", b=2)[:, :, :, :, par]))
            link(V.memset(vn[:, :], 0.0))
            V.memset(state[:, :, :, :], 0.0).then_inc(s["gstate_ready"], 1)
            dve.wait_ge(s["consts_ready"], 2)
            dve.wait_ge(s["gsum_exp"], 2)
            for t in range(TT):
                q2 = qkv[:, t, 0:512].rearrange("p (h d) -> p h d", h=H)
                k2 = qkv[:, t, 512:1024].rearrange("p (h d) -> p h d", h=H)
                v2 = qkv[:, t, 1024:].rearrange("p (h d) -> p h d", h=H)
                qk2 = qkv[:, t, 0:1024].rearrange("p (h d) -> p h d", h=2 * H)
                h3 = lambda ap: ap.rearrange("p (h d) -> p h d", h=H)
                b8 = lambda ap: bc(ap[:, t, :], DK, 2)
                link(tt(sq[:, :, :], qk2, qk2, ALU.mult))
                link(V.reduce_sum(ms[:, :], sq[:, :, :], AX.X))
                ts(ms[:, :], ms[:, :], EPS, None, ALU.add).then_inc(s["gms_ready"], 1)
                dve.wait_ge(s["grn_ready"], t + 1)
                link(ts(rn[:, 0:H], rn[:, 0:H], DK ** -0.5, None, ALU.mult))
                link(tt(qk2, qk2, bc(rn[:, :], DK, 2), ALU.mult))
                if t:
                    dve.wait_ge(s["gup_mm"], 2 * t)
                link(tt(h3(kb[:, :]), k2, b8(beta), ALU.mult))
                link(tt(h3(kbg[:, :]), h3(kb[:, :]), b8(eg), ALU.mult))
                link(tt(h3(kd[:, :]), k2, b8(ekd), ALU.mult))
                link(tt(h3(qg[:, :]), q2, b8(eg), ALU.mult))
                tt(v2, v2, b8(beta), ALU.mult).then_inc(s["gderived"], 1)
                dve.wait_ge(s["grow_mm"], t + 1)
                gc = gsum[:, 0, t * H:(t + 1) * H].rearrange("p (a b) -> p b a", b=2)
                for par in range(2):
                    link(tt(decay[:, par, :, :], ps[:, 4 + par, :].rearrange("p (a c) -> p a c", a=HP), bc(gc[:, par, :], P, 2), ALU.subtract))
                dec3 = decay[:, :, :, :].rearrange("p a b c -> p (a b) c")
                tt(dec3, dec3, bc(negmask[:, :], 2 * HP, 1), ALU.add).then_inc(s["gexp_in"], 1)
                dve.wait_ge(s["gexp_ready"], t + 1)
                full = lambda b: ps[:, b:b + 2, :].rearrange("p a (b c) -> p (a b) c", b=HP)
                w3 = lambda ap: ap[:, :, :, :].rearrange("p a b c -> p (a b) c")
                dve.wait_ge(s["gkk_mm"], 2 * t + 1)
                tt(w3(upper), full(6), dec3, ALU.mult).then_inc(s["gkk_taken"], 1)
                dve.wait_ge(s["gkk_mm"], 2 * t + 2)
                tt(w3(attnT), full(0), dec3, ALU.mult).then_inc(s["gkk_taken"], 1)
                dve.wait_ge(s["gkk_taken"], 2 * t + 1)
                for lv in range(6):
                    if lv:
                        dve.wait_ge(s["gy_mm"], 6 * t + lv)
                        dve.wait_ge(s["glev_done"], 6 * t + lv)
                    tt(w3(offd), w3(upper), bc(level[1 << lv][:, :], 2 * HP, 1), ALU.mult).then_inc(s["goffd_ready"], 1)
                    idb = bc(ident[:, :], 2 * HP, 1)
                    if lv == 0:
                        dve.wait_ge(s["gy_mm"], 6 * t + 1)
                        dve.wait_ge(s["goffd_ready"], 6 * t + 1)
                        link(tt(w3(inv), idb, full(2), ALU.subtract))
                        tt(w3(invT), idb, w3(offd), ALU.subtract).then_inc(s["glev_done"], 1)
                    else:
                        dve.wait_ge(s["glev_mm"], 5 * t + lv)
                        if lv < 5:
                            link(tt(w3(inv), w3(inv), full(4), ALU.subtract))
                        tt(w3(invT), w3(invT), full(6), ALU.subtract).then_inc(s["glev_done"], 1)
                dve.wait_ge(s["guw_taken"], 2 * (t + 1))
                for c in range(2):
                    n = 2 * t + c
                    r = slice(c * CH, (c + 1) * CH)
                    dve.wait_ge(s["gws_mm"], n + 1)
                    tt(vn[r, :], usb[r, :], ps[r, 4, :], ALU.subtract).then_inc(s["gvn_ready"], 1)
                    dve.wait_ge(s["go_mm"], n + 1)
                    for par in range(2):
                        pr = slice(par * DK, (par + 1) * DK)
                        link(tt(state[pr, :, par, :], state[pr, :, par, :], bc(egp[pr, c, t, :], DK, 2), ALU.mult))
                    for par in range(2):
                        pr = slice(par * DK, (par + 1) * DK)
                        up = ps[pr, 6, :].rearrange("p (a b d) -> p a b d", a=HP, b=2)[:, :, par, :]
                        ins = tt(state[pr, :, par, :], state[pr, :, par, :], up, ALU.add)
                        if par:
                            ins.then_inc(s["gstate_ready"], 1)
                        else:
                            link(ins)
                dve.wait_ge(s["go_taken"], 2 * (t + 1))
                link(tt(sq[:, 0:H, :], h3(otok[:, :]), h3(otok[:, :]), ALU.mult))
                link(V.reduce_sum(ms[:, 0:H], sq[:, 0:H, :], AX.X))
                ts(ms[:, 0:H], ms[:, 0:H], 1.0 / DK, EPS, ALU.mult, ALU.add).then_inc(s["onsq_ready"], 1)
                dve.wait_ge(s["onrs_ready"], t + 1)
                if t:
                    dve.wait_ge(s["oT_mm"], t)
                link(tt(h3(onrm[:, :]), h3(otok[:, :]), bc(rn[:, 0:H], DK, 2), ALU.mult))
                link(tt(h3(onrm[:, :]), h3(onrm[:, :]), bc(ggdn[:, :], H, 1), ALU.mult))
                tt(onrm[:, :], onrm[:, :], zs[:, t, :], ALU.mult).then_inc(s["onorm_ready"], 1)
            if stop(dve, 4):
                return
            dve.drain().then_inc(s["gdn_over"], 1)
            dve.wait_ge(s["gdn_over"], 4)

            f32 = np.float32
            two_pi = 2 * np.pi
            c1 = float(f32(6.28125))
            c2 = float((f32(two_pi - c1).view(np.uint32) & np.uint32(0xFFFFF000)).view(f32))
            c3 = float(f32(two_pi - c1 - c2))
            magic = float(1.5 * 2 ** 23)
            pi = float(np.nextafter(f32(np.pi), f32(0)))
            half_dim = ROPE // 2
            freqs = np.power(f32(THETA), -np.arange(half_dim, dtype=f32) / f32(half_dim)).astype(f32)
            for j in range(half_dim):
                last = V.memset(invf[:, j:j + 1], float(freqs[j]))
            link(last)
            link(V.tensor_copy(posf[:, :], pos_i[:, :]))
            a0, a1, a2, a3, a4, a5 = (a[:, :, :] for a in ang)
            link(tt(a0, bc(posf[:, :], half_dim, 2), bc(invf[:, :], TT, 1), ALU.mult))
            link(ts(a1, a0, 1 / two_pi, magic, ALU.mult, ALU.add))
            link(ts(a1, a1, magic, None, ALU.subtract))
            for c in (c1, c2, c3):
                link(stt(a0, a1, -c, a0, ALU.mult, ALU.add))
            link(ts(a2, a0, pi, -pi, ALU.min, ALU.max))
            link(ts(a3, a0, np.pi / 2, None, ALU.add))
            link(ts(a4, a3, pi, -two_pi, ALU.is_gt, ALU.mult))
            link(tt(a5, a3, a4, ALU.add))
            ts(a5, a5, pi, -pi, ALU.min, ALU.max).then_inc(s["ang_ready"], 1)
            dve.wait_ge(s["msq_ready"], 1)
            link(ts(rss[:, 0, :], rss[:, 0, :], 1.0 / QL, EPS, ALU.mult, ALU.add))
            ts(rss[:, 1, :], rss[:, 1, :], 1.0 / KVL, EPS, ALU.mult, ALU.add).then_inc(s["mms_ready"], 1)
            dve.wait_ge(s["mrs_ready"], 1)
            for t in range(TT):
                cq, ckv = ptok[:, t, 16:16 + QL], ptok[:, t, 16 + QL:16 + QL + KVL]
                link(ts(cq, cq, rrs[:, 0, t:t + 1], None, ALU.mult))
                ts(ckv, ckv, rrs[:, 1, t:t + 1], None, ALU.mult).then_inc(s["mcn_ready"], 1)
            for t in range(TT):
                a = 2 * (t % 2)
                dve.wait_ge(s["mcT_mm"], t + 1)
                link(tt(cqT[:, :, t * P:(t + 1) * P], ps[:, a, 0:QL].rearrange("p (a b) -> p a b", a=3), bc(gcq[:, :], P, 2), ALU.mult))
                tt(ckvT[:, :, t * P:(t + 1) * P], ps[:, a + 1, 0:KVL].rearrange("p (a b) -> p a b", a=2), bc(gckv[:, :], P, 2), ALU.mult)\
                    .then_inc(s["mcT_taken"], 1)
            dve.wait_ge(s["trig_ready"], 2)
            for t in range(TT):
                dve.wait_ge(s["mproj_taken"], 4 * (t + 1))
                link(tt(qsq[:, :, :], qk[:, :, :], qk[:, :, :], ALU.mult))
                link(V.reduce_sum(qms[:, :], qsq[:, :, :], AX.X))
                ts(qms[:, :], qms[:, :], 1.0 / QK, EPS, ALU.mult, ALU.add).then_inc(s["mqms_ready"], 1)
                dve.wait_ge(s["mqrs_ready"], t + 1)
                link(tt(qk[:, :, :], qk[:, :, :], bc(qrn[:, :], QK, 2), ALU.mult))
                for g in range(2):
                    part = qk[:, g * H:(g + 1) * H, :]
                    link(tt(part, part, bc(gqk[:, g, :], H, 1), ALU.mult))
                x1, x2r = qk[:, :, NOPE:NOPE + half_dim], qk[:, :, NOPE + half_dim:]
                ct, st = bc(cos[:, t, :], 2 * H, 1), bc(sin[:, t, :], 2 * H, 1)
                link(tt(rt[0][:, :, :], x1, ct, ALU.mult))
                link(tt(rt[1][:, :, :], x2r, st, ALU.mult))
                link(tt(rt[2][:, :, :], x2r, ct, ALU.mult))
                link(tt(rt[3][:, :, :], x1, st, ALU.mult))
                link(tt(x1, rt[0][:, :, :], rt[1][:, :, :], ALU.subtract))
                tt(x2r, rt[2][:, :, :], rt[3][:, :, :], ALU.add).then_inc(s["mrope_ready"], 1)
            NU = TT * H
            for i in range(NU + 1):
                if i < NU:
                    t = i // H
                    n = (t + 1) * P
                    dve.wait_ge(s["score_mm"], i + 1)
                    link(V.memset(ps[0:CH, 4 + i % 2, n - CH:n], NEG))
                    link(V.reduce_max(mx[:, i:i + 1], ps[:, 4 + i % 2, 0:n], AX.X))
                    ts(nmx[:, i:i + 1], mx[:, i:i + 1], -QK ** -0.5, None, ALU.mult).then_inc(s["negmax_ready"], 1)
                if i:
                    j = i - 1
                    n = (j // H + 1) * P
                    dve.wait_ge(s["prob_ready"], j + 1)
                    link(V.reciprocal(rinv[:, j:j + 1], rsum[:, j:j + 1]))
                    ts(prob[:, j % 2, 0:n], prob[:, j % 2, 0:n], rinv[:, j:j + 1], None, ALU.mult).then_inc(s["probn_ready"], 1)
            if stop(dve, 5):
                return
            dve.drain().then_inc(s["mla_over"], 1)
            dve.wait_ge(s["mla_over"], 4)
            for n in range(2):
                dve.wait_ge(s["ga_sig"], TT * (n + 1))
                dve.wait_ge(s["gb_sig"], TT * (n + 1))
                for t in range(TT):
                    dve.wait_ge(s["y_mm"], n * TT + t + 1)
                    link(tt(siga[:, t, :], siga[:, t, :], ps[:, 4, :], ALU.mult))
                    link(tt(sigb[:, t, :], sigb[:, t, :], ps[:, 5, :], ALU.mult))
                    tt(siga[:, t, :], siga[:, t, :], sigb[:, t, :], ALU.add).then_inc(s["merged_ready"], 1)
            dve.wait_ge(x_loaded[0], 32)
            for u in range(2 * TT):
                n, t = divmod(u, TT)
                dve.wait_ge(s["xo_mm"], u + 1)
                xs = x2[:, t, n * 512:(n + 1) * 512]
                tt(xs, xs, ps[:, u % 2, :], ALU.add).then_inc(s["x2_ready"], 1)
            if stop(dve, 6):
                return
            dve.wait_ge(x2_stored, 16)
            for t in range(TT):
                dve.wait_ge(s["ss2_ready"], t + 1)
                ts(ss[:, t:t + 1], ss[:, t:t + 1], 1.0 / D, EPS, ALU.mult, ALU.add).then_inc(s["ms2_ready"], 1)
            for t in range(TT):
                dve.wait_ge(s["rs2_ready"], t + 1)
                ts(x2[:, t, :], x2[:, t, :], rs[:, t:t + 1], None, ALU.mult).then_inc(s["h2n_ready"], 1)
            for u in range(2 * TT):
                t, hf = divmod(u, 2)
                b = (slice(None), slice(4 * hf, 4 * hf + 4), slice(t * P, (t + 1) * P))
                dve.wait_ge(s["h2T_mm"], u + 1)
                tt(h2T[b], ps[:, u % 2, :].rearrange("p (a b) -> p a b", a=4), bc(g2[:, 4 * hf:4 * hf + 4], P, 2), ALU.mult)\
                    .then_inc(s["h2T_taken"], 1)
                dve.wait_ge(s["h2_hi"], u + 1)
                tt(h2lo[b], h2T[b], h2hi[b].bitcast(F32), ALU.subtract).then_inc(s["h2_lo"], 1)
            for m in range(SETS):
                dve.wait_ge(s["sc_taken"], m + 1)
                for t in range(TT):
                    last = V.max(tops[:, t, m, 0:8], sc[:, t, m, :])
                link(last)
                for t in range(TT):
                    V.max_index(topi[:, t, m, 0:8], tops[:, t, m, 0:8], sc[:, t, m, :])
                    last = V.match_replace(sc2[:, t, :], tops[:, t, m, 0:8], sc[:, t, m, :], -BIG)
                link(last)
                for t in range(TT):
                    last = V.max(tops[:, t, m, 8:16], sc2[:, t, :])
                link(last)
                for t in range(TT):
                    last = V.max_index(topi[:, t, m, 8:16], tops[:, t, m, 8:16], sc2[:, t, :])
                link(last)
            link(V.tensor_copy(topf[:, :, :, :].rearrange("p a b c -> p (a b c)"), topi[:, :, :, :].rearrange("p a b c -> p (a b c)")))
            side = lambda ap, t, p: ap[:, t, :, :].rearrange("p (h s) k -> p h s k", s=2)[:, :, p, :]
            b4 = lambda ap, at: bc(ap, PK, at)
            c256 = lambda ap, h: ap[:, h, :, :].rearrange("p a b -> p (a b)")
            for t in range(TT):
                link(tt(cand[:, :, :, :], b4(side(tops, t, 0), 3), b4(side(tops, t, 1), 2), ALU.add))
                if t:
                    dve.wait_ge(s["selT_mm"], t)
                for h in range(H):
                    last = V.max(best[:, h, 0:8], c256(cand, h))
                link(last)
                for h in range(H):
                    V.max_index(bpos[:, h, 0:8], best[:, h, 0:8], c256(cand, h))
                    last = V.match_replace(c256(cand2, h), best[:, h, 0:8], c256(cand, h), -BIG)
                link(last)
                for h in range(H):
                    last = V.max(best[:, h, 8:16], c256(cand2, h))
                link(last)
                for h in range(H):
                    last = V.max_index(bpos[:, h, 8:16], best[:, h, 8:16], c256(cand2, h))
                link(last)
                link(V.tensor_copy(gsm[:, 0, :], best[:, :, 0]))
                tt(best[:, :, :], best[:, :, :], bc(gsm[:, 0, :], PK, 2), ALU.subtract).then_inc(s["best_ready"], 1)
                link(ts(apos[:, 0, :, :], bpos[:, :, :], 4, None, ALU.logical_shift_right))
                link(ts(apos[:, 1, :, :], bpos[:, :, :], 15, None, ALU.bitwise_and))
                link(V.tensor_copy(afl[:, :, :, :], apos[:, :, :, :]))
                for p, place in ((0, 1), (1, 0)):
                    io = iota[:, 0:PK]
                    io4 = bc(bc(io, PK, 1), H, 1)
                    link(tt(cand[:, :, :, :], io4, b4(afl[:, p, :, :], 3), ALU.is_equal))
                    link(tt(cand[:, :, :, :], cand[:, :, :, :], b4(side(topf, t, p), 2), ALU.mult))
                    link(V.reduce_sum(sel[:, place, :, :], cand[:, :, :, :], AX.X))
                dve.wait_ge(s["gexp2_ready"], t + 1)
                link(V.reduce_sum(gsm[:, 1, :], best[:, :, :], AX.X))
                link(V.reciprocal(gsm[:, 1, :], gsm[:, 1, :]))
                tt(sel[:, 2, :, :], best[:, :, :], bc(gsm[:, 1, :], PK, 2), ALU.mult).then_inc(s["sel_ready"], 1)
                dve.wait_ge(s["selT_mm"], t + 1)
                cols = slice(t * P, (t + 1) * P)
                for i, dst in enumerate((jT, iT, gateT)):
                    last = V.tensor_copy(dst[:, cols], ps[:, t % 2, i * P:(i + 1) * P])
                last.then_inc(s["selT_taken"], 1)
            dve.drain().then_inc(s["early_over"], 1)
            dve.wait_ge(s["early_over"], 4)
            if stop(dve, 7):
                return
            wide = lambda sl: ps[:, 2 * sl:2 * sl + 2, :].rearrange("p a b -> p (a b)")

            def u_lo(sl, n):
                dve.wait_ge(s["u_hi"], n)
                tt(opr_lo[:, sl, :], wide(sl), opr_hi[:, sl, :].bitcast(F32), ALU.subtract).then_inc(s["u_lo"], 1)

            def onehots(sl, g, t0, half):
                for j in range(GT):
                    at = bass.ds(t0 + j, 1)
                    ts(selB[:, sl, j, :], iota[:, :], jT[:, at], None, ALU.is_equal)
                    last = ts(selA[:, sl, j, :], iota[:, half * HALF:(half + 1) * HALF], iT[:, at], gateT[:, at], ALU.is_equal, ALU.mult)
                last.then_inc(s["onehot_ready"], 1)

            def weigh(sl, g, t0):
                dve.wait_ge(s["spread_mm"], g + 1)
                a = act[:, :, bass.ds(t0, GT)]
                tt(a, a, ps[:, sl, :].rearrange("p (t i) -> p i t", t=GT), ALU.mult).then_inc(s["spread_taken"], 1)

            def v_split(sl, n, use, at):
                dve.wait_ge(s["v_hi"], n)
                tt(opr_lo[:, sl, :], raw[:, sl, :], opr_hi[:, sl, :].bitcast(F32), ALU.subtract).then_inc(s["v_lo"], 1)
                a = act[:, at, :] if isinstance(at, int) else act[:, bass.ds(at, 1), :].rearrange("p a b -> p (a b)")
                V.tensor_copy(w_hi[:, sl, :], a).then_inc(s["w_hi_ready"], 1)
                dve.wait_ge(s["w_hi_ready"], n)
                tt(w_lo[:, sl, :], a, w_hi[:, sl, :].bitcast(F32), ALU.subtract).then_inc(s["w_ready"], 1)

            for half in range(2):
                base = half * HALF
                for sl in range(2):
                    u_lo(sl, base + 1 + sl)
                with dve.Fori(0, HALF // 2 - 1) as it:
                    for sl in range(2):
                        u_lo(sl, 2 * it + (base + 3 + sl))
                ng = S // GT
                gb = half * ng
                dve.wait_ge(s["act_ready"], base + HALF)
                dve.wait_ge(s["u_tmm"], base + HALF)
                if half:
                    for sl in range(2):
                        dve.wait_ge(y_stored[sl], 16 * KD // 2)
                onehots(0, gb, 0, half)
                onehots(1, gb + 1, GT, half)
                with dve.Fori(0, ng // 2 - 1) as it:
                    for sl in range(2):
                        weigh(sl, 2 * it + (gb + sl), it * (2 * GT) + sl * GT)
                        onehots(sl, None, it * (2 * GT) + (2 + sl) * GT, half)
                for sl in range(2):
                    weigh(sl, gb + ng - 2 + sl, (ng - 2 + sl) * GT)
                dve.wait_ge(s["spread_taken"], gb + ng)
                for sl in range(2):
                    v_split(sl, base + 1 + sl, None, sl)
                with dve.Fori(1, HALF // 2) as it:
                    for sl in range(2):
                        dve.wait_ge(s["v_mm"], 2 * it + (base - 1 + sl))
                        v_split(sl, 2 * it + (base + 1 + sl), None, 2 * it + sl)
            dve.wait_ge(s["v_mm"], NK)
            dve.wait_ge(y_loaded, 32)
            for k in range(KD):
                tt(ysum[:, k, :], y0T[:, k, :], ps[:, k, :], ALU.add).then_inc(s["y_copied"], 1)
            for u in range(2 * TT):
                t, hf = divmod(u, 2)
                dve.wait_ge(s["yT_mm"], u + 1)
                xs = xb[:, t, hf * 512:(hf + 1) * 512]
                tt(xs, xs, ps[:, u % 2, :], ALU.add).then_inc(s["y_added"], 1)

        @block.gpsimd
        def _(pool):
            link = linker(pool, s["pool_step"])
            G = nc.gpsimd
            ge, sel_ = ALU.is_ge, G.affine_select
            link(G.memset(ones[:, :], 1.0))
            link(G.memset(half_neg[:, :], -0.5))
            link(sel_(out=ident[:, :], in_=ones[:, :], pattern=[[-1, P]], base=0, channel_multiplier=1, compare_op=ALU.is_equal, fill=0.0))
            for t in range(TT):
                pool.wait_ge(s["meansq_ready"], t + 1)
                G.tensor_tensor(rs[:, t:t + 1], ss[:, t:t + 1], half_neg[:, 0:1], ALU.pow).then_inc(s["rstd_ready"], 1)
                if not t:
                    pool.wait_ge(s["pool_step"], 3)
                    G.nop().then_inc(s["consts_ready"], 1)
            for b in (2, 4, 8, 16, 32, 64):
                m = same[b][:, :].rearrange("p (n i) -> p n i", i=b)
                link(sel_(out=m, in_=ones[:, :].rearrange("p (n i) -> p n i", i=b), pattern=[[-b, P // b], [0, b]], base=0,
                          channel_multiplier=1, compare_op=ge, fill=0.0))
                link(sel_(out=m, in_=m, pattern=[[b, P // b], [0, b]], base=b - 1, channel_multiplier=-1, compare_op=ge, fill=0.0))
            link(sel_(out=causal[:, :], in_=same[64][:, :], pattern=[[1, P]], base=0, channel_multiplier=-1, compare_op=ge, fill=0.0))
            link(sel_(out=strict[:, :], in_=same[64][:, :], pattern=[[1, P]], base=-1, channel_multiplier=-1, compare_op=ge, fill=0.0))
            link(G.tensor_scalar(negmask[:, :], causal[:, :], -NEG, NEG, ALU.mult, ALU.add))
            for b in (1, 2, 4, 8, 16, 32):
                inner = ident if b == 1 else same[b]
                link(G.tensor_tensor(level[b][:, :], same[2 * b][:, :], inner[:, :], ALU.subtract))
                link(G.tensor_tensor(level[b][:, :], level[b][:, :], strict[:, :], ALU.mult))
            link(sel_(out=chunk_ones[:, 0, :], in_=ones[:, :], pattern=[[0, P]], base=CH - 1, channel_multiplier=-1, compare_op=ge, fill=0.0))
            link(sel_(out=chunk_ones[:, 1, :], in_=ones[:, :], pattern=[[0, P]], base=-CH, channel_multiplier=1, compare_op=ge, fill=0.0))
            link(G.iota(iota_i[:, :], pattern=[[1, P]], base=0, channel_multiplier=0))
            link(G.tensor_copy(iota[:, :], iota_i[:, :]))
            G.nop().then_inc(s["consts_ready"], 1)
            if stop(pool, 3):
                return
            pool.wait_ge(s["gates_ready"], 1)
            for t in range(TT):
                if t:
                    pool.wait_ge(s["grow_mm"], t)
                gt = gdec[:, t, :].rearrange("p (a b) -> p b a", b=2)
                for par in range(2):
                    last = G.tensor_tensor(gm[:, par, :, :], bc(causal[:, :], HP, 1), bc(gt[:, par, :], P, 2), ALU.mult)
                last.then_inc(s["gmask_ready"], 1)
                pool.wait_ge(s["gms_ready"], t + 1)
                G.tensor_tensor(rn[:, :], ms[:, :], half_neg[:, :], ALU.pow).then_inc(s["grn_ready"], 1)
                pool.wait_ge(s["onsq_ready"], t + 1)
                G.tensor_tensor(rn[:, 0:H], ms[:, 0:H], half_neg[:, 0:H], ALU.pow).then_inc(s["onrs_ready"], 1)
            if stop(pool, 4):
                return
            pool.drain().then_inc(s["gdn_over"], 1)
            pool.wait_ge(s["gdn_over"], 4)
            pool.wait_ge(s["mms_ready"], 1)
            fl = lambda ap: ap[:, :, :].rearrange("p a b -> p (a b)")
            G.tensor_tensor(fl(rrs), fl(rss), half_neg[:, 0:2 * TT], ALU.pow).then_inc(s["mrs_ready"], 1)
            for t in range(TT):
                pool.wait_ge(s["mqms_ready"], t + 1)
                G.tensor_tensor(qrn[:, :], qms[:, :], half_neg[:, :], ALU.pow).then_inc(s["mqrs_ready"], 1)
            if stop(pool, 5):
                return
            pool.drain().then_inc(s["mla_over"], 1)
            if stop(pool, 6):
                return
            for t in range(TT):
                pool.wait_ge(s["ms2_ready"], t + 1)
                G.tensor_tensor(rs[:, t:t + 1], ss[:, t:t + 1], half_neg[:, 0:1], ALU.pow).then_inc(s["rs2_ready"], 1)
            pool.drain().then_inc(s["early_over"], 1)


_INS = ["x", "positions", "norm1_g", "w_in", "conv_w", "a_log", "dt_bias", "gdn_norm_g", "w_gdn_out", "cq_norm_g",
        "w_uq", "ckv_norm_g", "w_ukv", "q_norm_g", "k_norm_g", "w_mla_out", "w_o", "norm2_g", "w_pq", "sub_keys",
        "u_tab", "v_tab"]


def kernel(**inputs):
    import concourse.bacc as _bacc
    from concourse.bass_utils import run_bass_kernel_spmd as _run

    nc = _bacc.Bacc("TRN2", target_bir_lowering=False, num_devices=1)
    arrays, args = {}, []
    for name in _INS:
        a = np.ascontiguousarray(inputs[name])
        arrays[f"in_{name}_dram"] = a
        args.append(nc.dram_tensor(f"in_{name}_dram", a.shape, mybir.dt.from_np(a.dtype), kind="ExternalInput").ap())
    args.append(nc.dram_tensor("out_0_dram", (1, S, D), F32, kind="ExternalOutput").ap())
    build(nc, *args)
    r = _run(nc, [arrays], core_ids=[0])
    return r.results[0]["out_0_dram"]
```

```python
from contextlib import ExitStack

import numpy as np
import concourse.bass as bass
from concourse import mybir

F32 = mybir.dt.float32
F32R = mybir.dt.float32r
F16 = mybir.dt.float16
I32 = mybir.dt.int32
U32 = mybir.dt.uint32
ALU = mybir.AluOpType
ACT = mybir.ActivationFunctionType
AX = mybir.AxisListType

P = 128
S = 512
D = 1024
TT = S // P
KD = D // P
CH = 64
EPS = 1e-6
H = 8
HP = H // 2
DK = 64
QKV = 3 * H * DK
CONV = 4
NOPE, ROPE = 64, 32
QK = NOPE + ROPE
QL, KVL = 384, 256
THETA = 10000.0
PK = 16
NK = 128
SETS = 2 * H
NE = NK * NK
GROUPS = (56, 40, 32)
ARENA = max(GROUPS)
GT = 8
NG = S // GT
ST = 2 * GT
CB = 4
GSCALE = 4096.0
NCAND = 112
BIG = 3.0e38
NEG = -1.0e30
OFF_Z = QKV
OFF_BA = OFF_Z + 512
OFF_CKV = OFF_BA + 16 + QL
OFF_GATES = OFF_CKV + KVL + ROPE
NW = 2
PARTS = 5
LEAD = TT * PARTS
SPREAD = S // 16


def build(nc, x, positions, norm1_g, w_in, conv_w, a_log, dt_bias, gdn_norm_g, w_gdn_out,
          cq_norm_g, w_uq, ckv_norm_g, w_ukv, q_norm_g, k_norm_g, w_mla_out,
          w_o, norm2_g, w_pq, sub_keys, u_tab, v_tab, out):
    x_d = x.rearrange("a (t p) d -> p (a t) d", p=P)
    out_d = out.rearrange("a (t p) d -> p (a t) d", p=P)
    w_in_d = w_in.rearrange("l (k p) n -> p (l k) n", p=P)
    w_uq_d = w_uq.rearrange("l (k p) n -> p (l k) n", p=P)
    w_ukv_d = w_ukv.rearrange("l (k p) n -> p (l k) n", p=P)
    w_gdn_d = w_gdn_out.rearrange("l (k p) n -> p (l k) n", p=P)
    w_mla_d = w_mla_out.rearrange("l (k p) n -> p (l k) n", p=P)
    w_o_d = w_o.rearrange("l (k p) n -> p (l k) n", p=P)
    w_pq_d = w_pq.rearrange("l (k p) n -> p (l k) n", p=P)
    sk_d = sub_keys.rearrange("l h s n d -> n (l h s) d")
    u_d = u_tab.rearrange("l e d -> (l e) d")
    v_d = v_tab.rearrange("l e d -> (l e) d")
    y_d = nc.dram_tensor("y_of_groups", [2, P, KD, S], F32).ap()
    g_d = nc.dram_tensor("gate_matrix", [S // ST, P, NK, ST], F32).ap()

    ctx = ExitStack()

    def sb(name, shape, dt=F32, stack=ctx):
        return stack.enter_context(nc.sbuf_tensor(name, shape, dt))

    def sem(name):
        return ctx.enter_context(nc.semaphore(name))

    with ctx:
        ident = sb("ident", [P, P])
        iota = sb("iota", [P, P])
        jT = sb("jT", [P, S], F16)
        iT = sb("iT", [P, S], F16)
        gate_hi = sb("gate_hi", [P, S], F16)
        gate_lo = sb("gate_lo", [P, S], F16)
        lent = ExitStack()
        tposed = sb("tposed", [P, 3, HP, P], stack=lent)
        attnT = sb("attnT", [P, 2, 2, HP, P], stack=lent)
        decay = sb("decay", [P, 2, HP, P], stack=lent)
        upper = sb("upper", [P, 2, HP, P], stack=lent)
        inv = sb("inv", [P, 2, HP, P], stack=lent)
        invT = sb("invT", [P, 2, HP, P], stack=lent)
        lent.close()
        h2hi = sb("h2hi", [P, KD, S], F32R)
        h2lo = sb("h2lo", [P, KD, S], F32R)

        early = ExitStack()

        def eb(name, shape, dt=F32, stack=early):
            return sb(name, shape, dt, stack)

        wring = eb("wring", [P, NW, KD * 512])
        hT = eb("hT", [P, KD, S])
        ones = eb("ones", [P, P])
        same = {b: eb(f"same{b}", [P, P]) for b in (2, 4, 8, 16, 32, 64)}
        level = {b: eb(f"level{b}", [P, P]) for b in (1, 2, 4, 8, 16, 32)}
        causal = eb("causal", [P, P])
        strict = eb("strict", [P, P])
        negmask = eb("negmask", [P, P])
        chunk_ones = eb("chunk_ones", [P, 2, P])
        iota_i = eb("iota_i", [P, P], I32)
        half_neg = eb("half_neg", [P, 2 * H])
        g1 = eb("g1", [P, KD])
        g2 = eb("g2", [P, KD])
        gcq = eb("gcq", [P, 3])
        gckv = eb("gckv", [P, 2])
        cw = eb("cw", [P, QKV // P, CONV])
        alog = eb("alog", [P, H])
        dtb = eb("dtb", [P, H])
        ggdn = eb("ggdn", [P, DK])
        gqk = eb("gqk", [P, 2, QK])
        pos_i = eb("pos_i", [P, TT], I32)
        oaT = eb("oaT", [P, HP, S])
        obT = eb("obT", [P, HP, S])
        ss = eb("ss", [P, TT])
        rs = eb("rs", [P, TT])
        ptok = eb("ptok", [P, TT, 16 + QL + KVL + ROPE])
        cos = eb("cos", [P, TT, ROPE // 2])
        sin = eb("sin", [P, TT, ROPE // 2])

        gdn = ExitStack()
        qkv = eb("qkv", [P, TT, QKV], stack=gdn)
        zs = eb("zs", [P, TT, 512], stack=gdn)
        beta = eb("beta", [P, TT, H], stack=gdn)
        gdec = eb("gdec", [P, TT, H], stack=gdn)
        gtmp = [eb(f"gtmp{i}", [P, TT, H], stack=gdn) for i in range(6)]
        ealog = eb("ealog", [P, H], stack=gdn)
        gsum = eb("gsum", [P, 4, TT * H], stack=gdn)
        eg = eb("eg", [P, TT, H], stack=gdn)
        ekd = eb("ekd", [P, TT, H], stack=gdn)
        egl = eb("egl", [P, 2, TT, H], stack=gdn)
        egp = eb("egp", [P, 2, TT, HP], stack=gdn)
        state = eb("state", [P, HP, 2, DK], stack=gdn)
        s1 = ExitStack()
        xt = eb("xt", [P, TT, D], stack=s1)
        xjunk = eb("xjunk", [P, D], stack=s1)
        cin = eb("cin", [P, 2, S + 3], stack=s1)
        cacc = eb("cacc", [P, 2, S], stack=s1)
        csil = eb("csil", [P, 2, S], stack=s1)
        s1.close()
        s2 = ExitStack()
        sq = eb("sq", [P, 2 * H, DK], stack=s2)
        ms = eb("ms", [P, 2 * H], stack=s2)
        rn = eb("rn", [P, 2 * H], stack=s2)
        kb = eb("kb", [P, 512], stack=s2)
        oms = eb("oms", [P, H], stack=s2)
        orn = eb("orn", [P, H], stack=s2)
        kbg = eb("kbg", [P, 2, 512], stack=s2)
        kd = eb("kd", [P, 2, 512], stack=s2)
        qgT = eb("qgT", [P, 2, HP, P], stack=s2)
        offd = eb("offd", [P, 2, HP, P], stack=s2)
        qg = eb("qg", [P, 512], stack=s2)
        gm = eb("gm", [P, 2, HP, P], stack=s2)
        ysb = eb("ysb", [P, 2, HP, P], stack=s2)
        usb = eb("usb", [P, 512], stack=s2)
        wT = eb("wT", [P, HP, P], stack=s2)
        vn = eb("vn", [P, 512], stack=s2)
        otok = eb("otok", [P, 512], stack=s2)
        onrm = eb("onrm", [P, 512], stack=s2)
        s2.close()
        gdn.close()

        mla = ExitStack()
        cqT = eb("cqT", [P, 3, S], stack=mla)
        ckvT = eb("ckvT", [P, 2, S], stack=mla)
        rss = eb("rss", [P, 2, TT], stack=mla)
        rrs = eb("rrs", [P, 2, TT], stack=mla)
        qk = eb("qk", [P, 2 * H, QK], stack=mla)
        qsq = eb("qsq", [P, 2 * H, QK], stack=mla)
        qms = eb("qms", [P, 2 * H], stack=mla)
        qrn = eb("qrn", [P, 2 * H], stack=mla)
        ang = [eb(f"ang{i}", [P, TT, ROPE // 2], stack=mla) for i in range(6)]
        invf = eb("invf", [P, ROPE // 2], stack=mla)
        posf = eb("posf", [P, TT], stack=mla)
        rt = [eb(f"rt{i}", [P, 2 * H, ROPE // 2], stack=mla) for i in range(4)]
        qkT = eb("qkT", [QK, 2 * H, S], stack=mla)
        vtok = eb("vtok", [P, TT, H, DK], stack=mla)
        prob = eb("prob", [P, 2, S], stack=mla)
        pT = eb("pT", [P, 2, TT, P], stack=mla)
        mx = eb("mx", [P, 2 * TT * H], stack=mla)
        nmx = eb("nmx", [P, TT * H], stack=mla)
        rsum = eb("rsum", [P, TT * H], stack=mla)
        rinv = eb("rinv", [P, TT * H], stack=mla)
        mla.close()

        mrg = ExitStack()
        siga = eb("siga", [P, TT, 512], stack=mrg)
        sigb = eb("sigb", [P, TT, 512], stack=mrg)
        mergedT = eb("mergedT", [P, KD, S], stack=mrg)
        x2 = eb("x2", [P, TT, D], stack=mrg)
        junk2 = eb("junk2", [P, D], stack=mrg)
        mrg.close()
        pk = ExitStack()
        h2T = hT
        skT = eb("skT", [P, SETS, NK], stack=pk)
        qTm = eb("qTm", [P, 2, S], stack=pk)
        sc = eb("sc", [P, TT, SETS, NK], stack=pk)
        sc2 = eb("sc2", [P, TT, NK], stack=pk)
        tops = eb("tops", [P, TT, SETS, PK], stack=pk)
        topi = eb("topi", [P, TT, SETS, PK], U32, stack=pk)
        topf = eb("topf", [P, TT, SETS, PK], stack=pk)
        cand = eb("cand", [P, H, NCAND], stack=pk)
        cand2 = eb("cand2", [P, H, NCAND], stack=pk)
        pick = eb("pick", [P, H, PK, PK], stack=pk)
        best = eb("best", [P, H, PK], stack=pk)
        bpos = eb("bpos", [P, H, PK], U32, stack=pk)
        apos = eb("apos", [P, 4, H, PK], U32, stack=pk)
        afl = eb("afl", [P, 4, H, PK], stack=pk)
        low = eb("low", [P, H, PK], stack=pk)
        sel = eb("sel", [P, 3, H, PK], stack=pk)
        gsm = eb("gsm", [P, 2, H], stack=pk)
        pk.close()
        early.close()

        spread = ExitStack()
        iota8 = sb("iota8", [P, NK, GT], F16, spread)
        colhot = sb("colhot", [P, 2, NK, GT], F16, spread)
        rowhot = sb("rowhot", [P, NK, GT], F16, spread)
        rowhi = sb("rowhi", [P, 2, NK, GT], F16, spread)
        rowlo = sb("rowlo", [P, 2, NK, GT], F16, spread)
        stage = sb("stage", [P, 2, NK, ST], F32, spread)
        spread.close()
        vph = ExitStack()
        w_hi = sb("w_hi", [P, 2, S], F32R, vph)
        w_lo = sb("w_lo", [P, 2, S], F32R, vph)
        gring = sb("gring", [P, 2, S // ST, CB, ST], F32, vph)
        vph.close()
        room = sb("room", [P, 8 * 1024])
        raw = sb("raw", [P, 2, D])
        opr_hi = sb("opr_hi", [P, 2, D], F32R)
        opr_lo = sb("opr_lo", [P, 2, D], F32R)
        act = sb("act", [P, ARENA, S])

        ps = ctx.enter_context(nc.psum_tensor("ps", [P, 8, 512], F32))

        ystage = gring[:, :, :, :, :].rearrange("p s a b c -> p (s a b c)").rearrange("p (k n) -> p k n", k=KD)
        y0T = act[:, GROUPS[2]:GROUPS[2] + KD, :]
        y1T = act[:, GROUPS[2] + KD:GROUPS[2] + 2 * KD, :]
        xb = act[:, GROUPS[2] + 2 * KD:GROUPS[2] + 3 * KD, :].rearrange("p (t a) n -> p t (a n)", t=TT)

        names = """consts_ready small_loaded mask_step
            sumsq_ready meansq_ready rstd_ready xn_ready xT_mm hT_ready
            qkv_mm conv_in conv_out silu_ready qkvT_mm qkv_tok
            tok_mm tok_taken dve_step act_step pool_step
            gates_in gates_exp gates_ready gsum_mm gsum_exp
            gms_ready grn_ready gderived gT_mm gT_taken gmask_ready grow_mm gexp_in gexp_ready gdecay_done
            gkk_mm gqk_mm gqk_taken guw_mm guw_taken
            gws_mm gvn_ready go_mm go_taken gup_mm gstate_ready onsq_ready onrs_ready onorm_ready oT_mm oT_taken gdn_over
            msq_ready mms_ready mrs_ready mcn_ready mcT_mm mcT_taken ang_ready trig_ready
            mproj_mm mproj_taken mqms_ready mqrs_ready mrope_ready mqT_mm mqT_taken
            score_mm negmax_ready prob_ready probn_ready pT_mm pT_taken av_mm av_taken mla_over
            ga_mm ga_sig gb_mm gb_sig y_mm merged_ready mT_mm mT_taken xo_mm x2_ready ss2_ready ms2_ready rs2_ready
            h2n_ready h2T_mm h2T_taken h2_hi h2_lo sk_mm sk_taken pq_mm pq_taken sc_mm sc_taken topk_ready
            best_ready gexp2_ready sel_ready selT_mm selT_taken early_over
            u_tmm u_hi u_lo u_mm act_ready onehot_ready rowhot_ready spread_mm gate_taken
            v_hi v_lo w_prod w_hi_ready w_ready v_mm y_copied ypre_ready yT_mm y_added""".split()
        s = {n: sem(n) for n in names}
        offd_ready, y_mm, y_taken, lev_mm, lev_done = ([sem(f"g{n}{par}") for par in range(2)] for n in
                                                       ("offd_ready", "y_mm", "y_taken", "lev_mm", "lev_done"))
        w_loaded = [sem(f"w_loaded{i}") for i in range(NW)]
        w_used = sem("w_used")
        x_loaded = [sem(f"x_loaded{t}") for t in range(TT)]
        raw_loaded = [sem(f"raw_loaded{i}") for i in range(2)]
        gate_stored = [sem(f"gate_stored{i}") for i in range(2)]
        gate_loaded = [sem(f"gate_loaded{i}") for i in range(2)]
        y_stored = sem("y_stored")
        x2_stored = sem("x2_stored")
        y_loaded = sem("y_loaded")
        out_stored = sem("out_stored")

        panels = []
        for n in range(3):
            panels.append(("qkv_mm", 4 * (n + 1), [(w_in_d[:, :, n * 512:(n + 1) * 512], 0, KD, 512)]))
        PAN_TOK = len(panels)
        TOK = [(OFF_Z, 512), (OFF_BA, 16 + QL), (OFF_CKV, KVL + ROPE)]
        for n, (at, w) in enumerate(TOK):
            panels.append(("tok_mm", TT * (n + 1), [(w_in_d[:, :, at:at + w], 0, KD, w)]))
        PAN_UQ = len(panels)
        panels.append(("mproj_mm", TT, [(w_uq_d, 0, 3, H * QK)]))
        PAN_UKV = len(panels)
        panels.append(("mproj_mm", TT, [(w_ukv_d, 0, 2, H * 2 * DK)]))
        PAN_MERGE = len(panels)
        for n in range(2):
            for g, name in enumerate(("ga_mm", "gb_mm")):
                at = OFF_GATES + g * D + n * 512
                panels.append((name, TT * (n + 1), [(w_in_d[:, :, at:at + 512], 0, KD, 512)]))
            panels.append(("y_mm", TT * (n + 1), [(w_gdn_d[:, :, n * 512:(n + 1) * 512], 0, HP, 512),
                                                  (w_mla_d[:, :, n * 512:(n + 1) * 512], HP * 512, HP, 512)]))
        PAN_O = len(panels)
        for n in range(2):
            panels.append(("xo_mm", TT * (n + 1), [(w_o_d[:, :, n * 512:(n + 1) * 512], 0, KD, 512)]))
        PAN_SK = len(panels)
        panels.append(("sk_mm", SETS // 4, [(sk_d, 0, SETS, NK)]))
        PAN_PQ = len(panels)
        for n in range(4):
            panels.append(("pq_mm", 4 * (n + 1), [(w_pq_d[:, :, n * 512:(n + 1) * 512], 0, KD, 512)]))

        def panel(n, k, w, at=0):
            return wring[:, n % NW, at:at + k * w].rearrange("p (k w) -> p k w", k=k)

        def loads_by(n):
            return sum(16 * len(panels[m][2]) for m in range(n % NW, n + 1, NW))

        def linker(eng, step):
            count = [0]

            def link(ins):
                count[0] += 1
                ins.then_inc(step, 1)
                eng.wait_ge(step, count[0])
            return link

        block = ctx.enter_context(nc.Block())
        bc = lambda ap, n, at: ap.unsqueeze(at).to_broadcast(list(ap.shape[:at]) + [n] + list(ap.shape[at:]))

        @block.sync
        def _(sp):
            for t in range(TT):
                sp.dma_start(xt[:, t, :], x_d[:, t, :]).then_inc(x_loaded[t], 16)
            for n, (_, _, parts) in enumerate(panels):
                if n == PAN_PQ + 1:
                    sp.wait_ge(s["x2_ready"], 2 * TT)
                    sp.dma_start(out_d, x2[:, :, :]).then_inc(x2_stored, 16)
                if n >= NW:
                    sp.wait_ge(s[panels[n - NW][0]], panels[n - NW][1])
                if n == PAN_MERGE:
                    sp.wait_ge(s["mla_over"], 4)
                    sp.dma_start(x2[:, :, :], x_d).then_inc(x_loaded[0], 16)
                for src, at, k, w in parts:
                    sp.dma_start(panel(n, k, w, at), src).then_inc(w_loaded[n % NW], 16)
            sp.wait_ge(x2_stored, 16)
            sp.wait_ge(s["early_over"], 4)

            def gate_piece(slot, b):
                sp.dma_start(gring[:, slot, :, :, :].rearrange("p g i t -> p g (i t)"),
                             g_d[:, :, bass.ds(b, CB), :].rearrange("g p i t -> p g (i t)"))\
                  .then_inc(gate_loaded[slot], 16)

            base = 0
            for g, size in enumerate(GROUPS):
                for sl in range(2):
                    if g:
                        sp.wait_ge(s["v_lo"], base - 1 + sl)
                    sp.dma_start(raw[:, sl, :], u_d[(base + sl) * P:(base + sl + 1) * P, :]).then_inc(raw_loaded[sl], 16)
                if g:
                    for k in range(KD):
                        sp.wait_ge(s["y_copied"], (g - 1) * KD + k + 1)
                    sp.dma_start(y_d[g - 1], ystage).then_inc(y_stored, 16)
                if g == 2:
                    sp.wait_ge(s["v_mm"], base)
                    sp.wait_ge(y_stored, 32)
                    sp.dma_start(y0T, y_d[0]).then_inc(y_loaded, 16)
                    sp.dma_start(y1T, y_d[1]).then_inc(y_loaded, 16)
                    sp.dma_start(xb, out_d).then_inc(y_loaded, 16)
                with sp.Fori(1, size // 2) as it:
                    for sl in range(2):
                        sp.wait_ge(s["u_tmm"], 2 * it + (base - 1 + sl))
                        sp.dma_start(raw[:, sl, :], u_d[bass.ds((2 * it + (base + sl)) * P, P), :])\
                          .then_inc(raw_loaded[sl], 16)
                for sl in range(2):
                    sp.wait_ge(s["u_tmm"], base + size - 1 + sl)
                    sp.dma_start(raw[:, sl, :], v_d[(base + sl) * P:(base + sl + 1) * P, :]).then_inc(raw_loaded[sl], 16)
                if g:
                    sp.wait_ge(y_stored, 16 * g)
                else:
                    for slot in range(2):
                        sp.wait_ge(gate_stored[slot], 16 * (S // ST // 2))
                    sp.wait_ge(s["spread_mm"], NG)
                gate_piece(0, base)
                gate_piece(1, base + CB)

                def values(b, sl):
                    sp.wait_ge(s["v_lo"], b - 1)
                    sp.dma_start(raw[:, sl, :], v_d[bass.ds(b * P, P), :]).then_inc(raw_loaded[sl], 16)

                for k in range(2, 2 * CB):
                    values(base + k, k % 2)
                with sp.Fori(1, size // (2 * CB)) as it:
                    b = it * (2 * CB)
                    for k in range(2 * CB):
                        values(b + (base + k), k % 2)
                        if k % CB == 0:
                            sp.wait_ge(s["w_prod"], b + (base + k - CB))
                            gate_piece(k // CB, b + (base + k))
                base += size
            for t in range(TT):
                sp.wait_ge(s["y_added"], 2 * (t + 1))
                sp.dma_start(out_d[:, t, :], xb[:, t, :]).then_inc(out_stored, 16)
            sp.wait_ge(out_stored, 16 * TT)

        @block.tensor
        def _(pe):
            def take_panel(n, *shape):
                pe.wait_ge(w_loaded[n % NW], loads_by(n))
                return panel(n, *shape)

            pe.wait_ge(s["consts_ready"], 1)
            for u in range(2 * TT):
                t, hf = divmod(u, 2)
                if not hf:
                    pe.wait_ge(s["xn_ready"], t + 1)
                if u >= 2:
                    pe.wait_ge(s["hT_ready"], u - 1)
                for b in range(4):
                    last = pe.transpose(ps[:, u % 2, b * P:(b + 1) * P], xt[:, t, (4 * hf + b) * P:(4 * hf + b + 1) * P], ident[:, :])
                last.then_inc(s["xT_mm"], 1)
            pe.wait_ge(s["hT_ready"], 2 * TT)

            NB = QKV // P
            for m in range(NB + 2):
                if m < NB:
                    if m % 4 == 0:
                        wp = take_panel(m // 4, KD, 512)
                    if m >= 2:
                        pe.wait_ge(s["conv_in"], m - 1)
                    for k in range(KD):
                        last = pe.matmul(ps[:, 2 + m % 2, :], wp[:, k, (m % 4) * P:(m % 4 + 1) * P], hT[:, k, :],
                                         start=k == 0, stop=k == KD - 1)
                    last.then_inc(s["qkv_mm"], 1)
                if m >= 2:
                    j = m - 2
                    pe.wait_ge(s["silu_ready"], j + 1)
                    if j >= 2:
                        pe.wait_ge(s["qkv_tok"], j - 1)
                    for t in range(TT):
                        last = pe.transpose(ps[:, 4 + j % 2, t * P:(t + 1) * P], csil[:, j % 2, t * P:(t + 1) * P], ident[:, :])
                    last.then_inc(s["qkvT_mm"], 1)
            for n, (_, w) in enumerate(TOK):
                wp = take_panel(PAN_TOK + n, KD, w)
                for t in range(TT):
                    u = n * TT + t
                    if u >= 2:
                        pe.wait_ge(s["tok_taken"], u - 1)
                    for k in range(KD):
                        last = pe.matmul(ps[:, 6 + u % 2, 0:w], hT[:, k, t * P:(t + 1) * P], wp[:, k, :],
                                         start=k == 0, stop=k == KD - 1)
                    last.then_inc(s["tok_mm"], 1)

            pe.wait_ge(s["consts_ready"], 2)
            pe.wait_ge(s["gates_ready"], 1)
            gflat = gdec[:, :, :].rearrange("p t h -> p (t h)")
            for i, m in enumerate((causal[:, :], same[64][:, :], chunk_ones[:, 0, :], chunk_ones[:, 1, :])):
                last = pe.matmul(ps[:, 0, i * 32:(i + 1) * 32], m, gflat, start=True, stop=True)
            last.then_inc(s["gsum_mm"], 1)
            pe.wait_ge(s["gsum_exp"], 1)
            pe.wait_ge(s["conv_in"], NB)
            pe.wait_ge(s["qkv_tok"], NB)
            pe.wait_ge(s["tok_taken"], 3 * TT)
            def decay_rows(t):
                pe.wait_ge(s["gmask_ready"], t + 1)
                for par in range(2):
                    last = pe.matmul(ps[:, par, :], ones[:, :], gm[:, par, :, :].rearrange("p a b -> p (a b)"),
                                     start=True, stop=True)
                last.then_inc(s["grow_mm"], 1)

            def scan_carry(t, c):
                n = 2 * t + c
                r = slice(c * CH, (c + 1) * CH)
                pe.wait_ge(s["guw_taken"], 2 * (t + 1))
                pe.wait_ge(s["gstate_ready"], n + 1)
                if n:
                    pe.wait_ge(s["go_taken"], n)
                for hp in range(HP):
                    last = pe.matmul(ps[r, 0, hp * P:(hp + 1) * P], wT[:, hp, r],
                                     state[:, hp, :, :].rearrange("p a d -> p (a d)"), start=True, stop=True)
                last.then_inc(s["gws_mm"], 1)

            def scan_update(t, c):
                n = 2 * t + c
                r = slice(c * CH, (c + 1) * CH)
                pe.wait_ge(s["gvn_ready"], n + 1)
                for hp in range(HP):
                    last = pe.matmul(ps[:, 1, hp * P:(hp + 1) * P], kd[r, t % 2, hp * P:(hp + 1) * P], vn[r, hp * P:(hp + 1) * P],
                                     start=True, stop=True)
                last.then_inc(s["gup_mm"], 1)
                for hp in range(HP):
                    pe.matmul(ps[r, 0, hp * P:(hp + 1) * P], qgT[:, t % 2, hp, r],
                              state[:, hp, :, :].rearrange("p a d -> p (a d)"), start=True, stop=False)
                    for par in range(2):
                        h = 2 * hp + par
                        last = pe.matmul(ps[r, 0, h * DK:(h + 1) * DK], attnT[:, t % 2, par, hp, r], vn[:, h * DK:(h + 1) * DK],
                                         start=False, stop=par == 1)
                last.then_inc(s["go_mm"], 1)

            def out_transposes(t):
                pe.wait_ge(s["onorm_ready"], t + 1)
                for hp in range(HP):
                    last = pe.transpose(ps[:, 4, hp * P:(hp + 1) * P], onrm[:, hp * P:(hp + 1) * P], ident[:, :])
                last.then_inc(s["oT_mm"], 1)

            decay_rows(0)
            for t in range(TT):
                pe.wait_ge(s["gderived"], t + 1)
                pe.wait_ge(s["gexp_in"], t + 1)
                srcs = (qkv[:, t, 512:1024], kb[:, :], qkv[:, t, 0:512], qg[:, :])
                for i, src in enumerate(srcs):
                    for hp in range(HP):
                        last = pe.transpose(ps[:, i, hp * P:(hp + 1) * P], src[:, hp * P:(hp + 1) * P], ident[:, :])
                    last.then_inc(s["gT_mm"], 1)
                for par in range(2):
                    r = slice(par * DK, (par + 1) * DK)
                    pe.wait_ge(s["gT_taken"], 4 * t + 2)
                    for hp in range(HP):
                        last = pe.matmul(ps[:, 6 + par, hp * P:(hp + 1) * P], tposed[r, 0, hp, :], tposed[r, 1, hp, :],
                                         start=True, stop=True)
                    last.then_inc(s["gkk_mm"], 1)
                pe.wait_ge(s["gT_taken"], 4 * t + 4)
                if t >= 2:
                    pe.wait_ge(s["oT_taken"], t - 1)
                for par in range(2):
                    r = slice(par * DK, (par + 1) * DK)
                    for hp in range(HP):
                        last = pe.matmul(ps[:, 4 + par, hp * P:(hp + 1) * P], tposed[r, 0, hp, :], tposed[r, 2, hp, :],
                                         start=True, stop=True)
                last.then_inc(s["gqk_mm"], 1)
                for lv in range(6):
                    for par in range(2):
                        pe.wait_ge(offd_ready[par], 6 * t + lv + 1)
                        if lv:
                            pe.wait_ge(lev_done[par], 6 * t + lv)
                        for hp in range(HP):
                            last = pe.matmul(ps[:, 2 + par, hp * P:(hp + 1) * P], offd[:, par, hp, :],
                                             inv[:, par, hp, :] if lv else ident[:, :], start=True, stop=True)
                        last.then_inc(y_mm[par], 1)
                    if lv == 1:
                        pe.wait_ge(s["gqk_taken"], t + 1)
                    for par in range(2 if lv else 0):
                        pe.wait_ge(y_taken[par], 5 * t + lv)
                        for hp in range(HP if lv < 5 else 0):
                            pe.matmul(ps[:, 4 + par, hp * P:(hp + 1) * P], invT[:, par, hp, :], ysb[:, par, hp, :],
                                      start=True, stop=True)
                        for hp in range(HP):
                            last = pe.matmul(ps[:, 6 + par, hp * P:(hp + 1) * P], ysb[:, par, hp, :], invT[:, par, hp, :],
                                             start=True, stop=True)
                        last.then_inc(lev_mm[par], 1)
                    if t and lv in (0, 2):
                        scan_carry(t - 1, lv // 2)
                    if t and lv in (1, 3):
                        scan_update(t - 1, lv // 2)
                    if lv == 4 and t + 1 < TT:
                        if t:
                            pe.wait_ge(s["go_taken"], 2 * t)
                            pe.wait_ge(s["gstate_ready"], 2 * t + 1)
                        decay_rows(t + 1)
                for par in range(2):
                    pe.wait_ge(lev_done[par], 6 * (t + 1))
                for hp in range(HP):
                    for par in range(2):
                        h = 2 * hp + par
                        pe.matmul(ps[:, 2, h * DK:(h + 1) * DK], invT[:, par, hp, :], qkv[:, t, 1024 + h * DK:1024 + (h + 1) * DK],
                                  start=True, stop=True)
                        last = pe.matmul(ps[par * DK:(par + 1) * DK, 3, hp * P:(hp + 1) * P], kbg[:, t % 2, h * DK:(h + 1) * DK],
                                         invT[:, par, hp, :], start=True, stop=True)
                last.then_inc(s["guw_mm"], 1)
                if t:
                    out_transposes(t - 1)
                pe.wait_ge(s["guw_taken"], 2 * (t + 1))
            for c in range(2):
                scan_carry(TT - 1, c)
                scan_update(TT - 1, c)
            pe.wait_ge(s["oT_taken"], TT - 1)
            out_transposes(TT - 1)

            pe.drain().then_inc(s["gdn_over"], 1)
            pe.wait_ge(s["gdn_over"], 4)
            for t in range(TT):
                pe.wait_ge(s["mcn_ready"], t + 1)
                if t >= 2:
                    pe.wait_ge(s["mcT_taken"], t - 1)
                a = 2 * (t % 2)
                for b in range(3):
                    pe.transpose(ps[:, a, b * P:(b + 1) * P], ptok[:, t, 16 + b * P:16 + (b + 1) * P], ident[:, :])
                for b in range(2):
                    last = pe.transpose(ps[:, a + 1, b * P:(b + 1) * P],
                                        ptok[:, t, 16 + QL + b * P:16 + QL + (b + 1) * P], ident[:, :])
                last.then_inc(s["mcT_mm"], 1)
            pe.wait_ge(s["mcT_taken"], TT)
            wq = take_panel(PAN_UQ, 3, H * QK)
            wkv = take_panel(PAN_UKV, 2, H * 2 * DK)
            for t in range(TT + 1):
                if t < TT:
                    if t:
                        pe.wait_ge(s["mproj_taken"], 4 * t)
                    for bank, w, src, n0, n1 in ((4, wq, cqT, 0, 512), (5, wq, cqT, 512, 768),
                                                 (6, wkv, ckvT, 0, 512), (7, wkv, ckvT, 512, 1024)):
                        nk = src.shape[1]
                        for k in range(nk):
                            last = pe.matmul(ps[:, bank, 0:n1 - n0], src[:, k, t * P:(t + 1) * P], w[:, k, n0:n1],
                                             start=k == 0, stop=k == nk - 1)
                    last.then_inc(s["mproj_mm"], 1)
                if t:
                    j = t - 1
                    pe.wait_ge(s["mrope_ready"], j + 1)
                    if j:
                        pe.wait_ge(s["mqT_taken"], 4 * j)
                    for b in range(4):
                        for i in range(4):
                            last = pe.transpose(ps[0:QK, b, i * P:(i + 1) * P], qk[:, 4 * b + i, :], ident[:, :])
                        last.then_inc(s["mqT_mm"], 1)
            pe.wait_ge(s["mqT_taken"], 4 * TT)
            NU = TT * H
            for i in range(NU + 2):
                if i < NU:
                    t, h = divmod(i, H)
                    if i >= 2:
                        pe.wait_ge(s["prob_ready"], i - 1)
                    pe.matmul(ps[:, 4 + i % 2, 0:(t + 1) * P], qkT[:, h, t * P:(t + 1) * P], qkT[:, H + h, 0:(t + 1) * P],
                              start=True, stop=True).then_inc(s["score_mm"], 1)
                if 1 <= i <= NU:
                    j = i - 1
                    t = j // H
                    pe.wait_ge(s["probn_ready"], j + 1)
                    if j >= 2:
                        pe.wait_ge(s["pT_taken"], j - 1)
                    for k in range(t + 1):
                        last = pe.transpose(ps[:, 6 + j % 2, k * P:(k + 1) * P], prob[:, j % 2, k * P:(k + 1) * P], ident[:, :])
                    last.then_inc(s["pT_mm"], 1)
                if i >= 2:
                    j = i - 2
                    t, h = divmod(j, H)
                    hp, par = divmod(h, 2)
                    pe.wait_ge(s["pT_taken"], j + 1)
                    if h == 0 and t >= 2:
                        pe.wait_ge(s["av_taken"], t - 1)
                    for k in range(t + 1):
                        last = pe.matmul(ps[par * DK:(par + 1) * DK, t % 2, hp * P:(hp + 1) * P], vtok[:, k, h, :],
                                         pT[:, j % 2, k, :], start=k == 0, stop=k == t)
                    last.then_inc(s["av_mm"], 1)
            pe.drain().then_inc(s["mla_over"], 1)
            pe.wait_ge(s["mla_over"], 4)
            for n in range(2):
                for g, (name, taken) in enumerate((("ga_mm", "ga_sig"), ("gb_mm", "gb_sig"))):
                    wp = take_panel(PAN_MERGE + 3 * n + g, KD, 512)
                    for t in range(TT):
                        u = n * TT + t
                        if u >= 2:
                            pe.wait_ge(s[taken], u - 1)
                        for k in range(KD):
                            last = pe.matmul(ps[:, 2 * g + u % 2, :], hT[:, k, t * P:(t + 1) * P], wp[:, k, :],
                                             start=k == 0, stop=k == KD - 1)
                        last.then_inc(s[name], 1)
                wp = take_panel(PAN_MERGE + 3 * n + 2, KD, 512)
                for t in range(TT + 1):
                    if t < TT:
                        u = n * TT + t
                        if u:
                            pe.wait_ge(s["merged_ready"], u)
                        for b, src in enumerate((oaT, obT)):
                            for k in range(HP):
                                last = pe.matmul(ps[:, 4 + b, :], src[:, k, t * P:(t + 1) * P], wp[:, b * HP + k, :],
                                                 start=k == 0, stop=k == HP - 1)
                        last.then_inc(s["y_mm"], 1)
                    if t:
                        u = n * TT + t - 1
                        pe.wait_ge(s["merged_ready"], u + 1)
                        if u >= 2:
                            pe.wait_ge(s["mT_taken"], u - 1)
                        for b in range(4):
                            last = pe.transpose(ps[:, 6 + u % 2, b * P:(b + 1) * P], siga[:, t - 1, b * P:(b + 1) * P], ident[:, :])
                        last.then_inc(s["mT_mm"], 1)
            pe.wait_ge(s["mT_taken"], 2 * TT)
            for n in range(2):
                wp = take_panel(PAN_O + n, KD, 512)
                for t in range(TT):
                    u = n * TT + t
                    if u >= 2:
                        pe.wait_ge(s["x2_ready"], u - 1)
                    for k in range(KD):
                        last = pe.matmul(ps[:, u % 2, :], mergedT[:, k, t * P:(t + 1) * P], wp[:, k, :],
                                         start=k == 0, stop=k == KD - 1)
                    last.then_inc(s["xo_mm"], 1)
            wp = take_panel(PAN_SK, SETS, NK)
            for u in range(SETS // 4):
                if u >= 2:
                    pe.wait_ge(s["sk_taken"], u - 1)
                for b in range(4):
                    last = pe.transpose(ps[:, 2 + u % 2, b * P:(b + 1) * P], wp[:, 4 * u + b, :], ident[:, :])
                last.then_inc(s["sk_mm"], 1)
            pe.wait_ge(s["x2_ready"], 2 * TT)
            for u in range(2 * TT):
                t, hf = divmod(u, 2)
                pe.wait_ge(s["h2n_ready"], t + 1)
                if u >= 2:
                    pe.wait_ge(s["h2T_taken"], u - 1)
                for b in range(4):
                    last = pe.transpose(ps[:, u % 2, b * P:(b + 1) * P], x2[:, t, (4 * hf + b) * P:(4 * hf + b + 1) * P], ident[:, :])
                last.then_inc(s["h2T_mm"], 1)
            pe.wait_ge(s["h2T_taken"], 2 * TT)
            pe.wait_ge(s["sk_taken"], SETS // 4)
            for m in range(SETS + 1):
                if m < SETS:
                    if m % 4 == 0:
                        wp = take_panel(PAN_PQ + m // 4, KD, 512)
                    if m >= 2:
                        pe.wait_ge(s["pq_taken"], m - 1)
                    for k in range(KD):
                        last = pe.matmul(ps[:, 4 + m % 2, :], wp[:, k, (m % 4) * P:(m % 4 + 1) * P], h2T[:, k, :],
                                         start=k == 0, stop=k == KD - 1)
                    last.then_inc(s["pq_mm"], 1)
                if m:
                    j = m - 1
                    pe.wait_ge(s["pq_taken"], j + 1)
                    if j >= 2:
                        pe.wait_ge(s["sc_taken"], j - 1)
                    for t in range(TT):
                        last = pe.matmul(ps[:, 6 + j % 2, t * P:(t + 1) * P], qTm[:, j % 2, t * P:(t + 1) * P], skT[:, j, :],
                                         start=True, stop=True)
                    last.then_inc(s["sc_mm"], 1)
            pe.drain().then_inc(s["early_over"], 1)
            pe.wait_ge(s["early_over"], 4)

            def selection(t):
                pe.wait_ge(s["sel_ready"], t + 1)
                if t:
                    pe.wait_ge(s["selT_taken"], t)
                for i in range(3):
                    last = pe.transpose(ps[:, 6, i * P:(i + 1) * P], sel[:, i, :, :].rearrange("p h k -> p (h k)"), ident[:, :])
                last.then_inc(s["selT_mm"], 1)

            def u_transposes(sl, use):
                pe.wait_ge(raw_loaded[sl], use)
                for k in range(KD):
                    last = pe.transpose(ps[:, 2 * sl + k // 4, (k % 4) * P:(k % 4 + 1) * P], raw[:, sl, k * P:(k + 1) * P], ident[:, :])
                last.then_inc(s["u_tmm"], 1)

            def u_products(sl, n, k0=0, k1=KD):
                if not k0:
                    pe.wait_ge(s["u_lo"], n)
                for k in range(k0, k1):
                    c = slice(k * P, (k + 1) * P)
                    pe.matmul(ps[:, 4 + sl, :], opr_hi[:, sl, c], h2hi[:, k, :], start=k == 0, stop=False)
                    pe.matmul(ps[:, 4 + sl, :], opr_hi[:, sl, c], h2lo[:, k, :], start=False, stop=False)
                    last = pe.matmul(ps[:, 4 + sl, :], opr_lo[:, sl, c], h2hi[:, k, :], start=False, stop=k == KD - 1)
                if k1 == KD:
                    last.then_inc(s["u_mm"], 1)

            def spread_gates(g, slot, first=False):
                pe.wait_ge(s["onehot_ready"], g + 1)
                for b in range(2):
                    if not first:
                        pe.wait_ge(s["gate_taken"], 2 * g - 1 + b)
                    for j in range(4):
                        o = ps[:, 6 + b, j * P:(j + 1) * P]
                        pe.matmul(o, colhot[:, slot, :, 4 * b + j], rowhi[:, slot, :, 4 * b + j], start=True, stop=False)
                        last = pe.matmul(o, colhot[:, slot, :, 4 * b + j], rowlo[:, slot, :, 4 * b + j], start=False, stop=True)
                last.then_inc(s["spread_mm"], 1)

            def u_spread(i, use, sl, first=False):
                u_transposes(1 - sl, use)
                j = i - LEAD
                u_products(sl, i + 1, 0, KD // 2)
                spread_gates(2 * j, 0, first)
                u_products(sl, i + 1, KD // 2, KD)
                spread_gates(2 * j + 1, 1)

            def v_products(sl, n, first, final):
                pe.wait_ge(s["v_lo"], n)
                pe.wait_ge(s["w_ready"], n)
                for k in range(KD):
                    c = slice(k * P, (k + 1) * P)
                    pe.matmul(ps[:, k, :], opr_hi[:, sl, c], w_hi[:, sl, :], start=first, stop=False)
                    pe.matmul(ps[:, k, :], opr_hi[:, sl, c], w_lo[:, sl, :], start=False, stop=False)
                    last = pe.matmul(ps[:, k, :], opr_lo[:, sl, c], w_hi[:, sl, :], start=False, stop=final)
                last.then_inc(s["v_mm"], 1)

            base = uses = 0
            for g, size in enumerate(GROUPS):
                if g:
                    pe.wait_ge(s["y_copied"], (g - 1) * KD + 2)
                u_transposes(0, 16 * (uses + 1))
                if g == 0:
                    for i in range(LEAD):
                        u_transposes(1 - i % 2, 16 * ((i + 1) // 2 + 1))
                        u_products(i % 2, i + 1)
                        if (i >= PARTS and i % PARTS == 0) or i == LEAD - 1:
                            selection((i + 1) // PARTS - 1)
                    pe.wait_ge(s["selT_taken"], TT)
                    for sl in range(2):
                        u_spread(LEAD + sl, 16 * ((LEAD + sl + 1) // 2 + 1), sl, first=not sl)
                    with pe.Fori(LEAD // 2 + 1, (LEAD + SPREAD) // 2) as it:
                        for sl in range(2):
                            u_spread(2 * it + sl, 16 * it + 16 * (1 + sl), sl)
                    for i in range(LEAD + SPREAD, size):
                        if i < size - 1:
                            u_transposes(1 - i % 2, 16 * ((i + 1) // 2 + 1))
                        u_products(i % 2, i + 1)
                    pe.wait_ge(s["gate_taken"], 2 * NG)
                else:
                    pe.wait_ge(s["y_copied"], g * KD)
                    with pe.Fori(0, size // 2 - 1) as it:
                        u_transposes(1, 16 * it + 16 * (uses + 1))
                        u_products(0, 2 * it + (base + 1))
                        u_transposes(0, 16 * it + 16 * (uses + 2))
                        u_products(1, 2 * it + (base + 2))
                    u_transposes(1, 16 * (uses + size // 2))
                    u_products(0, base + size - 1)
                    u_products(1, base + size)
                pe.wait_ge(s["act_ready"], base + size)
                v_products(0, base + 1, True, False)
                v_products(1, base + 2, False, False)
                with pe.Fori(1, size // 2 - 1) as it:
                    v_products(0, 2 * it + (base + 1), False, False)
                    v_products(1, 2 * it + (base + 2), False, False)
                v_products(0, base + size - 1, False, False)
                v_products(1, base + size, False, True)
                base += size
                uses += size
            pe.wait_ge(s["y_copied"], 3 * KD)
            for u in range(2 * TT):
                t, hf = divmod(u, 2)
                if u >= 2:
                    pe.wait_ge(s["y_added"], u - 1)
                for b in range(4):
                    last = pe.transpose(ps[:, u % 2, b * P:(b + 1) * P], y0T[:, 4 * hf + b, t * P:(t + 1) * P], ident[:, :])
                last.then_inc(s["yT_mm"], 1)

        @block.scalar
        def _(act_e):
            link = linker(act_e, s["act_step"])
            A = nc.scalar.activation
            with nc.allow_non_contiguous_dma(reason="small vectors onto partitions"):
                col = lambda v: v.rearrange("l (k p) -> p (l k)", p=P)
                row = lambda v, n: v.to_broadcast([P, n])
                loads = [(g1[:, :], col(norm1_g)), (g2[:, :], col(norm2_g)), (gcq[:, :], col(cq_norm_g)),
                         (gckv[:, :], col(ckv_norm_g)),
                         (alog[:, :], row(a_log, H)), (dtb[:, :], row(dt_bias, H)), (ggdn[:, :], row(gdn_norm_g, DK)),
                         (gqk[:, 0, :], row(q_norm_g, QK)), (gqk[:, 1, :], row(k_norm_g, QK)),
                         (pos_i[:, :], positions.rearrange("b (t p) -> p (b t)", p=P))]
                loads += [(cw[:, :, j], conv_w[:, j, :].rearrange("l (m p) -> p (l m)", p=P)) for j in range(CONV)]
                for dst, src in loads:
                    act_e.dma_start(dst, src).then_inc(s["small_loaded"], 16)
            small = 16 * len(loads)
            for t in range(TT):
                act_e.wait_ge(x_loaded[t], 16)
                link(A(xjunk[:, :], xt[:, t, :], ACT.Square, accum_out=ss[:, t:t + 1]))
                act_e.nop().then_inc(s["sumsq_ready"], 1)
            NB = QKV // P
            for m in range(NB + 1):
                if m < NB:
                    act_e.wait_ge(s["qkv_mm"], m + 1)
                    if m >= 2:
                        act_e.wait_ge(s["conv_out"], m - 1)
                    A(cin[:, m % 2, 3:], ps[:, 2 + m % 2, :], ACT.Copy).then_inc(s["conv_in"], 1)
                if m:
                    j = m - 1
                    act_e.wait_ge(s["conv_out"], j + 1)
                    if j >= 2:
                        act_e.wait_ge(s["qkvT_mm"], j - 1)
                    A(csil[:, j % 2, :], cacc[:, j % 2, :], ACT.Silu).then_inc(s["silu_ready"], 1)
            for n, (_, w) in enumerate(TOK):
                for t in range(TT):
                    u = n * TT + t
                    act_e.wait_ge(s["tok_mm"], u + 1)
                    src = ps[:, 6 + u % 2, 0:w]
                    if n == 0:
                        ins = A(zs[:, t, :], src, ACT.Silu)
                    elif n == 1:
                        ins = A(ptok[:, t, 0:w], src, ACT.Copy)
                    else:
                        ins = A(ptok[:, t, 16 + QL:16 + QL + w], src, ACT.Copy)
                    ins.then_inc(s["tok_taken"], 1)
            act_e.wait_ge(s["tok_taken"], 3 * TT)
            act_e.wait_ge(s["small_loaded"], small)
            link(A(beta[:, :, :], ptok[:, :, 0:H], ACT.Sigmoid))
            link(A(ealog[:, :], alog[:, :], ACT.Exp))
            act_e.wait_ge(s["gates_in"], 1)
            link(A(gtmp[2][:, :, :], gtmp[1][:, :, :], ACT.Exp))
            act_e.nop().then_inc(s["gates_exp"], 1)
            act_e.wait_ge(s["gates_in"], 2)
            link(A(gtmp[4][:, :, :], gtmp[3][:, :, :], ACT.Ln))
            act_e.nop().then_inc(s["gates_exp"], 1)
            act_e.wait_ge(s["gsum_mm"], 1)
            link(A(gsum[:, :, :], ps[:, 0, 0:P].rearrange("p (a b) -> p a b", a=4), ACT.Copy))
            link(A(eg[:, :, :].rearrange("p t h -> p (t h)"), gsum[:, 0, :], ACT.Exp))
            link(A(egl[:, :, :, :].rearrange("p c t h -> p (c t h)"), gsum[:, 2:4, :].rearrange("p a b -> p (a b)"), ACT.Exp))
            act_e.nop().then_inc(s["gsum_exp"], 1)
            act_e.wait_ge(s["gates_in"], 3)
            link(A(ekd[:, :, :], gtmp[5][:, :, :], ACT.Exp))
            act_e.nop().then_inc(s["gsum_exp"], 1)
            def decay_exp(t):
                act_e.wait_ge(s["gexp_in"], t + 1)
                A(decay[:, :, :, :], decay[:, :, :, :], ACT.Exp).then_inc(s["gexp_ready"], 1)

            def take_scan(t, c):
                r = slice(c * CH, (c + 1) * CH)
                act_e.wait_ge(s["go_mm"], 2 * t + c + 1)
                if t:
                    act_e.wait_ge(s["onorm_ready"], t)
                A(otok[r, :], ps[r, 0, :], ACT.Copy).then_inc(s["go_taken"], 1)

            def take_out(t):
                act_e.wait_ge(s["oT_mm"], t + 1)
                A(oaT[:, :, t * P:(t + 1) * P], ps[:, 4, :].rearrange("p (a b) -> p a b", a=HP), ACT.Copy).then_inc(s["oT_taken"], 1)

            decay_exp(0)
            for t in range(TT):
                for i in range(4):
                    act_e.wait_ge(s["gT_mm"], 4 * t + i + 1)
                    dst = tposed[:, i, :, :] if i < 3 else qgT[:, t % 2, :, :]
                    A(dst, ps[:, i, :].rearrange("p (a b) -> p a b", a=HP), ACT.Copy).then_inc(s["gT_taken"], 1)
                for lv in range(1, 6):
                    for par in range(2):
                        act_e.wait_ge(y_mm[par], 6 * t + lv + 1)
                        if 5 * t + lv > 1:
                            act_e.wait_ge(lev_mm[par], 5 * t + lv - 1)
                        A(ysb[:, par, :, :], ps[:, 2 + par, :].rearrange("p (b c) -> p b c", b=HP), ACT.Copy).then_inc(y_taken[par], 1)
                    if t and lv in (1, 3):
                        take_scan(t - 1, lv // 2)
                if t + 1 < TT:
                    decay_exp(t + 1)
                act_e.wait_ge(s["guw_mm"], t + 1)
                if t:
                    act_e.wait_ge(s["gvn_ready"], 2 * t)
                A(usb[:, :], ps[:, 2, :], ACT.Copy).then_inc(s["guw_taken"], 1)
                A(wT[:, :, :], ps[:, 3, :].rearrange("p (a b) -> p a b", a=HP), ACT.Copy).then_inc(s["guw_taken"], 1)
                if t:
                    take_out(t - 1)
            for c in range(2):
                take_scan(TT - 1, c)
            take_out(TT - 1)
            act_e.drain().then_inc(s["gdn_over"], 1)
            act_e.wait_ge(s["gdn_over"], 4)
            qf = qsq[:, :, :].rearrange("p a b -> p (a b)")
            for t in range(TT):
                link(A(qf[:, 0:QL], ptok[:, t, 16:16 + QL], ACT.Square, accum_out=rss[:, 0, t:t + 1]))
                link(A(qf[:, 0:KVL], ptok[:, t, 16 + QL:16 + QL + KVL], ACT.Square, accum_out=rss[:, 1, t:t + 1]))
            act_e.nop().then_inc(s["msq_ready"], 1)
            act_e.wait_ge(s["ang_ready"], 1)
            A(sin[:, :, :], ang[2][:, :, :], ACT.Sin).then_inc(s["trig_ready"], 1)
            A(cos[:, :, :], ang[5][:, :, :], ACT.Sin).then_inc(s["trig_ready"], 1)
            for t in range(TT):
                act_e.wait_ge(s["mproj_mm"], t + 1)
                if t:
                    act_e.wait_ge(s["mqT_mm"], 4 * t)
                A(qk[:, 0:H, :].rearrange("p a b -> p (a b)"), ps[:, 4:6, :].rearrange("p a b -> p (a b)")[:, 0:H * QK], ACT.Copy)\
                    .then_inc(s["mproj_taken"], 1)
                kv = ps[:, 6:8, :].rearrange("p a (h c) -> p (a h) c", c=2 * DK)
                A(qk[:, H:, 0:NOPE], kv[:, :, 0:NOPE], ACT.Copy).then_inc(s["mproj_taken"], 1)
                A(vtok[:, t, :, :], kv[:, :, NOPE:], ACT.Copy).then_inc(s["mproj_taken"], 1)
                A(qk[:, H:, NOPE:], bc(ptok[:, t, 16 + QL + KVL:], H, 1), ACT.Copy).then_inc(s["mproj_taken"], 1)
                for b in range(4):
                    act_e.wait_ge(s["mqT_mm"], 4 * t + b + 1)
                    A(qkT[:, 4 * b:4 * b + 4, t * P:(t + 1) * P], ps[0:QK, b, :].rearrange("p (a b) -> p a b", a=4), ACT.Copy)\
                        .then_inc(s["mqT_taken"], 1)
            NU = TT * H
            for i in range(NU + 1):
                if i < NU:
                    t = i // H
                    act_e.wait_ge(s["negmax_ready"], i + 1)
                    if i >= 2:
                        act_e.wait_ge(s["pT_mm"], i - 1)
                    A(prob[:, i % 2, 0:(t + 1) * P], ps[:, 4 + i % 2, 0:(t + 1) * P], ACT.Exp, bias=nmx[:, i:i + 1],
                      scale=QK ** -0.5, accum_out=rsum[:, i:i + 1]).then_inc(s["prob_ready"], 1)
                if i:
                    j = i - 1
                    t, h = divmod(j, H)
                    act_e.wait_ge(s["pT_mm"], j + 1)
                    if j >= 2:
                        act_e.wait_ge(s["av_mm"], j - 1)
                    A(pT[:, j % 2, 0:t + 1, :], ps[:, 6 + j % 2, 0:(t + 1) * P].rearrange("p (a b) -> p a b", b=P), ACT.Copy)\
                        .then_inc(s["pT_taken"], 1)
                    if h == 1 and t:
                        act_e.wait_ge(s["av_mm"], t * H)
                        A(obT[:, :, (t - 1) * P:t * P], ps[:, (t - 1) % 2, :].rearrange("p (a b) -> p a b", a=HP), ACT.Copy)\
                            .then_inc(s["av_taken"], 1)
            act_e.wait_ge(s["av_mm"], NU)
            A(obT[:, :, (TT - 1) * P:], ps[:, (TT - 1) % 2, :].rearrange("p (a b) -> p a b", a=HP), ACT.Copy)\
                .then_inc(s["av_taken"], 1)
            act_e.drain().then_inc(s["mla_over"], 1)
            act_e.wait_ge(s["mla_over"], 4)
            for n in range(2):
                for g, (name, taken, dst) in enumerate((("ga_mm", "ga_sig", siga), ("gb_mm", "gb_sig", sigb))):
                    if n:
                        act_e.wait_ge(s["mT_mm"], TT)
                    for t in range(TT):
                        u = n * TT + t
                        act_e.wait_ge(s[name], u + 1)
                        A(dst[:, t, :], ps[:, 2 * g + u % 2, :], ACT.Sigmoid).then_inc(s[taken], 1)
                for t in range(TT):
                    u = n * TT + t
                    act_e.wait_ge(s["mT_mm"], u + 1)
                    A(mergedT[:, 4 * n:4 * n + 4, t * P:(t + 1) * P], ps[:, 6 + u % 2, :].rearrange("p (a b) -> p a b", a=4), ACT.Copy)\
                        .then_inc(s["mT_taken"], 1)
            for t in range(TT):
                act_e.wait_ge(s["x2_ready"], TT + t + 1)
                link(A(junk2[:, :], x2[:, t, :], ACT.Square, accum_out=ss[:, t:t + 1]))
                act_e.nop().then_inc(s["ss2_ready"], 1)
            for u in range(SETS // 4):
                act_e.wait_ge(s["sk_mm"], u + 1)
                A(skT[:, 4 * u:4 * u + 4, :], ps[:, 2 + u % 2, :].rearrange("p (a b) -> p a b", a=4), ACT.Copy).then_inc(s["sk_taken"], 1)
            for u in range(2 * TT):
                t, hf = divmod(u, 2)
                act_e.wait_ge(s["h2T_taken"], u + 1)
                b = (slice(None), slice(4 * hf, 4 * hf + 4), slice(t * P, (t + 1) * P))
                A(h2hi[b], h2T[b], ACT.Copy).then_inc(s["h2_hi"], 1)
            for m in range(SETS + 1):
                if m < SETS:
                    act_e.wait_ge(s["pq_mm"], m + 1)
                    if m >= 2:
                        act_e.wait_ge(s["sc_mm"], m - 1)
                    A(qTm[:, m % 2, :], ps[:, 4 + m % 2, :], ACT.Copy).then_inc(s["pq_taken"], 1)
                if m:
                    j = m - 1
                    act_e.wait_ge(s["sc_mm"], j + 1)
                    A(sc[:, :, j, :], ps[:, 6 + j % 2, :].rearrange("p (t n) -> p t n", t=TT), ACT.Copy).then_inc(s["sc_taken"], 1)
            act_e.drain().then_inc(s["early_over"], 1)
            act_e.wait_ge(s["early_over"], 4)
            wide = lambda sl: ps[:, 2 * sl:2 * sl + 2, :].rearrange("p a b -> p (a b)")

            def u_hi(sl, n):
                act_e.wait_ge(s["u_tmm"], n)
                A(opr_hi[:, sl, :], wide(sl), ACT.Copy).then_inc(s["u_hi"], 1)

            def u_act(sl, n, at):
                act_e.wait_ge(s["u_mm"], n)
                A(act[:, at, :] if isinstance(at, int) else act[:, bass.ds(at, 1), :].rearrange("p a b -> p (a b)"),
                  ps[:, 4 + sl, :], ACT.Gelu).then_inc(s["act_ready"], 1)

            def take_gates(g, half, slot):
                act_e.wait_ge(s["spread_mm"], g + 1)
                for b in range(2):
                    at = half * GT + 4 * b
                    A(stage[:, slot, :, at:at + 4].rearrange("p i t -> p t i"), ps[:, 6 + b, :].rearrange("p (t i) -> p t i", t=4),
                      ACT.Copy, scale=1 / GSCALE).then_inc(s["gate_taken"], 1)

            def store_gates(j, slot):
                act_e.wait_ge(s["gate_taken"], 4 * j + 4)
                dst = g_d[bass.ds(j, 1)].rearrange("a p i t -> p (a i t)")
                act_e.dma_start(dst, stage[:, slot, :, :].rearrange("p i t -> p (i t)")).then_inc(gate_stored[slot], 16)

            def u_gates(i, sl, at, first=False, stored=None):
                u_act(1 - sl, i, at)
                j = i - LEAD
                if not first:
                    take_gates(2 * j - 1, 1, 1 - sl)
                    store_gates(j - 1, 1 - sl)
                u_hi(1 - sl, i + 2)
                if stored is not None:
                    act_e.wait_ge(gate_stored[sl], stored)
                take_gates(2 * j, 0, sl)

            def v_hi(sl, n, use):
                act_e.wait_ge(raw_loaded[sl], use)
                A(opr_hi[:, sl, :], raw[:, sl, :], ACT.Copy).then_inc(s["v_hi"], 1)
                act_e.wait_ge(s["w_prod"], n)
                a = act[:, bass.ds(n - 1 - base, 1), :].rearrange("p a b -> p (a b)")
                A(w_hi[:, sl, :], a, ACT.Copy).then_inc(s["w_hi_ready"], 1)

            base = uses = 0
            for g, size in enumerate(GROUPS):
                if g:
                    act_e.wait_ge(s["v_mm"], base)
                u_hi(0, base + 1)
                u_hi(1, base + 2)
                if g == 0:
                    for i in range(1, LEAD):
                        u_act((i - 1) % 2, i, i - 1)
                        u_hi((i + 1) % 2, i + 2)
                        if i % PARTS == 3:
                            act_e.wait_ge(s["best_ready"], i // PARTS + 1)
                            A(best[:, :, :], best[:, :, :], ACT.Exp).then_inc(s["gexp2_ready"], 1)
                    for sl in range(2):
                        u_gates(LEAD + sl, sl, LEAD + sl - 1, first=not sl)
                    with act_e.Fori(LEAD // 2 + 1, (LEAD + SPREAD) // 2) as it:
                        for sl in range(2):
                            u_gates(2 * it + sl, sl, 2 * it + (sl - 1), stored=it * 16 - 16 * (LEAD // 2))
                    for i in range(LEAD + SPREAD, size + 1):
                        u_act((i - 1) % 2, i, i - 1)
                        if i == LEAD + SPREAD:
                            take_gates(NG - 1, 1, 1)
                            store_gates(NG // 2 - 1, 1)
                        if i < size - 1:
                            u_hi((i + 1) % 2, i + 2)
                else:
                    with act_e.Fori(0, size // 2 - 1) as it:
                        for sl in range(2):
                            u_act(sl, 2 * it + (base + 1 + sl), 2 * it + sl)
                            u_hi(sl, 2 * it + (base + 3 + sl))
                    for sl in range(2):
                        u_act(sl, base + size - 1 + sl, size - 2 + sl)
                rb = uses + size // 2
                for sl in range(2):
                    v_hi(sl, base + 1 + sl, 16 * (rb + 1))
                with act_e.Fori(1, size // 2) as it:
                    for sl in range(2):
                        act_e.wait_ge(s["v_mm"], 2 * it + (base - 1 + sl))
                        v_hi(sl, 2 * it + (base + 1 + sl), 16 * it + 16 * (rb + 1))
                act_e.wait_ge(s["v_mm"], base + size)
                if g < 2:
                    for k in range(KD):
                        A(ystage[:, k, :], ps[:, k, :], ACT.Copy).then_inc(s["y_copied"], 1)
                base += size
                uses += size

        @block.vector
        def _(dve):
            link = linker(dve, s["dve_step"])
            V = nc.vector
            tt, ts, stt = V.tensor_tensor, V.tensor_scalar, V.scalar_tensor_tensor
            for t in range(TT):
                dve.wait_ge(s["sumsq_ready"], t + 1)
                ts(ss[:, t:t + 1], ss[:, t:t + 1], 1.0 / D, EPS, ALU.mult, ALU.add).then_inc(s["meansq_ready"], 1)
            for sl in range(2):
                link(V.memset(cin[:, sl, 0:3], 0.0))
            for t in range(TT):
                dve.wait_ge(s["rstd_ready"], t + 1)
                ts(xt[:, t, :], xt[:, t, :], rs[:, t:t + 1], None, ALU.mult).then_inc(s["xn_ready"], 1)
            dve.wait_ge(s["small_loaded"], 16 * 14)
            for u in range(2 * TT):
                t, hf = divmod(u, 2)
                dve.wait_ge(s["xT_mm"], u + 1)
                tt(hT[:, 4 * hf:4 * hf + 4, t * P:(t + 1) * P], ps[:, u % 2, :].rearrange("p (a b) -> p a b", a=4),
                   bc(g1[:, 4 * hf:4 * hf + 4], P, 2), ALU.mult).then_inc(s["hT_ready"], 1)
            NB = QKV // P
            for m in range(NB + 2):
                if m < NB:
                    dve.wait_ge(s["conv_in"], m + 1)
                    if m >= 2:
                        dve.wait_ge(s["silu_ready"], m - 1)
                    x0, acc = cin[:, m % 2, :], cacc[:, m % 2, :]
                    link(ts(acc, x0[:, 0:S], cw[:, m, 0:1], None, ALU.mult))
                    for j in (1, 2):
                        link(stt(acc, x0[:, j:j + S], cw[:, m, j:j + 1], acc, ALU.mult, ALU.add))
                    stt(acc, x0[:, 3:3 + S], cw[:, m, 3:4], acc, ALU.mult, ALU.add).then_inc(s["conv_out"], 1)
                if m >= 2:
                    j = m - 2
                    dve.wait_ge(s["qkvT_mm"], j + 1)
                    V.tensor_copy(qkv[:, :, j * P:(j + 1) * P], ps[:, 4 + j % 2, :].rearrange("p (t c) -> p t c", t=TT))\
                        .then_inc(s["qkv_tok"], 1)
            dve.wait_ge(s["tok_taken"], 3 * TT)
            araw = ptok[:, :, H:2 * H]
            link(tt(gtmp[0][:, :, :], araw, bc(dtb[:, :], TT, 1), ALU.add))
            link(ts(gtmp[1][:, :, :], gtmp[0][:, :, :], -1.0, None, ALU.mult))
            tt(gtmp[1][:, :, :], gtmp[0][:, :, :], gtmp[1][:, :, :], ALU.min).then_inc(s["gates_in"], 1)
            dve.wait_ge(s["gates_exp"], 1)
            ts(gtmp[3][:, :, :], gtmp[2][:, :, :], 1.0, None, ALU.add).then_inc(s["gates_in"], 1)
            dve.wait_ge(s["gates_in"], 2)
            link(ts(gtmp[5][:, :, :], gtmp[3][:, :, :], 1.0, 1e-30, ALU.subtract, ALU.max))
            link(V.reciprocal(gtmp[5][:, :, :], gtmp[5][:, :, :]))
            link(tt(gtmp[5][:, :, :], gtmp[5][:, :, :], gtmp[2][:, :, :], ALU.mult))
            dve.wait_ge(s["gates_exp"], 2)
            link(tt(gtmp[5][:, :, :], gtmp[5][:, :, :], gtmp[4][:, :, :], ALU.mult))
            link(ts(gtmp[0][:, :, :], gtmp[0][:, :, :], 0.0, None, ALU.max))
            link(tt(gtmp[5][:, :, :], gtmp[5][:, :, :], gtmp[0][:, :, :], ALU.add))
            link(tt(gtmp[5][:, :, :], gtmp[5][:, :, :], bc(ealog[:, :], TT, 1), ALU.mult))
            ts(gdec[:, :, :], gtmp[5][:, :, :], -1.0, None, ALU.mult).then_inc(s["gates_ready"], 1)
            dve.wait_ge(s["gsum_exp"], 1)
            fl = lambda ap: ap.rearrange("p t h -> p (t h)")
            tt(fl(gtmp[5][:, :, :]), gsum[:, 1, :], gsum[:, 0, :], ALU.subtract).then_inc(s["gates_in"], 1)
            for par in range(2):
                r = slice(par * DK, (par + 1) * DK)
                link(V.tensor_copy(egp[r, :, :, :], egl[r, :, :, :].rearrange("p c t (a b) -> p c t a b", b=2)[:, :, :, :, par]))
            link(V.memset(vn[:, :], 0.0))
            V.memset(state[:, :, :, :], 0.0).then_inc(s["gstate_ready"], 1)
            dve.wait_ge(s["consts_ready"], 2)
            dve.wait_ge(s["gsum_exp"], 2)
            h3 = lambda ap: ap.rearrange("p (h d) -> p h d", h=H)
            dec3 = decay[:, :, :, :].rearrange("p a b c -> p (a b) c")
            head = lambda b: ps[:, b, :].rearrange("p (b c) -> p b c", b=HP)
            id4 = bc(ident[:, :], HP, 1)

            def norms(t):
                qk2 = qkv[:, t, 0:1024].rearrange("p (h d) -> p h d", h=2 * H)
                link(tt(sq[:, :, :], qk2, qk2, ALU.mult))
                link(V.reduce_sum(ms[:, :], sq[:, :, :], AX.X))
                ts(ms[:, :], ms[:, :], EPS, None, ALU.add).then_inc(s["gms_ready"], 1)

            def derive(t):
                q2, k2, v2 = (h3(qkv[:, t, i * 512:(i + 1) * 512]) for i in range(3))
                qk2 = qkv[:, t, 0:1024].rearrange("p (h d) -> p h d", h=2 * H)
                b8 = lambda ap: bc(ap[:, t, :], DK, 2)
                dve.wait_ge(s["grn_ready"], t + 1)
                link(ts(rn[:, 0:H], rn[:, 0:H], DK ** -0.5, None, ALU.mult))
                link(tt(qk2, qk2, bc(rn[:, :], DK, 2), ALU.mult))
                link(tt(h3(kb[:, :]), k2, b8(beta), ALU.mult))
                tt(h3(kbg[:, t % 2, :]), h3(kb[:, :]), b8(eg), ALU.mult)
                tt(h3(kd[:, t % 2, :]), k2, b8(ekd), ALU.mult)
                tt(h3(qg[:, :]), q2, b8(eg), ALU.mult)
                tt(v2, v2, b8(beta), ALU.mult).then_inc(s["gderived"], 1)

            def decays(t):
                dve.wait_ge(s["grow_mm"], t + 1)
                gc = gsum[:, 0, t * H:(t + 1) * H].rearrange("p (a b) -> p b a", b=2)
                for par in range(2):
                    last = tt(decay[:, par, :, :], head(par), bc(gc[:, par, :], P, 2), ALU.subtract)
                link(last)
                tt(dec3, dec3, bc(negmask[:, :], 2 * HP, 1), ALU.add).then_inc(s["gexp_in"], 1)

            def off_diagonal(lv, par):
                return tt(offd[:, par, :, :], upper[:, par, :, :], bc(level[1 << lv][:, :], HP, 1), ALU.mult)

            def new_values(t, c):
                r = slice(c * CH, (c + 1) * CH)
                dve.wait_ge(s["gws_mm"], 2 * t + c + 1)
                tt(vn[r, :], usb[r, :], ps[r, 0, :], ALU.subtract).then_inc(s["gvn_ready"], 1)

            def new_state(t, c):
                dve.wait_ge(s["go_mm"], 2 * t + c + 1)
                for par in range(2):
                    pr = slice(par * DK, (par + 1) * DK)
                    last = tt(state[pr, :, par, :], state[pr, :, par, :], bc(egp[pr, c, t, :], DK, 2), ALU.mult)
                link(last)
                for par in range(2):
                    pr = slice(par * DK, (par + 1) * DK)
                    up = ps[pr, 1, :].rearrange("p (a b d) -> p a b d", a=HP, b=2)[:, :, par, :]
                    last = tt(state[pr, :, par, :], state[pr, :, par, :], up, ALU.add)
                last.then_inc(s["gstate_ready"], 1)

            def out_squares(t):
                dve.wait_ge(s["go_taken"], 2 * (t + 1))
                link(tt(sq[:, 0:H, :], h3(otok[:, :]), h3(otok[:, :]), ALU.mult))
                link(V.reduce_sum(oms[:, :], sq[:, 0:H, :], AX.X))
                ts(oms[:, :], oms[:, :], 1.0 / DK, EPS, ALU.mult, ALU.add).then_inc(s["onsq_ready"], 1)

            def out_norm(t):
                dve.wait_ge(s["onrs_ready"], t + 1)
                if t:
                    dve.wait_ge(s["oT_mm"], t)
                link(tt(h3(onrm[:, :]), h3(otok[:, :]), bc(orn[:, :], DK, 2), ALU.mult))
                link(tt(h3(onrm[:, :]), h3(onrm[:, :]), bc(ggdn[:, :], H, 1), ALU.mult))
                tt(onrm[:, :], onrm[:, :], zs[:, t, :], ALU.mult).then_inc(s["onorm_ready"], 1)

            norms(0)
            decays(0)
            derive(0)
            for t in range(TT):
                dve.wait_ge(s["gexp_ready"], t + 1)
                for par in range(2):
                    dve.wait_ge(s["gkk_mm"], 2 * t + par + 1)
                    link(tt(upper[:, par, :, :], head(6 + par), decay[:, par, :, :], ALU.mult))
                    off_diagonal(0, par).then_inc(offd_ready[par], 1)
                dve.wait_ge(s["gqk_mm"], t + 1)
                tt(attnT[:, t % 2, :, :, :], ps[:, 4:6, :].rearrange("p a (b c) -> p a b c", b=HP), decay[:, :, :, :], ALU.mult)\
                    .then_inc(s["gqk_taken"], 1)
                for lv in range(6):
                    for par in range(2):
                        dve.wait_ge(y_mm[par], 6 * t + lv + 1)
                        if lv == 0:
                            dve.wait_ge(offd_ready[par], 6 * t + 1)
                            tt(inv[:, par, :, :], id4, head(2 + par), ALU.subtract)
                            tt(invT[:, par, :, :], id4, offd[:, par, :, :], ALU.subtract).then_inc(lev_done[par], 1)
                            dve.wait_ge(lev_done[par], 6 * t + 1)
                        if lv < 5:
                            off_diagonal(lv + 1, par).then_inc(offd_ready[par], 1)
                    for par in range(2 if lv else 0):
                        dve.wait_ge(lev_mm[par], 5 * t + lv)
                        if lv < 5:
                            tt(inv[:, par, :, :], inv[:, par, :, :], head(4 + par), ALU.subtract)
                        tt(invT[:, par, :, :], invT[:, par, :, :], head(6 + par), ALU.subtract).then_inc(lev_done[par], 1)
                    if t and lv in (0, 2):
                        new_values(t - 1, lv // 2)
                    if lv == 1 and t + 1 < TT:
                        norms(t + 1)
                    if t and lv in (1, 3):
                        new_state(t - 1, lv // 2)
                    if t and lv == 3:
                        out_squares(t - 1)
                    if lv == 3 and t + 1 < TT:
                        derive(t + 1)
                    if lv == 4 and t + 1 < TT:
                        decays(t + 1)
                    if t and lv == 4:
                        out_norm(t - 1)
            for c in range(2):
                new_values(TT - 1, c)
                new_state(TT - 1, c)
            out_squares(TT - 1)
            out_norm(TT - 1)
            dve.drain().then_inc(s["gdn_over"], 1)
            dve.wait_ge(s["gdn_over"], 4)

            f32 = np.float32
            two_pi = 2 * np.pi
            c1 = float(f32(6.28125))
            c2 = float((f32(two_pi - c1).view(np.uint32) & np.uint32(0xFFFFF000)).view(f32))
            c3 = float(f32(two_pi - c1 - c2))
            magic = float(1.5 * 2 ** 23)
            pi = float(np.nextafter(f32(np.pi), f32(0)))
            half_dim = ROPE // 2
            freqs = np.power(f32(THETA), -np.arange(half_dim, dtype=f32) / f32(half_dim)).astype(f32)
            for j in range(half_dim):
                last = V.memset(invf[:, j:j + 1], float(freqs[j]))
            link(last)
            link(V.tensor_copy(posf[:, :], pos_i[:, :]))
            a0, a1, a2, a3, a4, a5 = (a[:, :, :] for a in ang)
            link(tt(a0, bc(posf[:, :], half_dim, 2), bc(invf[:, :], TT, 1), ALU.mult))
            link(ts(a1, a0, 1 / two_pi, magic, ALU.mult, ALU.add))
            link(ts(a1, a1, magic, None, ALU.subtract))
            for c in (c1, c2, c3):
                link(stt(a0, a1, -c, a0, ALU.mult, ALU.add))
            link(ts(a2, a0, pi, -pi, ALU.min, ALU.max))
            link(ts(a3, a0, np.pi / 2, None, ALU.add))
            link(ts(a4, a3, pi, -two_pi, ALU.is_gt, ALU.mult))
            link(tt(a5, a3, a4, ALU.add))
            ts(a5, a5, pi, -pi, ALU.min, ALU.max).then_inc(s["ang_ready"], 1)
            dve.wait_ge(s["msq_ready"], 1)
            link(ts(rss[:, 0, :], rss[:, 0, :], 1.0 / QL, EPS, ALU.mult, ALU.add))
            ts(rss[:, 1, :], rss[:, 1, :], 1.0 / KVL, EPS, ALU.mult, ALU.add).then_inc(s["mms_ready"], 1)
            dve.wait_ge(s["mrs_ready"], 1)
            for t in range(TT):
                cq, ckv = ptok[:, t, 16:16 + QL], ptok[:, t, 16 + QL:16 + QL + KVL]
                link(ts(cq, cq, rrs[:, 0, t:t + 1], None, ALU.mult))
                ts(ckv, ckv, rrs[:, 1, t:t + 1], None, ALU.mult).then_inc(s["mcn_ready"], 1)
            for t in range(TT):
                a = 2 * (t % 2)
                dve.wait_ge(s["mcT_mm"], t + 1)
                link(tt(cqT[:, :, t * P:(t + 1) * P], ps[:, a, 0:QL].rearrange("p (a b) -> p a b", a=3), bc(gcq[:, :], P, 2), ALU.mult))
                tt(ckvT[:, :, t * P:(t + 1) * P], ps[:, a + 1, 0:KVL].rearrange("p (a b) -> p a b", a=2), bc(gckv[:, :], P, 2), ALU.mult)\
                    .then_inc(s["mcT_taken"], 1)
            dve.wait_ge(s["trig_ready"], 2)
            for t in range(TT):
                dve.wait_ge(s["mproj_taken"], 4 * (t + 1))
                link(tt(qsq[:, :, :], qk[:, :, :], qk[:, :, :], ALU.mult))
                link(V.reduce_sum(qms[:, :], qsq[:, :, :], AX.X))
                ts(qms[:, :], qms[:, :], 1.0 / QK, EPS, ALU.mult, ALU.add).then_inc(s["mqms_ready"], 1)
                dve.wait_ge(s["mqrs_ready"], t + 1)
                link(tt(qk[:, :, :], qk[:, :, :], bc(qrn[:, :], QK, 2), ALU.mult))
                for g in range(2):
                    part = qk[:, g * H:(g + 1) * H, :]
                    link(tt(part, part, bc(gqk[:, g, :], H, 1), ALU.mult))
                x1, x2r = qk[:, :, NOPE:NOPE + half_dim], qk[:, :, NOPE + half_dim:]
                ct, st = bc(cos[:, t, :], 2 * H, 1), bc(sin[:, t, :], 2 * H, 1)
                link(tt(rt[0][:, :, :], x1, ct, ALU.mult))
                link(tt(rt[1][:, :, :], x2r, st, ALU.mult))
                link(tt(rt[2][:, :, :], x2r, ct, ALU.mult))
                link(tt(rt[3][:, :, :], x1, st, ALU.mult))
                link(tt(x1, rt[0][:, :, :], rt[1][:, :, :], ALU.subtract))
                tt(x2r, rt[2][:, :, :], rt[3][:, :, :], ALU.add).then_inc(s["mrope_ready"], 1)
            NU = TT * H
            for i in range(NU + 1):
                if i < NU:
                    t = i // H
                    n = (t + 1) * P
                    dve.wait_ge(s["score_mm"], i + 1)
                    link(V.memset(ps[0:CH, 4 + i % 2, n - CH:n], NEG))
                    link(V.reduce_max(mx[:, i:i + 1], ps[:, 4 + i % 2, 0:n], AX.X))
                    ts(nmx[:, i:i + 1], mx[:, i:i + 1], -QK ** -0.5, None, ALU.mult).then_inc(s["negmax_ready"], 1)
                if i:
                    j = i - 1
                    n = (j // H + 1) * P
                    dve.wait_ge(s["prob_ready"], j + 1)
                    link(V.reciprocal(rinv[:, j:j + 1], rsum[:, j:j + 1]))
                    ts(prob[:, j % 2, 0:n], prob[:, j % 2, 0:n], rinv[:, j:j + 1], None, ALU.mult).then_inc(s["probn_ready"], 1)
            dve.drain().then_inc(s["mla_over"], 1)
            dve.wait_ge(s["mla_over"], 4)
            for n in range(2):
                dve.wait_ge(s["ga_sig"], TT * (n + 1))
                dve.wait_ge(s["gb_sig"], TT * (n + 1))
                for t in range(TT):
                    dve.wait_ge(s["y_mm"], n * TT + t + 1)
                    link(tt(siga[:, t, :], siga[:, t, :], ps[:, 4, :], ALU.mult))
                    link(tt(sigb[:, t, :], sigb[:, t, :], ps[:, 5, :], ALU.mult))
                    tt(siga[:, t, :], siga[:, t, :], sigb[:, t, :], ALU.add).then_inc(s["merged_ready"], 1)
            dve.wait_ge(x_loaded[0], 32)
            for u in range(2 * TT):
                n, t = divmod(u, TT)
                dve.wait_ge(s["xo_mm"], u + 1)
                xs = x2[:, t, n * 512:(n + 1) * 512]
                tt(xs, xs, ps[:, u % 2, :], ALU.add).then_inc(s["x2_ready"], 1)
            dve.wait_ge(x2_stored, 16)
            for t in range(TT):
                dve.wait_ge(s["ss2_ready"], t + 1)
                ts(ss[:, t:t + 1], ss[:, t:t + 1], 1.0 / D, EPS, ALU.mult, ALU.add).then_inc(s["ms2_ready"], 1)
            for t in range(TT):
                dve.wait_ge(s["rs2_ready"], t + 1)
                ts(x2[:, t, :], x2[:, t, :], rs[:, t:t + 1], None, ALU.mult).then_inc(s["h2n_ready"], 1)
            for u in range(2 * TT):
                t, hf = divmod(u, 2)
                b = (slice(None), slice(4 * hf, 4 * hf + 4), slice(t * P, (t + 1) * P))
                dve.wait_ge(s["h2T_mm"], u + 1)
                tt(h2T[b], ps[:, u % 2, :].rearrange("p (a b) -> p a b", a=4), bc(g2[:, 4 * hf:4 * hf + 4], P, 2), ALU.mult)\
                    .then_inc(s["h2T_taken"], 1)
                dve.wait_ge(s["h2_hi"], u + 1)
                tt(h2lo[b], h2T[b], h2hi[b].bitcast(F32), ALU.subtract).then_inc(s["h2_lo"], 1)
            for m in range(SETS):
                dve.wait_ge(s["sc_taken"], m + 1)
                for t in range(TT):
                    last = V.max(tops[:, t, m, 0:8], sc[:, t, m, :])
                link(last)
                for t in range(TT):
                    V.max_index(topi[:, t, m, 0:8], tops[:, t, m, 0:8], sc[:, t, m, :])
                    last = V.match_replace(sc2[:, t, :], tops[:, t, m, 0:8], sc[:, t, m, :], -BIG)
                link(last)
                for t in range(TT):
                    last = V.max(tops[:, t, m, 8:16], sc2[:, t, :])
                link(last)
                for t in range(TT):
                    last = V.max_index(topi[:, t, m, 8:16], tops[:, t, m, 8:16], sc2[:, t, :])
                link(last)
            link(V.tensor_copy(topf[:, :, :, :].rearrange("p a b c -> p (a b c)"), topi[:, :, :, :].rearrange("p a b c -> p (a b c)")))
            dve.drain().then_inc(s["early_over"], 1)
            dve.wait_ge(s["early_over"], 4)
            side = lambda ap, t, p: ap[:, t, :, :].rearrange("p (h s) k -> p h s k", s=2)[:, :, p, :]
            b4 = lambda ap, at: bc(ap, PK, at)
            wide = lambda sl: ps[:, 2 * sl:2 * sl + 2, :].rearrange("p a b -> p (a b)")

            def u_lo(sl, n):
                dve.wait_ge(s["u_hi"], n)
                tt(opr_lo[:, sl, :], wide(sl), opr_hi[:, sl, :].bitcast(F32), ALU.subtract).then_inc(s["u_lo"], 1)

            def choose(t, part):
                if part == 0:
                    first, second = side(tops, t, 0), side(tops, t, 1)
                    link(tt(cand[:, :, 0:64].rearrange("p h (a b) -> p h a b", a=4), b4(first[:, :, 0:4], 3),
                            bc(second, 4, 2), ALU.add))
                    link(tt(cand[:, :, 64:].rearrange("p h (a b) -> p h a b", b=4), bc(first[:, :, 4:], 4, 3),
                            bc(second[:, :, 0:4], PK - 4, 2), ALU.add))
                    for h in range(H):
                        last = V.max(best[:, h, 0:8], cand[:, h, :])
                    link(last)
                    for h in range(H):
                        V.max_index(bpos[:, h, 0:8], best[:, h, 0:8], cand[:, h, :])
                        last = V.match_replace(cand2[:, h, :], best[:, h, 0:8], cand[:, h, :], -BIG)
                    link(last)
                elif part == 1:
                    for h in range(H):
                        last = V.max(best[:, h, 8:16], cand2[:, h, :])
                    link(last)
                    for h in range(H):
                        last = V.max_index(bpos[:, h, 8:16], best[:, h, 8:16], cand2[:, h, :])
                    link(last)
                elif part == 2:
                    link(V.tensor_copy(gsm[:, 0, :], best[:, :, 0]))
                    tt(best[:, :, :], best[:, :, :], bc(gsm[:, 0, :], PK, 2), ALU.subtract).then_inc(s["best_ready"], 1)
                    pos = bpos[:, :, :]
                    ts(apos[:, 0, :, :], pos, 4, None, ALU.logical_shift_right)
                    ts(apos[:, 1, :, :], pos, 15, None, ALU.bitwise_and)
                    ts(apos[:, 2, :, :], pos, 2, None, ALU.logical_shift_right)
                    ts(apos[:, 3, :, :], pos, 3, None, ALU.bitwise_and)
                    link(V.tensor_copy(low[:, :, :], pos))
                    V.tensor_copy(afl[:, :, :, :], apos[:, :, :, :])
                    link(ts(low[:, :, :], low[:, :, :], 64.0, None, ALU.is_lt))
                    link(ts(afl[:, 2, :, :], afl[:, 2, :, :], PK - 4.0, None, ALU.subtract))
                    link(tt(afl[:, 0:2, :, :], afl[:, 0:2, :, :], afl[:, 2:4, :, :], ALU.subtract))
                    link(tt(afl[:, 0:2, :, :], afl[:, 0:2, :, :], bc(low[:, :, :], 2, 1), ALU.mult))
                    link(tt(afl[:, 0:2, :, :], afl[:, 0:2, :, :], afl[:, 2:4, :, :], ALU.add))
                else:
                    p, place = ((0, 1), (1, 0))[part - 3]
                    if p == 0 and t:
                        dve.wait_ge(s["selT_mm"], t)
                    io4 = bc(bc(iota[:, 0:PK], PK, 1), H, 1)
                    link(tt(pick[:, :, :, :], io4, b4(afl[:, p, :, :], 3), ALU.is_equal))
                    link(tt(pick[:, :, :, :], pick[:, :, :, :], b4(side(topf, t, p), 2), ALU.mult))
                    link(V.reduce_sum(sel[:, place, :, :], pick[:, :, :, :], AX.X))
                    if p:
                        dve.wait_ge(s["gexp2_ready"], t + 1)
                        link(V.reduce_sum(gsm[:, 1, :], best[:, :, :], AX.X))
                        link(V.reciprocal(gsm[:, 1, :], gsm[:, 1, :]))
                        tt(sel[:, 2, :, :], best[:, :, :], bc(gsm[:, 1, :], PK, 2), ALU.mult).then_inc(s["sel_ready"], 1)

            def take_choice(t):
                dve.wait_ge(s["selT_mm"], t + 1)
                cols = slice(t * P, (t + 1) * P)
                V.tensor_copy(jT[:, cols], ps[:, 6, 0:P])
                V.tensor_copy(iT[:, cols], ps[:, 6, P:2 * P])
                gates = ps[:, 6, 2 * P:3 * P]
                link(ts(gate_hi[:, cols], gates, GSCALE, None, ALU.mult))
                stt(gate_lo[:, cols], gates, GSCALE, gate_hi[:, cols], ALU.mult, ALU.subtract).then_inc(s["selT_taken"], 1)

            def onehots(g, slot, first=False, used=True):
                tok = lambda ap: bc(ap[:, bass.ds(g * GT, GT)], NK, 1)
                if used:
                    dve.wait_ge(s["spread_mm"], g - 1)
                if not first:
                    dve.wait_ge(s["onehot_ready"], g)
                tt(rowhot[:, :, :], iota8[:, :, :], tok(iT), ALU.is_equal).then_inc(s["rowhot_ready"], 1)
                tt(colhot[:, slot, :, :], iota8[:, :, :], tok(jT), ALU.is_equal)
                dve.wait_ge(s["rowhot_ready"], g + 1)
                tt(rowhi[:, slot, :, :], rowhot[:, :, :], tok(gate_hi), ALU.mult)
                tt(rowlo[:, slot, :, :], rowhot[:, :, :], tok(gate_lo), ALU.mult).then_inc(s["onehot_ready"], 1)

            def u_onehots(i, sl, used=True, more=True):
                j = i - LEAD
                onehots(2 * j + 1, 1, used=used)
                u_lo(1 - sl, i + 2)
                if more:
                    onehots(2 * j + 2, 0)

            def weigh(n, sl, slot, k, piece):
                dve.wait_ge(gate_loaded[slot], piece)
                a = act[:, bass.ds(n - 1 - base, 1), :].rearrange("p a b -> p (a b)")
                a3 = a.rearrange("p (g t) -> p g t", t=ST)
                tt(a3, a3, gring[:, slot, :, k, :], ALU.mult).then_inc(s["w_prod"], 1)
                dve.wait_ge(s["v_hi"], n)
                tt(opr_lo[:, sl, :], raw[:, sl, :], opr_hi[:, sl, :].bitcast(F32), ALU.subtract).then_inc(s["v_lo"], 1)
                dve.wait_ge(s["w_hi_ready"], n)
                tt(w_lo[:, sl, :], a, w_hi[:, sl, :].bitcast(F32), ALU.subtract).then_inc(s["w_ready"], 1)

            V.tensor_copy(iota8[:, :, :], bc(iota[:, :], GT, 2))
            base = pieces = 0
            for g, size in enumerate(GROUPS):
                u_lo(0, base + 1)
                if g == 0:
                    for i in range(LEAD):
                        u_lo(1 - i % 2, i + 2)
                        t, part = divmod(i, PARTS)
                        choose(t, part)
                        if t and part == 2:
                            take_choice(t - 1)
                        if t == 1 and part == 3:
                            link(V.nop())
                            onehots(0, 0, first=True, used=False)
                    take_choice(TT - 1)
                    dve.wait_ge(s["selT_taken"], TT)
                    u_onehots(LEAD, 0, used=False)
                    u_onehots(LEAD + 1, 1)
                    with dve.Fori(LEAD // 2 + 1, (LEAD + SPREAD) // 2 - 1) as it:
                        for sl in range(2):
                            u_onehots(2 * it + sl, sl)
                    u_onehots(LEAD + SPREAD - 2, 0)
                    u_onehots(LEAD + SPREAD - 1, 1, more=False)
                    for i in range(LEAD + SPREAD, size - 1):
                        u_lo((i + 1) % 2, i + 2)
                else:
                    u_lo(1, base + 2)
                    with dve.Fori(0, size // 2 - 1) as it:
                        for sl in range(2):
                            u_lo(sl, 2 * it + (base + 3 + sl))
                dve.wait_ge(s["act_ready"], base + size)
                for k in range(2 * CB):
                    if k >= 2:
                        dve.wait_ge(s["v_mm"], base + k - 1)
                    weigh(base + k + 1, k % 2, k // CB, k % CB, 16 * (pieces + 1))
                with dve.Fori(1, size // (2 * CB)) as it:
                    for k in range(2 * CB):
                        b = it * (2 * CB) + (base + k)
                        dve.wait_ge(s["v_mm"], b - 1)
                        weigh(b + 1, k % 2, k // CB, k % CB, 16 * it + 16 * (pieces + 1))
                base += size
                pieces += size // (2 * CB)
            dve.wait_ge(y_loaded, 48)
            for k in range(KD):
                tt(y0T[:, k, :], y0T[:, k, :], y1T[:, k, :], ALU.add).then_inc(s["ypre_ready"], 1)
            dve.wait_ge(s["v_mm"], NK)
            for k in range(KD):
                dve.wait_ge(s["ypre_ready"], k + 1)
                tt(y0T[:, k, :], y0T[:, k, :], ps[:, k, :], ALU.add).then_inc(s["y_copied"], 1)
            for u in range(2 * TT):
                t, hf = divmod(u, 2)
                dve.wait_ge(s["yT_mm"], u + 1)
                xs = xb[:, t, hf * 512:(hf + 1) * 512]
                tt(xs, xs, ps[:, u % 2, :], ALU.add).then_inc(s["y_added"], 1)

        @block.gpsimd
        def _(pool):
            link = linker(pool, s["pool_step"])
            G = nc.gpsimd
            ge, sel_ = ALU.is_ge, G.affine_select
            link(G.memset(ones[:, :], 1.0))
            link(G.memset(half_neg[:, :], -0.5))
            link(sel_(out=ident[:, :], in_=ones[:, :], pattern=[[-1, P]], base=0, channel_multiplier=1, compare_op=ALU.is_equal, fill=0.0))
            for t in range(TT):
                pool.wait_ge(s["meansq_ready"], t + 1)
                G.tensor_tensor(rs[:, t:t + 1], ss[:, t:t + 1], half_neg[:, 0:1], ALU.pow).then_inc(s["rstd_ready"], 1)
                if not t:
                    pool.wait_ge(s["pool_step"], 3)
                    G.nop().then_inc(s["consts_ready"], 1)
            for b in (2, 4, 8, 16, 32, 64):
                m = same[b][:, :].rearrange("p (n i) -> p n i", i=b)
                link(sel_(out=m, in_=ones[:, :].rearrange("p (n i) -> p n i", i=b), pattern=[[-b, P // b], [0, b]], base=0,
                          channel_multiplier=1, compare_op=ge, fill=0.0))
                link(sel_(out=m, in_=m, pattern=[[b, P // b], [0, b]], base=b - 1, channel_multiplier=-1, compare_op=ge, fill=0.0))
            link(sel_(out=causal[:, :], in_=same[64][:, :], pattern=[[1, P]], base=0, channel_multiplier=-1, compare_op=ge, fill=0.0))
            link(sel_(out=strict[:, :], in_=same[64][:, :], pattern=[[1, P]], base=-1, channel_multiplier=-1, compare_op=ge, fill=0.0))
            link(G.tensor_scalar(negmask[:, :], causal[:, :], -NEG, NEG, ALU.mult, ALU.add))
            for b in (1, 2, 4, 8, 16, 32):
                inner = ident if b == 1 else same[b]
                link(G.tensor_tensor(level[b][:, :], same[2 * b][:, :], inner[:, :], ALU.subtract))
                link(G.tensor_tensor(level[b][:, :], level[b][:, :], strict[:, :], ALU.mult))
            link(sel_(out=chunk_ones[:, 0, :], in_=ones[:, :], pattern=[[0, P]], base=CH - 1, channel_multiplier=-1, compare_op=ge, fill=0.0))
            link(sel_(out=chunk_ones[:, 1, :], in_=ones[:, :], pattern=[[0, P]], base=-CH, channel_multiplier=1, compare_op=ge, fill=0.0))
            link(G.iota(iota_i[:, :], pattern=[[1, P]], base=0, channel_multiplier=0))
            link(G.tensor_copy(iota[:, :], iota_i[:, :]))
            G.nop().then_inc(s["consts_ready"], 1)
            pool.wait_ge(s["gates_ready"], 1)
            def decay_mask(t):
                gt = gdec[:, t, :].rearrange("p (a b) -> p b a", b=2)
                for par in range(2):
                    last = G.tensor_tensor(gm[:, par, :, :], bc(causal[:, :], HP, 1), bc(gt[:, par, :], P, 2), ALU.mult)
                last.then_inc(s["gmask_ready"], 1)

            def norm_power(t):
                pool.wait_ge(s["gms_ready"], t + 1)
                G.tensor_tensor(rn[:, :], ms[:, :], half_neg[:, :], ALU.pow).then_inc(s["grn_ready"], 1)

            def out_power(t):
                pool.wait_ge(s["onsq_ready"], t + 1)
                G.tensor_tensor(orn[:, :], oms[:, :], half_neg[:, 0:H], ALU.pow).then_inc(s["onrs_ready"], 1)

            decay_mask(0)
            norm_power(0)
            for t in range(TT):
                if t + 1 < TT:
                    pool.wait_ge(s["grow_mm"], t + 1)
                    decay_mask(t + 1)
                    norm_power(t + 1)
                if t:
                    out_power(t - 1)
            out_power(TT - 1)
            pool.drain().then_inc(s["gdn_over"], 1)
            pool.wait_ge(s["gdn_over"], 4)
            pool.wait_ge(s["mms_ready"], 1)
            fl = lambda ap: ap[:, :, :].rearrange("p a b -> p (a b)")
            G.tensor_tensor(fl(rrs), fl(rss), half_neg[:, 0:2 * TT], ALU.pow).then_inc(s["mrs_ready"], 1)
            for t in range(TT):
                pool.wait_ge(s["mqms_ready"], t + 1)
                G.tensor_tensor(qrn[:, :], qms[:, :], half_neg[:, :], ALU.pow).then_inc(s["mqrs_ready"], 1)
            pool.drain().then_inc(s["mla_over"], 1)
            for t in range(TT):
                pool.wait_ge(s["ms2_ready"], t + 1)
                G.tensor_tensor(rs[:, t:t + 1], ss[:, t:t + 1], half_neg[:, 0:1], ALU.pow).then_inc(s["rs2_ready"], 1)
            pool.drain().then_inc(s["early_over"], 1)


_INS = ["x", "positions", "norm1_g", "w_in", "conv_w", "a_log", "dt_bias", "gdn_norm_g", "w_gdn_out", "cq_norm_g",
        "w_uq", "ckv_norm_g", "w_ukv", "q_norm_g", "k_norm_g", "w_mla_out", "w_o", "norm2_g", "w_pq", "sub_keys",
        "u_tab", "v_tab"]


def kernel(**inputs):
    import concourse.bacc as _bacc
    from concourse.bass_utils import run_bass_kernel_spmd as _run

    nc = _bacc.Bacc("TRN2", target_bir_lowering=False, num_devices=1)
    arrays, args = {}, []
    for name in _INS:
        a = np.ascontiguousarray(inputs[name])
        arrays[f"in_{name}_dram"] = a
        args.append(nc.dram_tensor(f"in_{name}_dram", a.shape, mybir.dt.from_np(a.dtype), kind="ExternalInput").ap())
    args.append(nc.dram_tensor("out_0_dram", (1, S, D), F32, kind="ExternalOutput").ap())
    build(nc, *args)
    r = _run(nc, [arrays], core_ids=[0])
    return r.results[0]["out_0_dram"]
```

```python
from contextlib import ExitStack

import numpy as np
import concourse.bass as bass
from concourse import mybir

F32 = mybir.dt.float32
F32R = mybir.dt.float32r
F16 = mybir.dt.float16
I32 = mybir.dt.int32
U32 = mybir.dt.uint32
ALU = mybir.AluOpType
ACT = mybir.ActivationFunctionType
AX = mybir.AxisListType

P = 128
S = 512
D = 1024
TT = S // P
KD = D // P
CH = 64
EPS = 1e-6
H = 8
HP = H // 2
DK = 64
QKV = 3 * H * DK
CONV = 4
NOPE, ROPE = 64, 32
QK = NOPE + ROPE
QL, KVL = 384, 256
THETA = 10000.0
PK = 16
NK = 128
SETS = 2 * H
GROUPS = (56, 40, 32)
ARENA = max(GROUPS)
GT = 8
NG = S // GT
ST = 2 * GT
CB = 4
GSCALE = 4096.0
NCAND = 112
BIG = 3.0e38
NEG = -1.0e30
OFF_Z = QKV
OFF_BA = OFF_Z + 512
OFF_CKV = OFF_BA + 16 + QL
OFF_GATES = OFF_CKV + KVL + ROPE
SMALL = 9 + CONV
NW = 2
NS = 4
PARTS = 5
LATE = 4
LEAD = LATE + TT * PARTS
assert GROUPS[0] == LEAD + S // ST and sum(GROUPS) == NK and all(size % (2 * CB) == 0 for size in GROUPS)


def build(nc, x, positions, norm1_g, w_in, conv_w, a_log, dt_bias, gdn_norm_g, w_gdn_out,
          cq_norm_g, w_uq, ckv_norm_g, w_ukv, q_norm_g, k_norm_g, w_mla_out,
          w_o, norm2_g, w_pq, sub_keys, u_tab, v_tab, out):
    x_d = x.rearrange("a (t p) d -> p (a t) d", p=P)
    out_d = out.rearrange("a (t p) d -> p (a t) d", p=P)
    w_in_d = w_in.rearrange("l (k p) n -> p (l k) n", p=P)
    w_uq_d = w_uq.rearrange("l (k p) n -> p (l k) n", p=P)
    w_ukv_d = w_ukv.rearrange("l (k p) n -> p (l k) n", p=P)
    w_gdn_d = w_gdn_out.rearrange("l (k p) n -> p (l k) n", p=P)
    w_mla_d = w_mla_out.rearrange("l (k p) n -> p (l k) n", p=P)
    w_o_d = w_o.rearrange("l (k p) n -> p (l k) n", p=P)
    w_pq_d = w_pq.rearrange("l (k p) n -> p (l k) n", p=P)
    sk_d = sub_keys.rearrange("l h s n d -> n (l h s) d")
    u_d = u_tab.rearrange("l e d -> (l e) d")
    v_d = v_tab.rearrange("l e d -> (l e) d")
    sig_d = nc.dram_tensor("sigmoid_gates", [TT, P, 2, D], F32).ap()
    y_d = nc.dram_tensor("y_of_groups", [2, P, KD, S], F32).ap()
    g_d = nc.dram_tensor("gate_matrix", [S // ST, P, NK, ST], F32).ap()

    ctx = ExitStack()

    def sb(name, shape, dt=F32, stack=ctx):
        return stack.enter_context(nc.sbuf_tensor(name, shape, dt))

    def sem(name):
        return ctx.enter_context(nc.semaphore(name))

    with ctx:
        ident = sb("ident", [P, P])
        iota = sb("iota", [P, P])
        jT = sb("jT", [P, S], F16)
        iT = sb("iT", [P, S], F16)
        gate_hi = sb("gate_hi", [P, S], F16)
        gate_lo = sb("gate_lo", [P, S], F16)
        lent = ExitStack()
        tposed = sb("tposed", [P, 3, HP, P], stack=lent)
        attnT = sb("attnT", [P, 2, 2, HP, P], stack=lent)
        decay = sb("decay", [P, 2, HP, P], stack=lent)
        upper = sb("upper", [P, 2, HP, P], stack=lent)
        inv = sb("inv", [P, 2, HP, P], stack=lent)
        invT = sb("invT", [P, 2, HP, P], stack=lent)
        lent.close()
        lent = ExitStack()
        qk = sb("qk", [P, TT, 2 * H, QK], stack=lent)
        qsq = sb("qsq", [P, 2 * H, QK], stack=lent)
        lent.close()
        hhi = sb("hhi", [P, KD, S], F32R)
        hlo = sb("hlo", [P, KD, S], F32R)

        early = ExitStack()

        def eb(name, shape, dt=F32, stack=early):
            return sb(name, shape, dt, stack)

        wring = eb("wring", [P, NW, KD * 512])
        slices = ExitStack()
        cqT = eb("cqT", [P, 3, S], stack=slices)
        ckvT = eb("ckvT", [P, 2, S], stack=slices)
        slices.close()
        whi = eb("whi", [P, NS, 512], F32R)
        wlo = eb("wlo", [P, NS, 512], F32R)
        htmp = eb("htmp", [P, 2, 512])
        ones = eb("ones", [P, P])
        same = {b: eb(f"same{b}", [P, P]) for b in (2, 4, 8, 16, 32, 64)}
        level = {b: eb(f"level{b}", [P, P]) for b in (1, 2, 4, 8, 16, 32)}
        causal = eb("causal", [P, P])
        strict = eb("strict", [P, P])
        negmask = eb("negmask", [P, P])
        chunk_ones = eb("chunk_ones", [P, 2, P])
        iota_i = eb("iota_i", [P, P], I32)
        half_neg = eb("half_neg", [P, 2 * H])
        g1 = eb("g1", [P, KD])
        g2 = eb("g2", [P, KD])
        gcq = eb("gcq", [P, 3])
        gckv = eb("gckv", [P, 2])
        cw = eb("cw", [P, QKV // P, CONV])
        alog = eb("alog", [P, H])
        dtb = eb("dtb", [P, H])
        ggdn = eb("ggdn", [P, DK])
        gqk = eb("gqk", [P, 2, QK])
        pos_i = eb("pos_i", [P, TT], I32)
        oaT = eb("oaT", [P, HP, S])
        obT = eb("obT", [P, HP, S])
        sig_out = obT
        ss = eb("ss", [P, TT])
        rs = eb("rs", [P, TT])
        ptok = eb("ptok", [P, TT, 16 + QL + KVL + ROPE])
        cos = eb("cos", [P, TT, ROPE // 2])
        sin = eb("sin", [P, TT, ROPE // 2])
        rss = eb("rss", [P, 2, TT])
        rrs = eb("rrs", [P, 2, TT])
        ang = [eb(f"ang{i}", [P, TT, ROPE // 2]) for i in range(6)]
        invf = eb("invf", [P, ROPE // 2])
        posf = eb("posf", [P, TT])

        gdn = ExitStack()
        qkv = eb("qkv", [P, TT, QKV], stack=gdn)
        zs = eb("zs", [P, TT, 512], stack=gdn)
        beta = eb("beta", [P, TT, H], stack=gdn)
        gdec = eb("gdec", [P, TT, H], stack=gdn)
        gtmp = [eb(f"gtmp{i}", [P, TT, H], stack=gdn) for i in range(6)]
        ealog = eb("ealog", [P, H], stack=gdn)
        gsum = eb("gsum", [P, 4, TT * H], stack=gdn)
        eg = eb("eg", [P, TT, H], stack=gdn)
        ekd = eb("ekd", [P, TT, H], stack=gdn)
        egl = eb("egl", [P, 2, TT, H], stack=gdn)
        egp = eb("egp", [P, 2, TT, HP], stack=gdn)
        state = eb("state", [P, HP, 2, DK], stack=gdn)
        s1 = ExitStack()
        xt = eb("xt", [P, TT, D], stack=s1)
        xjunk = eb("xjunk", [P, D], stack=s1)
        cin = eb("cin", [P, 4, S + 3], stack=s1)
        cacc = eb("cacc", [P, 2, S], stack=s1)
        csil = eb("csil", [P, 2, S], stack=s1)
        s1.close()
        s2 = ExitStack()
        sq = eb("sq", [P, 2 * H, DK], stack=s2)
        ms = eb("ms", [P, 2 * H], stack=s2)
        rn = eb("rn", [P, 2 * H], stack=s2)
        kb = eb("kb", [P, 512], stack=s2)
        oms = eb("oms", [P, H], stack=s2)
        orn = eb("orn", [P, H], stack=s2)
        kbg = eb("kbg", [P, 2, 512], stack=s2)
        kd = eb("kd", [P, 2, 512], stack=s2)
        qgT = eb("qgT", [P, 2, HP, P], stack=s2)
        offd = eb("offd", [P, 2, HP, P], stack=s2)
        qg = eb("qg", [P, 512], stack=s2)
        gm = eb("gm", [P, 2, HP, P], stack=s2)
        ysb = eb("ysb", [P, 2, HP, P], stack=s2)
        usb = eb("usb", [P, 512], stack=s2)
        wT = eb("wT", [P, HP, P], stack=s2)
        vn = eb("vn", [P, 512], stack=s2)
        otok = eb("otok", [P, 512], stack=s2)
        onrm = eb("onrm", [P, 512], stack=s2)
        s2.close()
        gdn.close()

        mla = ExitStack()
        qms = eb("qms", [P, 2, 2 * H], stack=mla)
        qrn = eb("qrn", [P, 2, 2 * H], stack=mla)

        rt = [eb(f"rt{i}", [P, 2 * H, ROPE // 2], stack=mla) for i in range(4)]
        qkT = eb("qkT", [QK, 2 * H, S], stack=mla)
        vtok = eb("vtok", [P, TT, H, DK], stack=mla)
        prob = eb("prob", [P, 4, S], stack=mla)
        pT = eb("pT", [P, 2, TT, P], stack=mla)
        mx = eb("mx", [P, 2 * TT * H], stack=mla)
        nmx = eb("nmx", [P, TT * H], stack=mla)
        rsum = eb("rsum", [P, TT * H], stack=mla)
        rinv = eb("rinv", [P, TT * H], stack=mla)
        mla.close()

        mrg = ExitStack()
        sig = eb("sig", [P, 2, TT, 512], stack=mrg)
        merged_hi = eb("merged_hi", [P, KD, S], F32R, stack=mrg)
        merged_lo = eb("merged_lo", [P, KD, S], F32R, stack=mrg)
        x2 = eb("x2", [P, TT, D], stack=mrg)
        junk2 = eb("junk2", [P, D], stack=mrg)
        x2n = sig[:, :, :, :].rearrange("p g t n -> p (g t n)").rearrange("p (t n) -> p t n", t=TT)
        mrg.close()
        pk = ExitStack()
        sc = eb("sc", [P, TT, SETS, NK], stack=pk)
        keys = ExitStack()
        skT = eb("skT", [P, SETS, NK], stack=keys)
        qTm = eb("qTm", [P, 4, S], stack=keys)
        keys.close()
        cand = eb("cand", [P, H, NCAND], stack=pk)
        cand2 = eb("cand2", [P, H, NCAND], stack=pk)
        pick = eb("pick", [P, H, PK, PK], stack=pk)
        eb("keys_rest", [P, 2 * SETS * NK - 2 * H * NCAND - H * PK * PK], stack=pk)
        sc2 = eb("sc2", [P, TT, NK], stack=pk)
        tops = eb("tops", [P, TT, SETS, PK], stack=pk)
        topi = eb("topi", [P, TT, SETS, PK], U32, stack=pk)
        topf = eb("topf", [P, TT, SETS, PK], stack=pk)
        best = eb("best", [P, H, PK], stack=pk)
        bpos = eb("bpos", [P, H, PK], U32, stack=pk)
        apos = eb("apos", [P, 4, H, PK], U32, stack=pk)
        afl = eb("afl", [P, 4, H, PK], stack=pk)
        low = eb("low", [P, H, PK], stack=pk)
        sel = eb("sel", [P, 3, H, PK], stack=pk)
        gsm = eb("gsm", [P, 2, H], stack=pk)
        pk.close()
        early.close()

        spread = ExitStack()
        iota8 = sb("iota8", [P, NK, GT], F16, spread)
        colhot = sb("colhot", [P, 2, NK, GT], F16, spread)
        rowhot = sb("rowhot", [P, NK, GT], F16, spread)
        rowhi = sb("rowhi", [P, 2, NK, GT], F16, spread)
        rowlo = sb("rowlo", [P, 2, NK, GT], F16, spread)
        stage = sb("stage", [P, 2, NK, ST], F32, spread)
        spread.close()
        vph = ExitStack()
        w_hi = sb("w_hi", [P, 2, S], F32R, vph)
        w_lo = sb("w_lo", [P, 2, S], F32R, vph)
        gring = sb("gring", [P, 2, S // ST, CB, ST], F32, vph)
        vph.close()
        room = sb("room", [P, 8 * 1024])
        raw = sb("raw", [P, 2, D])
        opr_hi = sb("opr_hi", [P, 2, D], F32R)
        opr_lo = sb("opr_lo", [P, 2, D], F32R)
        act = sb("act", [P, ARENA, S])

        ps = ctx.enter_context(nc.psum_tensor("ps", [P, 8, 512], F32))

        ystage = gring[:, :, :, :, :].rearrange("p s a b c -> p (s a b c)").rearrange("p (k n) -> p k n", k=KD)
        y0T = act[:, GROUPS[2]:GROUPS[2] + KD, :]
        y1T = act[:, GROUPS[2] + KD:GROUPS[2] + 2 * KD, :]
        xb = act[:, GROUPS[2] + 2 * KD:GROUPS[2] + 3 * KD, :].rearrange("p (t a) n -> p t (a n)", t=TT)

        names = """consts_ready g1_loaded small_loaded
            sumsq_ready meansq_ready rstd_ready xn_ready xT_mm hT_ready h_hi h_lo
            slice_hi slice_ready slice_used dense_mm dense_taken
            conv_out silu_ready qkvT_mm qkv_tok dve_step act_step pool_step
            gates_in gates_exp gates_ready gsum_mm gsum_exp
            gms_ready grn_ready gderived gT_mm gT_taken gmask_ready grow_mm gexp_in gexp_ready
            gkk_mm gqk_mm gqk_taken guw_mm guw_taken
            gws_mm gvn_ready go_mm go_taken gup_mm gstate_ready onsq_ready onrs_ready onorm_ready oT_mm oT_taken gdn_over
            msq_ready mms_ready mrs_ready mcn_ready mcT_mm mcT_taken ang_ready trig_ready
            mproj_mm mproj_taken mqsq_ready mqms_ready mqrs_ready mrope_ready mqT_mm mqT_taken
            score_mm negmax_ready prob_ready probn_ready pT_mm pT_taken av_mm av_taken mla_over
            y_mm merged_ready mT_mm m_hi mT_taken ss2_ready ms2_ready rs2_ready
            h2n_ready h2T_mm h2T_taken sk_mm sk_taken sc_mm sc_taken
            best_ready gexp2_ready sel_ready selT_mm selT_taken early_over
            u_tmm u_hi u_lo u_mm act_ready onehot_ready rowhot_ready spread_mm gate_taken
            v_hi v_lo w_prod w_hi_ready w_ready v_mm y_bank y_copied ypre_ready yT_mm y_added""".split()
        s = {n: sem(n) for n in names}
        offd_ready, y_mm, y_taken, lev_mm, lev_done = ([sem(f"g{n}{par}") for par in range(2)] for n in
                                                       ("offd_ready", "y_mm", "y_taken", "lev_mm", "lev_done"))
        w_loaded = [sem(f"w_loaded{i}") for i in range(NW)]
        sig_stored = [sem(f"sig_stored{t}") for t in range(TT)]
        sig_loaded = [sem(f"sig_loaded{t}") for t in range(TT)]
        x_loaded = [sem(f"x_loaded{t}") for t in range(TT)]
        raw_loaded = [sem(f"raw_loaded{i}") for i in range(2)]
        gate_stored = [sem(f"gate_stored{i}") for i in range(2)]
        gate_loaded = [sem(f"gate_loaded{i}") for i in range(2)]
        y_stored = sem("y_stored")
        x2_stored = sem("x2_stored")
        y_loaded = sem("y_loaded")
        out_stored = sem("out_stored")

        panels, dense = [], []

        def dense_panel(src, w):
            dense.append((len(panels), w))
            panels.append(("slice_ready", KD * len(dense), [(src, 0, KD, w)]))

        for n in range(3):
            dense_panel(w_in_d[:, :, n * 512:(n + 1) * 512], 512)
        DENSE_TOK = len(dense)
        for at, w in ((OFF_Z, 512), (OFF_BA, 16 + QL), (OFF_CKV, KVL + ROPE)):
            dense_panel(w_in_d[:, :, at:at + w], w)
        DENSE_GATES = len(dense)
        for n in range(4):
            dense_panel(w_in_d[:, :, OFF_GATES + n * 512:OFF_GATES + (n + 1) * 512], 512)
        DENSE_O = len(dense)
        PAN_UQ = len(panels)
        panels.append(("mproj_mm", TT, [(w_uq_d, 0, 3, H * QK)]))
        PAN_UKV = len(panels)
        panels.append(("mproj_mm", TT, [(w_ukv_d, 0, 2, H * 2 * DK)]))
        PAN_Y = len(panels)
        for n in range(2):
            panels.append(("y_mm", TT * (n + 1), [(w_gdn_d[:, :, n * 512:(n + 1) * 512], 0, HP, 512),
                                                  (w_mla_d[:, :, n * 512:(n + 1) * 512], HP * 512, HP, 512)]))
        PAN_O = len(panels)
        for n in range(2):
            dense_panel(w_o_d[:, :, n * 512:(n + 1) * 512], 512)
        PAN_SK = len(panels)
        panels.append(("sk_mm", SETS // 4, [(sk_d, 0, SETS, NK)]))
        DENSE_PQ = len(dense)
        PAN_PQ = len(panels)
        for n in range(4):
            dense_panel(w_pq_d[:, :, n * 512:(n + 1) * 512], 512)

        def wait_used(eng, i):
            d, k = divmod(i, KD)
            if k == KD - 1:
                eng.wait_ge(s["dense_mm"], 4 * (d + 1))
            else:
                eng.wait_ge(s["slice_used"], (KD - 1) * d + k + 1)

        NB = QKV // P
        after = lambda m, lag: KD * (m // 4 + 1) + m % 4 + lag

        GATE_STEPS = [KD * (DENSE_TOK + 2) + j for j in (4, 5, 7, 9, 11, 18, 19, 21, 22)]

        LATENT_BANKS = (2, 6)
        LATENT_OUT = (4, 0)
        LATENT_STEP = KD * (DENSE_GATES + 1) + 3

        def wait_y_bank(eng, g, k):
            if k < KD - 1:
                eng.wait_ge(s["y_bank"], (KD - 1) * g + k + 1)
            else:
                eng.wait_ge(s["v_mm"], sum(GROUPS[:g + 1]))

        def panel(n, k, w, at=0):
            return wring[:, n % NW, at:at + k * w].rearrange("p (k w) -> p k w", k=k)

        def loads_by(n):
            return sum(16 * len(panels[m][2]) for m in range(n % NW, n + 1, NW))

        def linker(eng, step):
            count = [0]

            def link(ins):
                count[0] += 1
                ins.then_inc(step, 1)
                eng.wait_ge(step, count[0])
            return link

        block = ctx.enter_context(nc.Block())
        bc = lambda ap, n, at: ap.unsqueeze(at).to_broadcast(list(ap.shape[:at]) + [n] + list(ap.shape[at:]))

        @block.sync
        def _(sp):
            for t in range(TT):
                sp.dma_start(xt[:, t, :], x_d[:, t, :]).then_inc(x_loaded[t], 16)
            col = lambda v: v.rearrange("l (k p) -> p (l k)", p=P)
            row = lambda v, n: v.to_broadcast([P, n])
            small = [(gcq[:, :], col(cq_norm_g)), (gckv[:, :], col(ckv_norm_g)), (g2[:, :], col(norm2_g)),
                     (alog[:, :], row(a_log, H)), (dtb[:, :], row(dt_bias, H)), (ggdn[:, :], row(gdn_norm_g, DK)),
                     (gqk[:, 0, :], row(q_norm_g, QK)), (gqk[:, 1, :], row(k_norm_g, QK)),
                     (pos_i[:, :], positions.rearrange("b (t p) -> p (b t)", p=P))]
            small += [(cw[:, :, j], conv_w[:, j, :].rearrange("l (m p) -> p (l m)", p=P)) for j in range(CONV)]
            assert len(small) == SMALL
            with nc.allow_non_contiguous_dma(reason="small vectors onto partitions"):
                sp.dma_start(g1[:, :], col(norm1_g)).then_inc(s["g1_loaded"], 16)
            for n, (_, _, parts) in enumerate(panels):
                if n == 1:
                    with nc.allow_non_contiguous_dma(reason="small vectors onto partitions"):
                        for dst, src in small:
                            sp.dma_start(dst, src).then_inc(s["small_loaded"], 16)
                if n == PAN_PQ + 1:
                    sp.wait_ge(s["dense_taken"], 4 * DENSE_PQ)
                    sp.dma_start(out_d, x2[:, :, :]).then_inc(x2_stored, 16)
                if n == PAN_O:
                    sp.wait_ge(s["mla_over"], 4)
                    for hf in range(2):
                        for t in range(TT):
                            if hf:
                                sp.wait_ge(s["mT_mm"], t + 1)
                            else:
                                sp.wait_ge(sig_stored[t], 16 * 4)
                            sp.dma_start(sig[:, :, t, :], sig_d[t][:, :, hf * 512:(hf + 1) * 512]).then_inc(sig_loaded[t], 16)
                        if not hf:
                            sp.dma_start(x2[:, :, :], x_d).then_inc(x_loaded[0], 16)
                if n >= NW:
                    sp.wait_ge(s[panels[n - NW][0]], panels[n - NW][1])
                for src, at, k, w in parts:
                    sp.dma_start(panel(n, k, w, at), src).then_inc(w_loaded[n % NW], 16)
            sp.wait_ge(x2_stored, 16)
            sp.wait_ge(s["early_over"], 4)

            def gate_piece(slot, b):
                sp.dma_start(gring[:, slot, :, :, :].rearrange("p g i t -> p g (i t)"),
                             g_d[:, :, bass.ds(b, CB), :].rearrange("g p i t -> p g (i t)"))\
                  .then_inc(gate_loaded[slot], 16)

            base = 0
            for g, size in enumerate(GROUPS):
                for sl in range(2):
                    if g:
                        sp.wait_ge(s["v_lo"], base - 1 + sl)
                    sp.dma_start(raw[:, sl, :], u_d[(base + sl) * P:(base + sl + 1) * P, :]).then_inc(raw_loaded[sl], 16)

                def keys_of(b, sl):
                    sp.wait_ge(s["u_tmm"], b - 1)
                    sp.dma_start(raw[:, sl, :], u_d[bass.ds(b * P, P), :]).then_inc(raw_loaded[sl], 16)

                side_loads = 4 if g == 2 else g
                for i in range(1, side_loads + 1):
                    for sl in range(2):
                        keys_of(base + 2 * i + sl, sl)
                    if i == 1:
                        for k in range(KD):
                            sp.wait_ge(s["y_copied"], (g - 1) * KD + k + 1)
                        sp.dma_start(y_d[g - 1], ystage).then_inc(y_stored, 16)
                    else:
                        sp.wait_ge(y_stored, 32)
                        dst, src = ((y0T, y_d[0]), (y1T, y_d[1]), (xb, out_d))[i - 2]
                        sp.dma_start(dst, src).then_inc(y_loaded, 16)
                with sp.Fori(1 + side_loads, size // 2) as it:
                    for sl in range(2):
                        keys_of(2 * it + (base + sl), sl)
                for sl in range(2):
                    sp.wait_ge(s["u_tmm"], base + size - 1 + sl)
                    sp.dma_start(raw[:, sl, :], v_d[(base + sl) * P:(base + sl + 1) * P, :]).then_inc(raw_loaded[sl], 16)
                if g:
                    sp.wait_ge(y_stored, 16 * g)
                else:
                    for slot in range(2):
                        sp.wait_ge(gate_stored[slot], 16 * (S // ST // 2))
                    sp.wait_ge(s["spread_mm"], NG)
                gate_piece(0, base)
                gate_piece(1, base + CB)

                def values(b, sl):
                    sp.wait_ge(s["v_lo"], b - 1)
                    sp.dma_start(raw[:, sl, :], v_d[bass.ds(b * P, P), :]).then_inc(raw_loaded[sl], 16)

                for k in range(2, 2 * CB):
                    values(base + k, k % 2)
                with sp.Fori(1, size // (2 * CB)) as it:
                    b = it * (2 * CB)
                    for k in range(2 * CB):
                        values(b + (base + k), k % 2)
                        if k % CB == 0:
                            sp.wait_ge(s["w_prod"], b + (base + k - CB))
                            gate_piece(k // CB, b + (base + k))
                base += size
            for u in range(2 * TT):
                hf, t = divmod(u, TT)
                cols = slice(hf * 512, (hf + 1) * 512)
                sp.wait_ge(s["y_added"], u + 1)
                sp.dma_start(out_d[:, t, cols], xb[:, t, cols]).then_inc(out_stored, 16)
            sp.wait_ge(out_stored, 16 * 2 * TT)

        @block.tensor
        def _(pe):
            def take_panel(n, *shape):
                pe.wait_ge(w_loaded[n % NW], loads_by(n))
                return panel(n, *shape)

            pe.wait_ge(s["consts_ready"], 1)
            for u in range(2 * TT):
                t, hf = divmod(u, 2)
                if not hf:
                    pe.wait_ge(s["xn_ready"], t + 1)
                if u >= 2:
                    pe.wait_ge(s["hT_ready"], u - 1)
                for b in range(4):
                    last = pe.transpose(ps[:, 6 + u % 2, b * P:(b + 1) * P], xt[:, t, (4 * hf + b) * P:(4 * hf + b + 1) * P], ident[:, :])
                last.then_inc(s["xT_mm"], 1)
            pe.wait_ge(s["h_lo"], 2 * TT)

            def dense_slice(i, hi, lo, by_feature):
                d, k = divmod(i, KD)
                w = dense[d][1]
                pe.wait_ge(s["slice_ready"], i + 1)
                for b in range(4):
                    if k == 0 and d:
                        pe.wait_ge(s["dense_taken"], 4 * (d - 1) + b + 1)
                    cols = slice(b * P, (b + 1) * P)
                    for j, (a, c) in enumerate(((hi, whi), (hi, wlo), (lo, whi))):
                        st, mv = (c[:, i % NS, cols], a[:, k, :]) if by_feature else (a[:, k, cols], c[:, i % NS, 0:w])
                        last = pe.matmul(ps[:, b, 0:S if by_feature else w], st, mv, start=k == 0 and j == 0,
                                         stop=k == KD - 1 and j == 2)
                    if k == KD - 1:
                        last.then_inc(s["dense_mm"], 1)
                if k < KD - 1:
                    last.then_inc(s["slice_used"], 1)

            gflat = gdec[:, :, :].rearrange("p t h -> p (t h)")
            for i in range(KD * DENSE_O):
                dense_slice(i, hhi, hlo, i < KD * DENSE_TOK)
                for m in range(NB):
                    if i == after(m, 3):
                        pe.wait_ge(s["silu_ready"], m + 1)
                        if m >= 2:
                            pe.wait_ge(s["qkv_tok"], m - 1)
                        for t in range(TT):
                            last = pe.transpose(ps[:, 4 + m % 2, t * P:(t + 1) * P], csil[:, m % 2, t * P:(t + 1) * P], ident[:, :])
                        last.then_inc(s["qkvT_mm"], 1)
                if i == KD * DENSE_GATES + 8:
                    pe.wait_ge(s["consts_ready"], 2)
                    pe.wait_ge(s["gates_ready"], 1)
                    for j, m in enumerate((causal[:, :], same[64][:, :], chunk_ones[:, 0, :], chunk_ones[:, 1, :])):
                        last = pe.matmul(ps[:, 6, j * 32:(j + 1) * 32], m, gflat, start=True, stop=True)
                    last.then_inc(s["gsum_mm"], 1)
            pe.wait_ge(s["dense_taken"], 4 * DENSE_O)

            def decay_rows(t):
                pe.wait_ge(s["gmask_ready"], t + 1)
                for par in range(2):
                    last = pe.matmul(ps[:, par, :], ones[:, :], gm[:, par, :, :].rearrange("p a b -> p (a b)"),
                                     start=True, stop=True)
                last.then_inc(s["grow_mm"], 1)

            def scan_carry(t, c):
                n = 2 * t + c
                r = slice(c * CH, (c + 1) * CH)
                pe.wait_ge(s["guw_taken"], 2 * (t + 1))
                pe.wait_ge(s["gstate_ready"], n + 1)
                if n:
                    pe.wait_ge(s["go_taken"], n)
                for hp in range(HP):
                    last = pe.matmul(ps[r, 0, hp * P:(hp + 1) * P], wT[:, hp, r],
                                     state[:, hp, :, :].rearrange("p a d -> p (a d)"), start=True, stop=True)
                last.then_inc(s["gws_mm"], 1)

            def scan_update(t, c):
                n = 2 * t + c
                r = slice(c * CH, (c + 1) * CH)
                pe.wait_ge(s["gvn_ready"], n + 1)
                for hp in range(HP):
                    last = pe.matmul(ps[:, 1, hp * P:(hp + 1) * P], kd[r, t % 2, hp * P:(hp + 1) * P], vn[r, hp * P:(hp + 1) * P],
                                     start=True, stop=True)
                last.then_inc(s["gup_mm"], 1)
                for hp in range(HP):
                    pe.matmul(ps[r, 0, hp * P:(hp + 1) * P], qgT[:, t % 2, hp, r],
                              state[:, hp, :, :].rearrange("p a d -> p (a d)"), start=True, stop=False)
                    for par in range(2):
                        h = 2 * hp + par
                        last = pe.matmul(ps[r, 0, h * DK:(h + 1) * DK], attnT[:, t % 2, par, hp, r], vn[:, h * DK:(h + 1) * DK],
                                         start=False, stop=par == 1)
                last.then_inc(s["go_mm"], 1)

            def out_transposes(t, bank=4):
                pe.wait_ge(s["onorm_ready"], t + 1)
                for hp in range(HP):
                    last = pe.transpose(ps[:, bank, hp * P:(hp + 1) * P], onrm[:, hp * P:(hp + 1) * P], ident[:, :])
                last.then_inc(s["oT_mm"], 1)

            decay_rows(0)
            for t in range(TT):
                pe.wait_ge(s["gderived"], t + 1)
                pe.wait_ge(s["gexp_in"], t + 1)
                srcs = (qkv[:, t, 512:1024], kb[:, :], qkv[:, t, 0:512], qg[:, :])
                for i, src in enumerate(srcs):
                    for hp in range(HP):
                        last = pe.transpose(ps[:, i, hp * P:(hp + 1) * P], src[:, hp * P:(hp + 1) * P], ident[:, :])
                    last.then_inc(s["gT_mm"], 1)
                for par in range(2):
                    r = slice(par * DK, (par + 1) * DK)
                    pe.wait_ge(s["gT_taken"], 4 * t + 2)
                    for hp in range(HP):
                        last = pe.matmul(ps[:, 6 + par, hp * P:(hp + 1) * P], tposed[r, 0, hp, :], tposed[r, 1, hp, :],
                                         start=True, stop=True)
                    last.then_inc(s["gkk_mm"], 1)
                pe.wait_ge(s["gT_taken"], 4 * t + 4)
                if t >= 2:
                    pe.wait_ge(s["oT_taken"], t - 1)
                for par in range(2):
                    r = slice(par * DK, (par + 1) * DK)
                    for hp in range(HP):
                        last = pe.matmul(ps[:, 4 + par, hp * P:(hp + 1) * P], tposed[r, 0, hp, :], tposed[r, 2, hp, :],
                                         start=True, stop=True)
                last.then_inc(s["gqk_mm"], 1)
                for lv in range(6):
                    for par in range(2):
                        pe.wait_ge(offd_ready[par], 6 * t + lv + 1)
                        if lv:
                            pe.wait_ge(lev_done[par], 6 * t + lv)
                        for hp in range(HP):
                            last = pe.matmul(ps[:, 2 + par, hp * P:(hp + 1) * P], offd[:, par, hp, :],
                                             inv[:, par, hp, :] if lv else ident[:, :], start=True, stop=True)
                        last.then_inc(y_mm[par], 1)
                    if lv == 1:
                        pe.wait_ge(s["gqk_taken"], t + 1)
                    for par in range(2 if lv else 0):
                        pe.wait_ge(y_taken[par], 5 * t + lv)
                        for hp in range(HP if lv < 5 else 0):
                            pe.matmul(ps[:, 4 + par, hp * P:(hp + 1) * P], invT[:, par, hp, :], ysb[:, par, hp, :],
                                      start=True, stop=True)
                        for hp in range(HP):
                            last = pe.matmul(ps[:, 6 + par, hp * P:(hp + 1) * P], ysb[:, par, hp, :], invT[:, par, hp, :],
                                             start=True, stop=True)
                        last.then_inc(lev_mm[par], 1)
                    if t and lv in (0, 2):
                        scan_carry(t - 1, lv // 2)
                    if t and lv in (1, 3):
                        scan_update(t - 1, lv // 2)
                    if lv == 4 and t + 1 < TT:
                        if t:
                            pe.wait_ge(s["go_taken"], 2 * t)
                            pe.wait_ge(s["gstate_ready"], 2 * t + 1)
                        decay_rows(t + 1)
                for par in range(2):
                    pe.wait_ge(lev_done[par], 6 * (t + 1))
                for hp in range(HP):
                    for par in range(2):
                        h = 2 * hp + par
                        pe.matmul(ps[:, 2, h * DK:(h + 1) * DK], invT[:, par, hp, :], qkv[:, t, 1024 + h * DK:1024 + (h + 1) * DK],
                                  start=True, stop=True)
                        last = pe.matmul(ps[par * DK:(par + 1) * DK, 3, hp * P:(hp + 1) * P], kbg[:, t % 2, h * DK:(h + 1) * DK],
                                         invT[:, par, hp, :], start=True, stop=True)
                last.then_inc(s["guw_mm"], 1)
                if t:
                    out_transposes(t - 1)
                pe.wait_ge(s["guw_taken"], 2 * (t + 1))

            def latent_transposes(t):
                pe.wait_ge(s["mcn_ready"], t + 1)
                if t >= 2:
                    pe.wait_ge(s["mcT_taken"], t - 1)
                a = LATENT_BANKS[t % 2]
                for b in range(3):
                    pe.transpose(ps[:, a, b * P:(b + 1) * P], ptok[:, t, 16 + b * P:16 + (b + 1) * P], ident[:, :])
                for b in range(2):
                    last = pe.transpose(ps[:, a + 1, b * P:(b + 1) * P],
                                        ptok[:, t, 16 + QL + b * P:16 + QL + (b + 1) * P], ident[:, :])
                last.then_inc(s["mcT_mm"], 1)

            def latent_products(t):
                if t >= 2:
                    pe.wait_ge(s["mproj_taken"], 4 * (t - 1))
                b = LATENT_OUT[t % 2]
                for bank, w, src, n0, n1 in ((b, wq, cqT, 0, 512), (b + 1, wq, cqT, 512, 768),
                                             (b + 2, wkv, ckvT, 0, 512), (b + 3, wkv, ckvT, 512, 1024)):
                    nk = src.shape[1]
                    for k in range(nk):
                        last = pe.matmul(ps[:, bank, 0:n1 - n0], src[:, k, t * P:(t + 1) * P], w[:, k, n0:n1],
                                         start=k == 0, stop=k == nk - 1)
                last.then_inc(s["mproj_mm"], 1)

            scan_carry(TT - 1, 0)
            latent_transposes(0)
            latent_transposes(1)
            scan_update(TT - 1, 0)
            latent_transposes(2)
            latent_transposes(3)
            scan_carry(TT - 1, 1)
            wq = take_panel(PAN_UQ, 3, H * QK)
            wkv = take_panel(PAN_UKV, 2, H * 2 * DK)
            pe.wait_ge(s["mcT_taken"], TT)
            pe.wait_ge(s["oT_taken"], TT - 1)
            scan_update(TT - 1, 1)
            latent_products(0)
            out_transposes(TT - 1, 2)

            pe.drain().then_inc(s["gdn_over"], 1)
            pe.wait_ge(s["gdn_over"], 4)
            for t in range(1, TT):
                latent_products(t)
            pe.wait_ge(s["mproj_taken"], 4 * TT)
            for t in range(TT):
                pe.wait_ge(s["mrope_ready"], t + 1)
                for b in range(4):
                    if t:
                        pe.wait_ge(s["mqT_taken"], 4 * (t - 1) + b + 1)
                    for i in range(4):
                        last = pe.transpose(ps[0:QK, b, i * P:(i + 1) * P], qk[:, t, 4 * b + i, :], ident[:, :])
                    last.then_inc(s["mqT_mm"], 1)
            pe.wait_ge(s["mqT_taken"], 4 * TT)
            NU = TT * H
            for i in range(NU + 3):
                if i < NU:
                    t, h = divmod(i, H)
                    if i >= 4:
                        pe.wait_ge(s["prob_ready"], i - 3)
                    pe.matmul(ps[:, 2 + i % 4, 0:(t + 1) * P], qkT[:, h, t * P:(t + 1) * P], qkT[:, H + h, 0:(t + 1) * P],
                              start=True, stop=True).then_inc(s["score_mm"], 1)
                if 2 <= i < NU + 2:
                    j = i - 2
                    t = j // H
                    pe.wait_ge(s["probn_ready"], j + 1)
                    if j >= 2:
                        pe.wait_ge(s["pT_taken"], j - 1)
                    for k in range(t + 1):
                        last = pe.transpose(ps[:, 6 + j % 2, k * P:(k + 1) * P], prob[:, j % 4, k * P:(k + 1) * P], ident[:, :])
                    last.then_inc(s["pT_mm"], 1)
                if i >= 3:
                    j = i - 3
                    t, h = divmod(j, H)
                    hp, par = divmod(h, 2)
                    pe.wait_ge(s["pT_taken"], j + 1)
                    if h == 0 and t >= 2:
                        pe.wait_ge(s["av_taken"], t - 1)
                    for k in range(t + 1):
                        last = pe.matmul(ps[par * DK:(par + 1) * DK, t % 2, hp * P:(hp + 1) * P], vtok[:, k, h, :],
                                         pT[:, j % 2, k, :], start=k == 0, stop=k == t)
                    last.then_inc(s["av_mm"], 1)
            pe.drain().then_inc(s["mla_over"], 1)
            pe.wait_ge(s["mla_over"], 4)
            for u in range(2 * TT + 1):
                if u < 2 * TT:
                    n, t = divmod(u, TT)
                    if not t:
                        wp = take_panel(PAN_Y + n, KD, 512)
                    if u >= 2:
                        pe.wait_ge(s["merged_ready"], u - 1)
                    for b, src in enumerate((oaT, obT)):
                        for k in range(HP):
                            last = pe.matmul(ps[:, 2 * (u % 2) + b, :], src[:, k, t * P:(t + 1) * P], wp[:, b * HP + k, :],
                                             start=k == 0, stop=k == HP - 1)
                    last.then_inc(s["y_mm"], 1)
                if u:
                    j = u - 1
                    pe.wait_ge(s["merged_ready"], j + 1)
                    if j >= 2:
                        pe.wait_ge(s["mT_taken"], j - 1)
                    for b in range(4):
                        last = pe.transpose(ps[:, 4 + j % 2, b * P:(b + 1) * P], sig[:, 0, j % TT, b * P:(b + 1) * P], ident[:, :])
                    last.then_inc(s["mT_mm"], 1)
            pe.wait_ge(s["mT_taken"], 2 * TT)
            for i in range(KD * DENSE_O, KD * DENSE_PQ):
                dense_slice(i, merged_hi, merged_lo, False)
            wp = take_panel(PAN_SK, SETS, NK)
            for u in range(SETS // 4):
                if u >= 2:
                    pe.wait_ge(s["sk_taken"], u - 1)
                for b in range(4):
                    last = pe.transpose(ps[:, 4 + u % 2, b * P:(b + 1) * P], wp[:, 4 * u + b, :], ident[:, :])
                last.then_inc(s["sk_mm"], 1)
            for u in range(2 * TT):
                t, hf = divmod(u, 2)
                pe.wait_ge(s["h2n_ready"], t + 1)
                if u >= 2:
                    pe.wait_ge(s["h2T_taken"], u - 1)
                for b in range(4):
                    last = pe.transpose(ps[:, 6 + u % 2, b * P:(b + 1) * P], x2n[:, t, (4 * hf + b) * P:(4 * hf + b + 1) * P], ident[:, :])
                last.then_inc(s["h2T_mm"], 1)
            pe.wait_ge(s["h_lo"], 4 * TT)
            pe.wait_ge(s["sk_taken"], SETS // 4)
            def scores(m):
                pe.wait_ge(s["dense_taken"], 4 * DENSE_PQ + m + 1)
                if m >= 2:
                    pe.wait_ge(s["sc_taken"], m - 1)
                for t in range(TT):
                    last = pe.matmul(ps[:, 6 + m % 2, t * P:(t + 1) * P], qTm[:, m % 4, t * P:(t + 1) * P], skT[:, m, :],
                                     start=True, stop=True)
                last.then_inc(s["sc_mm"], 1)

            for j in range(KD * 4):
                dense_slice(KD * DENSE_PQ + j, hhi, hlo, True)
                for m in range(SETS - 4):
                    if j == after(m, 0):
                        scores(m)
            for m in range(SETS - 4, SETS):
                scores(m)
            pe.drain().then_inc(s["early_over"], 1)
            pe.wait_ge(s["early_over"], 4)

            def selection(t):
                pe.wait_ge(s["sel_ready"], t + 1)
                if t:
                    pe.wait_ge(s["selT_taken"], t)
                for i in range(3):
                    last = pe.transpose(ps[:, 6, i * P:(i + 1) * P], sel[:, i, :, :].rearrange("p h k -> p (h k)"), ident[:, :])
                last.then_inc(s["selT_mm"], 1)

            def u_transposes(sl, use):
                pe.wait_ge(raw_loaded[sl], use)
                for k in range(KD):
                    last = pe.transpose(ps[:, 2 * sl + k // 4, (k % 4) * P:(k % 4 + 1) * P], raw[:, sl, k * P:(k + 1) * P], ident[:, :])
                last.then_inc(s["u_tmm"], 1)

            def u_products(sl, n, k0=0, k1=KD):
                if not k0:
                    pe.wait_ge(s["u_lo"], n)
                for k in range(k0, k1):
                    c = slice(k * P, (k + 1) * P)
                    pe.matmul(ps[:, 4 + sl, :], opr_hi[:, sl, c], hhi[:, k, :], start=k == 0, stop=False)
                    pe.matmul(ps[:, 4 + sl, :], opr_hi[:, sl, c], hlo[:, k, :], start=False, stop=False)
                    last = pe.matmul(ps[:, 4 + sl, :], opr_lo[:, sl, c], hhi[:, k, :], start=False, stop=k == KD - 1)
                if k1 == KD:
                    last.then_inc(s["u_mm"], 1)

            def spread_gates(g, slot, first=False):
                pe.wait_ge(s["onehot_ready"], g + 1)
                for b in range(2):
                    if not first:
                        pe.wait_ge(s["gate_taken"], 2 * g - 1 + b)
                    for j in range(4):
                        o = ps[:, 6 + b, j * P:(j + 1) * P]
                        pe.matmul(o, colhot[:, slot, :, 4 * b + j], rowhi[:, slot, :, 4 * b + j], start=True, stop=False)
                        last = pe.matmul(o, colhot[:, slot, :, 4 * b + j], rowlo[:, slot, :, 4 * b + j], start=False, stop=True)
                last.then_inc(s["spread_mm"], 1)

            def u_spread(i, use, sl, first=False, more=True):
                if more:
                    u_transposes(1 - sl, use)
                j = i - LEAD
                u_products(sl, i + 1, 0, KD // 2)
                if first:
                    u_products(sl, i + 1, KD // 2, KD)
                    selection(TT - 1)
                    pe.wait_ge(s["selT_taken"], TT)
                spread_gates(2 * j, 0, first)
                if not first:
                    u_products(sl, i + 1, KD // 2, KD)
                spread_gates(2 * j + 1, 1)

            def v_products(sl, n, first, final):
                pe.wait_ge(s["v_lo"], n)
                pe.wait_ge(s["w_ready"], n)
                for k in range(KD):
                    c = slice(k * P, (k + 1) * P)
                    pe.matmul(ps[:, k, :], opr_hi[:, sl, c], w_hi[:, sl, :], start=first, stop=False)
                    pe.matmul(ps[:, k, :], opr_hi[:, sl, c], w_lo[:, sl, :], start=False, stop=False)
                    last = pe.matmul(ps[:, k, :], opr_lo[:, sl, c], w_hi[:, sl, :], start=False, stop=final)
                    if final and k < KD - 1:
                        last.then_inc(s["y_bank"], 1)
                last.then_inc(s["v_mm"], 1)

            base = uses = 0
            for g, size in enumerate(GROUPS):
                if g:
                    pe.wait_ge(s["y_copied"], (g - 1) * KD + 2)
                u_transposes(0, 16 * (uses + 1))
                if g == 0:
                    for i in range(LEAD):
                        u_transposes(1 - i % 2, 16 * ((i + 1) // 2 + 1))
                        u_products(i % 2, i + 1)
                        if i > PARTS and (i - LATE) % PARTS == 0:
                            selection((i - LATE) // PARTS - 1)
                    for sl in range(2):
                        u_spread(LEAD + sl, 16 * ((LEAD + sl + 1) // 2 + 1), sl, first=not sl)
                    with pe.Fori(LEAD // 2 + 1, size // 2 - 1) as it:
                        for sl in range(2):
                            u_spread(2 * it + sl, 16 * it + 16 * (1 + sl), sl)
                    for sl in range(2):
                        u_spread(size - 2 + sl, 16 * (size // 2), sl, more=not sl)
                    pe.wait_ge(s["gate_taken"], 2 * NG)
                else:
                    pe.wait_ge(s["y_copied"], g * KD)
                    with pe.Fori(0, size // 2 - 1) as it:
                        u_transposes(1, 16 * it + 16 * (uses + 1))
                        u_products(0, 2 * it + (base + 1))
                        u_transposes(0, 16 * it + 16 * (uses + 2))
                        u_products(1, 2 * it + (base + 2))
                    u_transposes(1, 16 * (uses + size // 2))
                    u_products(0, base + size - 1)
                    u_products(1, base + size)
                pe.wait_ge(s["act_ready"], base + size)
                v_products(0, base + 1, True, False)
                v_products(1, base + 2, False, False)
                with pe.Fori(1, size // 2 - 1) as it:
                    v_products(0, 2 * it + (base + 1), False, False)
                    v_products(1, 2 * it + (base + 2), False, False)
                v_products(0, base + size - 1, False, False)
                v_products(1, base + size, False, True)
                base += size
                uses += size
            for u in range(2 * TT):
                hf, t = divmod(u, TT)
                pe.wait_ge(s["y_copied"], 2 * KD + 4 * (hf + 1))
                if u >= 2:
                    pe.wait_ge(s["y_added"], u - 1)
                for b in range(4):
                    last = pe.transpose(ps[:, u % 2, b * P:(b + 1) * P], y0T[:, 4 * hf + b, t * P:(t + 1) * P], ident[:, :])
                last.then_inc(s["yT_mm"], 1)

        @block.scalar
        def _(act_e):
            link = linker(act_e, s["act_step"])
            A = nc.scalar.activation
            for t in range(TT):
                act_e.wait_ge(x_loaded[t], 16)
                link(A(xjunk[:, :], xt[:, t, :], ACT.Square, accum_out=ss[:, t:t + 1]))
                act_e.nop().then_inc(s["sumsq_ready"], 1)
            def split_hi(i):
                d, k = divmod(i, KD)
                n, w = dense[d]
                if k == 0:
                    act_e.wait_ge(w_loaded[n % NW], loads_by(n))
                if i >= NS:
                    wait_used(act_e, i - NS)
                A(whi[:, i % NS, 0:w], panel(n, KD, w)[:, k, :], ACT.Copy).then_inc(s["slice_hi"], 1)

            def h_part(u, taken):
                t, hf = divmod(u % (2 * TT), 2)
                act_e.wait_ge(taken, u % (2 * TT) + 1)
                A(hhi[:, 4 * hf:4 * hf + 4, t * P:(t + 1) * P], htmp[:, u % 2, :].rearrange("p (a b) -> p a b", a=4), ACT.Copy)\
                    .then_inc(s["h_hi"], 1)

            def take_dense(d):
                for b in range(4):
                    act_e.wait_ge(s["dense_mm"], 4 * d + b + 1)
                    w = dense[d][1]
                    src = ps[:, b, 0:w]
                    if d < DENSE_TOK:
                        m = 4 * d + b
                        if m >= 4:
                            act_e.wait_ge(s["conv_out"], m - 3)
                        ins = A(cin[:, b, 3:], src, ACT.Copy)
                    elif d == DENSE_TOK:
                        ins = A(zs[:, b, :], src, ACT.Silu)
                    elif d == DENSE_TOK + 1:
                        ins = A(ptok[:, b, 0:w], src, ACT.Copy)
                    elif d == DENSE_TOK + 2:
                        ins = A(ptok[:, b, 16 + QL:16 + QL + w], src, ACT.Copy)
                    elif d < DENSE_O:
                        if d > DENSE_GATES:
                            act_e.wait_ge(sig_stored[b], 16 * (d - DENSE_GATES))
                        ins = A(sig_out[:, b, :], src, ACT.Sigmoid)
                    else:
                        ins = A(qTm[:, b, :], src, ACT.Copy)
                    ins.then_inc(s["dense_taken"], 1)
                if DENSE_GATES <= d < DENSE_O:
                    g, n = divmod(d - DENSE_GATES, 2)
                    for b in range(4):
                        act_e.wait_ge(s["dense_taken"], 4 * d + b + 1)
                        act_e.dma_start(sig_d[b][:, g, n * 512:(n + 1) * 512], sig_out[:, b, :]).then_inc(sig_stored[b], 16)

            for u in range(2 * TT):
                h_part(u, s["hT_ready"])
                if u >= 2 * TT - NS:
                    split_hi(u - (2 * TT - NS))
            for i in range(KD * DENSE_O):
                if i >= NS:
                    split_hi(i)
                if i % KD == 2 and i > KD:
                    take_dense(i // KD - 1)
                for m in range(NB):
                    if i == after(m, 4):
                        act_e.wait_ge(s["conv_out"], m + 1)
                        if m >= 2:
                            act_e.wait_ge(s["qkvT_mm"], m - 1)
                        A(csil[:, m % 2, :], cacc[:, m % 2, :], ACT.Silu).then_inc(s["silu_ready"], 1)
                if i == GATE_STEPS[1]:
                    act_e.wait_ge(s["small_loaded"], 16 * SMALL)
                    act_e.wait_ge(s["dense_taken"], 4 * (DENSE_TOK + 2))
                    link(A(beta[:, :, :], ptok[:, :, 0:H], ACT.Sigmoid))
                    link(A(ealog[:, :], alog[:, :], ACT.Exp))
                    act_e.wait_ge(s["gates_in"], 1)
                    link(A(gtmp[2][:, :, :], gtmp[1][:, :, :], ACT.Exp))
                    act_e.nop().then_inc(s["gates_exp"], 1)
                if i == GATE_STEPS[3]:
                    act_e.wait_ge(s["gates_in"], 2)
                    link(A(gtmp[4][:, :, :], gtmp[3][:, :, :], ACT.Ln))
                    act_e.nop().then_inc(s["gates_exp"], 1)
                if i == GATE_STEPS[5]:
                    act_e.wait_ge(s["gsum_mm"], 1)
                    link(A(gsum[:, :, :], ps[:, 6, 0:P].rearrange("p (a b) -> p a b", a=4), ACT.Copy))
                    link(A(eg[:, :, :].rearrange("p t h -> p (t h)"), gsum[:, 0, :], ACT.Exp))
                    link(A(egl[:, :, :, :].rearrange("p c t h -> p (c t h)"), gsum[:, 2:4, :].rearrange("p a b -> p (a b)"), ACT.Exp))
                    act_e.nop().then_inc(s["gsum_exp"], 1)
                if i == GATE_STEPS[7]:
                    act_e.wait_ge(s["gates_in"], 3)
                    link(A(ekd[:, :, :], gtmp[5][:, :, :], ACT.Exp))
                    act_e.nop().then_inc(s["gsum_exp"], 1)
                if LATENT_STEP <= i < LATENT_STEP + TT:
                    t = i - LATENT_STEP
                    link(A(htmp[:, 0, 0:QL], ptok[:, t, 16:16 + QL], ACT.Square, accum_out=rss[:, 0, t:t + 1]))
                    link(A(htmp[:, 1, 0:KVL], ptok[:, t, 16 + QL:16 + QL + KVL], ACT.Square, accum_out=rss[:, 1, t:t + 1]))
                    if t == TT - 1:
                        act_e.nop().then_inc(s["msq_ready"], 1)
                if i == LATENT_STEP + 12:
                    act_e.wait_ge(s["ang_ready"], 1)
                    A(sin[:, :, :], ang[2][:, :, :], ACT.Sin).then_inc(s["trig_ready"], 1)
                    A(cos[:, :, :], ang[5][:, :, :], ACT.Sin).then_inc(s["trig_ready"], 1)
            take_dense(DENSE_O - 1)
            for t in range(TT):
                act_e.wait_ge(sig_stored[t], 16 * 4)

            def decay_exp(t):
                act_e.wait_ge(s["gexp_in"], t + 1)
                A(decay[:, :, :, :], decay[:, :, :, :], ACT.Exp).then_inc(s["gexp_ready"], 1)

            def take_scan(t, c):
                r = slice(c * CH, (c + 1) * CH)
                act_e.wait_ge(s["go_mm"], 2 * t + c + 1)
                if t:
                    act_e.wait_ge(s["onorm_ready"], t)
                A(otok[r, :], ps[r, 0, :], ACT.Copy).then_inc(s["go_taken"], 1)

            def take_out(t, bank=4):
                act_e.wait_ge(s["oT_mm"], t + 1)
                A(oaT[:, :, t * P:(t + 1) * P], ps[:, bank, :].rearrange("p (a b) -> p a b", a=HP), ACT.Copy).then_inc(s["oT_taken"], 1)

            decay_exp(0)
            for t in range(TT):
                for i in range(4):
                    act_e.wait_ge(s["gT_mm"], 4 * t + i + 1)
                    dst = tposed[:, i, :, :] if i < 3 else qgT[:, t % 2, :, :]
                    A(dst, ps[:, i, :].rearrange("p (a b) -> p a b", a=HP), ACT.Copy).then_inc(s["gT_taken"], 1)
                for lv in range(1, 6):
                    for par in range(2):
                        act_e.wait_ge(y_mm[par], 6 * t + lv + 1)
                        if 5 * t + lv > 1:
                            act_e.wait_ge(lev_mm[par], 5 * t + lv - 1)
                        A(ysb[:, par, :, :], ps[:, 2 + par, :].rearrange("p (b c) -> p b c", b=HP), ACT.Copy).then_inc(y_taken[par], 1)
                    if t and lv in (1, 3):
                        take_scan(t - 1, lv // 2)
                if t + 1 < TT:
                    decay_exp(t + 1)
                act_e.wait_ge(s["guw_mm"], t + 1)
                if t:
                    act_e.wait_ge(s["gvn_ready"], 2 * t)
                A(usb[:, :], ps[:, 2, :], ACT.Copy).then_inc(s["guw_taken"], 1)
                A(wT[:, :, :], ps[:, 3, :].rearrange("p (a b) -> p a b", a=HP), ACT.Copy).then_inc(s["guw_taken"], 1)
                if t:
                    take_out(t - 1)
            for c in range(2):
                take_scan(TT - 1, c)
            take_out(TT - 1, 2)
            act_e.drain().then_inc(s["gdn_over"], 1)
            act_e.wait_ge(s["gdn_over"], 4)
            for t in range(TT):
                act_e.wait_ge(s["mproj_mm"], t + 1)
                b, q = LATENT_OUT[t % 2], qk[:, t, :, :]
                A(q[:, 0:H, :].rearrange("p a b -> p (a b)"), ps[:, b:b + 2, :].rearrange("p a b -> p (a b)")[:, 0:H * QK], ACT.Copy)\
                    .then_inc(s["mproj_taken"], 1)
                kv = ps[:, b + 2:b + 4, :].rearrange("p a (h c) -> p (a h) c", c=2 * DK)
                A(q[:, H:, 0:NOPE], kv[:, :, 0:NOPE], ACT.Copy).then_inc(s["mproj_taken"], 1)
                A(vtok[:, t, :, :], kv[:, :, NOPE:], ACT.Copy).then_inc(s["mproj_taken"], 1)
                A(q[:, H:, NOPE:], bc(ptok[:, t, 16 + QL + KVL:], H, 1), ACT.Copy).then_inc(s["mproj_taken"], 1)
                act_e.wait_ge(s["mproj_taken"], 4 * (t + 1))
                if t:
                    act_e.wait_ge(s["mqms_ready"], t)
                A(qsq[:, :, :], q, ACT.Square).then_inc(s["mqsq_ready"], 1)
            for t in range(TT):
                for b in range(4):
                    act_e.wait_ge(s["mqT_mm"], 4 * t + b + 1)
                    A(qkT[:, 4 * b:4 * b + 4, t * P:(t + 1) * P], ps[0:QK, b, :].rearrange("p (a b) -> p a b", a=4), ACT.Copy)\
                        .then_inc(s["mqT_taken"], 1)
            NU = TT * H
            for i in range(NU + 2):
                if i < NU:
                    t = i // H
                    act_e.wait_ge(s["negmax_ready"], i + 1)
                    if i >= 4:
                        act_e.wait_ge(s["pT_mm"], i - 3)
                    A(prob[:, i % 4, 0:(t + 1) * P], ps[:, 2 + i % 4, 0:(t + 1) * P], ACT.Exp, bias=nmx[:, i:i + 1],
                      scale=QK ** -0.5, accum_out=rsum[:, i:i + 1]).then_inc(s["prob_ready"], 1)
                if i >= 2:
                    j = i - 2
                    t, h = divmod(j, H)
                    act_e.wait_ge(s["pT_mm"], j + 1)
                    if j >= 2:
                        act_e.wait_ge(s["av_mm"], j - 1)
                    A(pT[:, j % 2, 0:t + 1, :], ps[:, 6 + j % 2, 0:(t + 1) * P].rearrange("p (a b) -> p a b", b=P), ACT.Copy)\
                        .then_inc(s["pT_taken"], 1)
                    if h == 1 and t:
                        act_e.wait_ge(s["av_mm"], t * H)
                        A(obT[:, :, (t - 1) * P:t * P], ps[:, (t - 1) % 2, :].rearrange("p (a b) -> p a b", a=HP), ACT.Copy)\
                            .then_inc(s["av_taken"], 1)
            act_e.wait_ge(s["av_mm"], NU)
            A(obT[:, :, (TT - 1) * P:], ps[:, (TT - 1) % 2, :].rearrange("p (a b) -> p a b", a=HP), ACT.Copy)\
                .then_inc(s["av_taken"], 1)
            act_e.drain().then_inc(s["mla_over"], 1)
            act_e.wait_ge(s["mla_over"], 4)
            for u in range(2 * TT):
                n, t = divmod(u, TT)
                act_e.wait_ge(s["mT_mm"], u + 1)
                A(merged_hi[:, 4 * n:4 * n + 4, t * P:(t + 1) * P], ps[:, 4 + u % 2, :].rearrange("p (a b) -> p a b", a=4), ACT.Copy)\
                    .then_inc(s["m_hi"], 1)
            for i in range(KD * DENSE_O, KD * DENSE_PQ):
                split_hi(i)
            for t in range(TT):
                act_e.wait_ge(s["dense_taken"], 4 * (DENSE_PQ - 1) + t + 1)
                link(A(junk2[:, :], x2[:, t, :], ACT.Square, accum_out=ss[:, t:t + 1]))
                act_e.nop().then_inc(s["ss2_ready"], 1)
            for i in range(NS):
                split_hi(KD * DENSE_PQ + i)
            for u in range(SETS // 4):
                act_e.wait_ge(s["sk_mm"], u + 1)
                A(skT[:, 4 * u:4 * u + 4, :], ps[:, 4 + u % 2, :].rearrange("p (a b) -> p a b", a=4), ACT.Copy).then_inc(s["sk_taken"], 1)
            for u in range(2 * TT):
                h_part(2 * TT + u, s["h2T_taken"])
            act_e.wait_ge(x2_stored, 16)

            def take_scores(m):
                act_e.wait_ge(s["sc_mm"], m + 1)
                A(sc[:, :, m, :], ps[:, 6 + m % 2, :].rearrange("p (t n) -> p t n", t=TT), ACT.Copy).then_inc(s["sc_taken"], 1)

            for j in range(KD * 4):
                if j >= NS:
                    split_hi(KD * DENSE_PQ + j)
                if j % KD == 2 and j > KD:
                    take_dense(DENSE_PQ + j // KD - 1)
                for m in range(SETS - 4):
                    if j == after(m, 3):
                        take_scores(m)
            take_dense(DENSE_PQ + 3)
            for m in range(SETS - 4, SETS):
                take_scores(m)
            act_e.drain().then_inc(s["early_over"], 1)
            act_e.wait_ge(s["early_over"], 4)
            wide = lambda sl: ps[:, 2 * sl:2 * sl + 2, :].rearrange("p a b -> p (a b)")

            def u_hi(sl, n):
                act_e.wait_ge(s["u_tmm"], n)
                A(opr_hi[:, sl, :], wide(sl), ACT.Copy).then_inc(s["u_hi"], 1)

            def u_act(sl, n, at):
                act_e.wait_ge(s["u_mm"], n)
                A(act[:, at, :] if isinstance(at, int) else act[:, bass.ds(at, 1), :].rearrange("p a b -> p (a b)"),
                  ps[:, 4 + sl, :], ACT.Gelu).then_inc(s["act_ready"], 1)

            def take_gates(g, half, slot):
                act_e.wait_ge(s["spread_mm"], g + 1)
                for b in range(2):
                    at = half * GT + 4 * b
                    A(stage[:, slot, :, at:at + 4].rearrange("p i t -> p t i"), ps[:, 6 + b, :].rearrange("p (t i) -> p t i", t=4),
                      ACT.Copy, scale=1 / GSCALE).then_inc(s["gate_taken"], 1)

            def store_gates(j, slot):
                act_e.wait_ge(s["gate_taken"], 4 * j + 4)
                dst = g_d[bass.ds(j, 1)].rearrange("a p i t -> p (a i t)")
                act_e.dma_start(dst, stage[:, slot, :, :].rearrange("p i t -> p (i t)")).then_inc(gate_stored[slot], 16)

            def u_gates(i, sl, at, first=False, more=True, stored=None):
                u_act(1 - sl, i, at)
                j = i - LEAD
                if not first:
                    take_gates(2 * j - 1, 1, 1 - sl)
                    store_gates(j - 1, 1 - sl)
                if more:
                    u_hi(1 - sl, i + 2)
                if stored is not None:
                    act_e.wait_ge(gate_stored[sl], stored)
                take_gates(2 * j, 0, sl)

            def v_hi(sl, n, use):
                act_e.wait_ge(raw_loaded[sl], use)
                A(opr_hi[:, sl, :], raw[:, sl, :], ACT.Copy).then_inc(s["v_hi"], 1)
                act_e.wait_ge(s["w_prod"], n)
                a = act[:, bass.ds(n - 1 - base, 1), :].rearrange("p a b -> p (a b)")
                A(w_hi[:, sl, :], a, ACT.Copy).then_inc(s["w_hi_ready"], 1)

            base = uses = 0
            for g, size in enumerate(GROUPS):
                if g:
                    act_e.wait_ge(s["v_mm"], base)
                u_hi(0, base + 1)
                u_hi(1, base + 2)
                if g == 0:
                    for i in range(1, LEAD):
                        u_act((i - 1) % 2, i, i - 1)
                        u_hi((i + 1) % 2, i + 2)
                        if i > LATE and (i - LATE) % PARTS == 3:
                            act_e.wait_ge(s["best_ready"], (i - LATE) // PARTS + 1)
                            A(best[:, :, :], best[:, :, :], ACT.Exp).then_inc(s["gexp2_ready"], 1)
                    for sl in range(2):
                        u_gates(LEAD + sl, sl, LEAD + sl - 1, first=not sl)
                    with act_e.Fori(LEAD // 2 + 1, size // 2 - 1) as it:
                        for sl in range(2):
                            u_gates(2 * it + sl, sl, 2 * it + (sl - 1), stored=it * 16 - 16 * (LEAD // 2))
                    for sl in range(2):
                        u_gates(size - 2 + sl, sl, size - 3 + sl, more=not sl, stored=16 * (size // 2 - 1 - LEAD // 2))
                    u_act(1, size, size - 1)
                    take_gates(NG - 1, 1, 1)
                    store_gates(NG // 2 - 1, 1)
                else:
                    with act_e.Fori(0, size // 2 - 1) as it:
                        for sl in range(2):
                            u_act(sl, 2 * it + (base + 1 + sl), 2 * it + sl)
                            u_hi(sl, 2 * it + (base + 3 + sl))
                    for sl in range(2):
                        u_act(sl, base + size - 1 + sl, size - 2 + sl)
                rb = uses + size // 2
                for sl in range(2):
                    v_hi(sl, base + 1 + sl, 16 * (rb + 1))
                with act_e.Fori(1, size // 2) as it:
                    for sl in range(2):
                        act_e.wait_ge(s["v_mm"], 2 * it + (base - 1 + sl))
                        v_hi(sl, 2 * it + (base + 1 + sl), 16 * it + 16 * (rb + 1))
                if g < 2:
                    for k in range(KD):
                        wait_y_bank(act_e, g, k)
                        A(ystage[:, k, :], ps[:, k, :], ACT.Copy).then_inc(s["y_copied"], 1)
                base += size
                uses += size

        @block.vector
        def _(dve):
            link = linker(dve, s["dve_step"])
            V = nc.vector
            tt, ts, stt = V.tensor_tensor, V.tensor_scalar, V.scalar_tensor_tensor
            for t in range(TT):
                dve.wait_ge(s["sumsq_ready"], t + 1)
                ts(ss[:, t:t + 1], ss[:, t:t + 1], 1.0 / D, EPS, ALU.mult, ALU.add).then_inc(s["meansq_ready"], 1)
            link(V.memset(cin[:, :, 0:3], 0.0))
            for t in range(TT):
                dve.wait_ge(s["rstd_ready"], t + 1)
                ts(xt[:, t, :], xt[:, t, :], rs[:, t:t + 1], None, ALU.mult).then_inc(s["xn_ready"], 1)

            def split_lo(i):
                d, k = divmod(i, KD)
                n, w = dense[d]
                dve.wait_ge(s["slice_hi"], i + 1)
                tt(wlo[:, i % NS, 0:w], panel(n, KD, w)[:, k, :], whi[:, i % NS, 0:w].bitcast(F32), ALU.subtract)\
                    .then_inc(s["slice_ready"], 1)

            def h_rest(v):
                t, hf = divmod(v % (2 * TT), 2)
                b = (slice(None), slice(4 * hf, 4 * hf + 4), slice(t * P, (t + 1) * P))
                dve.wait_ge(s["h_hi"], v + 1)
                tt(hlo[b], htmp[:, v % 2, :].rearrange("p (a b) -> p a b", a=4), hhi[b].bitcast(F32), ALU.subtract)\
                    .then_inc(s["h_lo"], 1)

            def h_gain(v, mm, taken, gain):
                t, hf = divmod(v % (2 * TT), 2)
                dve.wait_ge(mm, v % (2 * TT) + 1)
                if v >= 2:
                    dve.wait_ge(s["h_lo"], v - 1)
                tt(htmp[:, v % 2, :].rearrange("p (a b) -> p a b", a=4), ps[:, 6 + v % 2, :].rearrange("p (a b) -> p a b", a=4),
                   bc(gain[:, 4 * hf:4 * hf + 4], P, 2), ALU.mult).then_inc(taken, 1)
                if v % (2 * TT):
                    h_rest(v - 1)
                if v % (2 * TT) == 2 * TT - 1:
                    h_rest(v)

            dve.wait_ge(s["g1_loaded"], 16)
            for u in range(2 * TT):
                h_gain(u, s["xT_mm"], s["hT_ready"], g1)
                if u >= 2 * TT - NS:
                    split_lo(u - (2 * TT - NS))
            dve.wait_ge(s["small_loaded"], 16 * SMALL)

            def conv(m):
                dve.wait_ge(s["dense_taken"], m + 1)
                if m >= 2:
                    dve.wait_ge(s["silu_ready"], m - 1)
                x0, acc = cin[:, m % 4, :], cacc[:, m % 2, :]
                link(ts(acc, x0[:, 0:S], cw[:, m, 0:1], None, ALU.mult))
                for j in (1, 2):
                    link(stt(acc, x0[:, j:j + S], cw[:, m, j:j + 1], acc, ALU.mult, ALU.add))
                stt(acc, x0[:, 3:3 + S], cw[:, m, 3:4], acc, ALU.mult, ALU.add).then_inc(s["conv_out"], 1)

            def norms(t):
                qk2 = qkv[:, t, 0:1024].rearrange("p (h d) -> p h d", h=2 * H)
                link(tt(sq[:, :, :], qk2, qk2, ALU.mult))
                link(V.reduce_sum(ms[:, :], sq[:, :, :], AX.X))
                ts(ms[:, :], ms[:, :], EPS, None, ALU.add).then_inc(s["gms_ready"], 1)

            def derive(t):
                q2, k2, v2 = (h3(qkv[:, t, i * 512:(i + 1) * 512]) for i in range(3))
                qk2 = qkv[:, t, 0:1024].rearrange("p (h d) -> p h d", h=2 * H)
                b8 = lambda ap: bc(ap[:, t, :], DK, 2)
                dve.wait_ge(s["grn_ready"], t + 1)
                link(ts(rn[:, 0:H], rn[:, 0:H], DK ** -0.5, None, ALU.mult))
                link(tt(qk2, qk2, bc(rn[:, :], DK, 2), ALU.mult))
                link(tt(h3(kb[:, :]), k2, b8(beta), ALU.mult))
                tt(h3(kbg[:, t % 2, :]), h3(kb[:, :]), b8(eg), ALU.mult)
                tt(h3(kd[:, t % 2, :]), k2, b8(ekd), ALU.mult)
                tt(h3(qg[:, :]), q2, b8(eg), ALU.mult)
                tt(v2, v2, b8(beta), ALU.mult).then_inc(s["gderived"], 1)

            h3 = lambda ap: ap.rearrange("p (h d) -> p h d", h=H)
            fl = lambda ap: ap.rearrange("p t h -> p (t h)")
            araw = ptok[:, :, H:2 * H]
            for i in range(KD * DENSE_O):
                if i >= NS:
                    split_lo(i)
                for m in range(NB):
                    if i == after(m, 3):
                        conv(m)
                    if i == after(m, 7):
                        dve.wait_ge(s["qkvT_mm"], m + 1)
                        V.tensor_copy(qkv[:, :, m * P:(m + 1) * P], ps[:, 4 + m % 2, :].rearrange("p (t c) -> p t c", t=TT))\
                            .then_inc(s["qkv_tok"], 1)
                if i == GATE_STEPS[0]:
                    dve.wait_ge(s["dense_taken"], 4 * (DENSE_TOK + 2))
                    link(tt(gtmp[0][:, :, :], araw, bc(dtb[:, :], TT, 1), ALU.add))
                    link(ts(gtmp[1][:, :, :], gtmp[0][:, :, :], -1.0, None, ALU.mult))
                    tt(gtmp[1][:, :, :], gtmp[0][:, :, :], gtmp[1][:, :, :], ALU.min).then_inc(s["gates_in"], 1)
                if i == GATE_STEPS[2]:
                    dve.wait_ge(s["gates_exp"], 1)
                    ts(gtmp[3][:, :, :], gtmp[2][:, :, :], 1.0, None, ALU.add).then_inc(s["gates_in"], 1)
                    dve.wait_ge(s["gates_in"], 2)
                    link(ts(gtmp[5][:, :, :], gtmp[3][:, :, :], 1.0, 1e-30, ALU.subtract, ALU.max))
                    link(V.reciprocal(gtmp[5][:, :, :], gtmp[5][:, :, :]))
                    link(tt(gtmp[5][:, :, :], gtmp[5][:, :, :], gtmp[2][:, :, :], ALU.mult))
                if i == GATE_STEPS[4]:
                    dve.wait_ge(s["gates_exp"], 2)
                    link(tt(gtmp[5][:, :, :], gtmp[5][:, :, :], gtmp[4][:, :, :], ALU.mult))
                    link(ts(gtmp[0][:, :, :], gtmp[0][:, :, :], 0.0, None, ALU.max))
                    link(tt(gtmp[5][:, :, :], gtmp[5][:, :, :], gtmp[0][:, :, :], ALU.add))
                    link(tt(gtmp[5][:, :, :], gtmp[5][:, :, :], bc(ealog[:, :], TT, 1), ALU.mult))
                    ts(gdec[:, :, :], gtmp[5][:, :, :], -1.0, None, ALU.mult).then_inc(s["gates_ready"], 1)
                if i == GATE_STEPS[6]:
                    norms(0)
                    dve.wait_ge(s["gsum_exp"], 1)
                    tt(fl(gtmp[5][:, :, :]), gsum[:, 1, :], gsum[:, 0, :], ALU.subtract).then_inc(s["gates_in"], 1)
                    for par in range(2):
                        r = slice(par * DK, (par + 1) * DK)
                        link(V.tensor_copy(egp[r, :, :, :], egl[r, :, :, :].rearrange("p c t (a b) -> p c t a b", b=2)[:, :, :, :, par]))
                    link(V.memset(vn[:, :], 0.0))
                    V.memset(state[:, :, :, :], 0.0).then_inc(s["gstate_ready"], 1)
                if i == GATE_STEPS[8]:
                    dve.wait_ge(s["consts_ready"], 2)
                    dve.wait_ge(s["gsum_exp"], 2)
                    derive(0)
                if i == LATENT_STEP:
                    f32 = np.float32
                    two_pi = 2 * np.pi
                    c1 = float(f32(6.28125))
                    c2 = float((f32(two_pi - c1).view(np.uint32) & np.uint32(0xFFFFF000)).view(f32))
                    c3 = float(f32(two_pi - c1 - c2))
                    magic = float(1.5 * 2 ** 23)
                    pi = float(np.nextafter(f32(np.pi), f32(0)))
                    half_dim = ROPE // 2
                    freqs = np.power(f32(THETA), -np.arange(half_dim, dtype=f32) / f32(half_dim)).astype(f32)
                    for j in range(half_dim):
                        last = V.memset(invf[:, j:j + 1], float(freqs[j]))
                    link(last)
                    link(V.tensor_copy(posf[:, :], pos_i[:, :]))
                    a0, a1, a2, a3, a4, a5 = (a[:, :, :] for a in ang)
                    link(tt(a0, bc(posf[:, :], half_dim, 2), bc(invf[:, :], TT, 1), ALU.mult))
                    link(ts(a1, a0, 1 / two_pi, magic, ALU.mult, ALU.add))
                    link(ts(a1, a1, magic, None, ALU.subtract))
                    for c in (c1, c2, c3):
                        link(stt(a0, a1, -c, a0, ALU.mult, ALU.add))
                    link(ts(a2, a0, pi, -pi, ALU.min, ALU.max))
                    link(ts(a3, a0, np.pi / 2, None, ALU.add))
                    link(ts(a4, a3, pi, -two_pi, ALU.is_gt, ALU.mult))
                    link(tt(a5, a3, a4, ALU.add))
                    ts(a5, a5, pi, -pi, ALU.min, ALU.max).then_inc(s["ang_ready"], 1)
                if i == LATENT_STEP + 5:
                    dve.wait_ge(s["msq_ready"], 1)
                    link(ts(rss[:, 0, :], rss[:, 0, :], 1.0 / QL, EPS, ALU.mult, ALU.add))
                    ts(rss[:, 1, :], rss[:, 1, :], 1.0 / KVL, EPS, ALU.mult, ALU.add).then_inc(s["mms_ready"], 1)
                if i == LATENT_STEP + 16:
                    dve.wait_ge(s["mrs_ready"], 1)
                    for t in range(TT):
                        cq, ckv = ptok[:, t, 16:16 + QL], ptok[:, t, 16 + QL:16 + QL + KVL]
                        link(ts(cq, cq, rrs[:, 0, t:t + 1], None, ALU.mult))
                        ts(ckv, ckv, rrs[:, 1, t:t + 1], None, ALU.mult).then_inc(s["mcn_ready"], 1)
            dec3 = decay[:, :, :, :].rearrange("p a b c -> p (a b) c")
            head = lambda b: ps[:, b, :].rearrange("p (b c) -> p b c", b=HP)
            id4 = bc(ident[:, :], HP, 1)

            def decays(t):
                dve.wait_ge(s["grow_mm"], t + 1)
                gc = gsum[:, 0, t * H:(t + 1) * H].rearrange("p (a b) -> p b a", b=2)
                for par in range(2):
                    last = tt(decay[:, par, :, :], head(par), bc(gc[:, par, :], P, 2), ALU.subtract)
                link(last)
                tt(dec3, dec3, bc(negmask[:, :], 2 * HP, 1), ALU.add).then_inc(s["gexp_in"], 1)

            def off_diagonal(lv, par):
                return tt(offd[:, par, :, :], upper[:, par, :, :], bc(level[1 << lv][:, :], HP, 1), ALU.mult)

            def new_values(t, c):
                r = slice(c * CH, (c + 1) * CH)
                dve.wait_ge(s["gws_mm"], 2 * t + c + 1)
                tt(vn[r, :], usb[r, :], ps[r, 0, :], ALU.subtract).then_inc(s["gvn_ready"], 1)

            def new_state(t, c):
                dve.wait_ge(s["go_mm"], 2 * t + c + 1)
                for par in range(2):
                    pr = slice(par * DK, (par + 1) * DK)
                    last = tt(state[pr, :, par, :], state[pr, :, par, :], bc(egp[pr, c, t, :], DK, 2), ALU.mult)
                link(last)
                for par in range(2):
                    pr = slice(par * DK, (par + 1) * DK)
                    up = ps[pr, 1, :].rearrange("p (a b d) -> p a b d", a=HP, b=2)[:, :, par, :]
                    last = tt(state[pr, :, par, :], state[pr, :, par, :], up, ALU.add)
                last.then_inc(s["gstate_ready"], 1)

            def out_squares(t):
                dve.wait_ge(s["go_taken"], 2 * (t + 1))
                link(tt(sq[:, 0:H, :], h3(otok[:, :]), h3(otok[:, :]), ALU.mult))
                link(V.reduce_sum(oms[:, :], sq[:, 0:H, :], AX.X))
                ts(oms[:, :], oms[:, :], 1.0 / DK, EPS, ALU.mult, ALU.add).then_inc(s["onsq_ready"], 1)

            def out_norm(t):
                dve.wait_ge(s["onrs_ready"], t + 1)
                if t:
                    dve.wait_ge(s["oT_mm"], t)
                link(tt(h3(onrm[:, :]), h3(otok[:, :]), bc(orn[:, :], DK, 2), ALU.mult))
                link(tt(h3(onrm[:, :]), h3(onrm[:, :]), bc(ggdn[:, :], H, 1), ALU.mult))
                tt(onrm[:, :], onrm[:, :], zs[:, t, :], ALU.mult).then_inc(s["onorm_ready"], 1)

            decays(0)
            for t in range(TT):
                dve.wait_ge(s["gexp_ready"], t + 1)
                for par in range(2):
                    dve.wait_ge(s["gkk_mm"], 2 * t + par + 1)
                    link(tt(upper[:, par, :, :], head(6 + par), decay[:, par, :, :], ALU.mult))
                    off_diagonal(0, par).then_inc(offd_ready[par], 1)
                dve.wait_ge(s["gqk_mm"], t + 1)
                tt(attnT[:, t % 2, :, :, :], ps[:, 4:6, :].rearrange("p a (b c) -> p a b c", b=HP), decay[:, :, :, :], ALU.mult)\
                    .then_inc(s["gqk_taken"], 1)
                for lv in range(6):
                    for par in range(2):
                        dve.wait_ge(y_mm[par], 6 * t + lv + 1)
                        if lv == 0:
                            dve.wait_ge(offd_ready[par], 6 * t + 1)
                            tt(inv[:, par, :, :], id4, head(2 + par), ALU.subtract)
                            tt(invT[:, par, :, :], id4, offd[:, par, :, :], ALU.subtract).then_inc(lev_done[par], 1)
                            dve.wait_ge(lev_done[par], 6 * t + 1)
                        if lv < 5:
                            off_diagonal(lv + 1, par).then_inc(offd_ready[par], 1)
                    for par in range(2 if lv else 0):
                        dve.wait_ge(lev_mm[par], 5 * t + lv)
                        if lv < 5:
                            tt(inv[:, par, :, :], inv[:, par, :, :], head(4 + par), ALU.subtract)
                        tt(invT[:, par, :, :], invT[:, par, :, :], head(6 + par), ALU.subtract).then_inc(lev_done[par], 1)
                    if t and lv in (0, 2):
                        new_values(t - 1, lv // 2)
                    if lv == 1 and t + 1 < TT:
                        norms(t + 1)
                    if t and lv in (1, 3):
                        new_state(t - 1, lv // 2)
                    if t and lv == 3:
                        out_squares(t - 1)
                    if lv == 3 and t + 1 < TT:
                        derive(t + 1)
                    if lv == 4 and t + 1 < TT:
                        decays(t + 1)
                    if t and lv == 4:
                        out_norm(t - 1)

            def latent_gains(t):
                a = LATENT_BANKS[t % 2]
                dve.wait_ge(s["mcT_mm"], t + 1)
                tt(cqT[:, :, t * P:(t + 1) * P], ps[:, a, 0:QL].rearrange("p (a b) -> p a b", a=3), bc(gcq[:, :], P, 2), ALU.mult)
                tt(ckvT[:, :, t * P:(t + 1) * P], ps[:, a + 1, 0:KVL].rearrange("p (a b) -> p a b", a=2), bc(gckv[:, :], P, 2), ALU.mult)\
                    .then_inc(s["mcT_taken"], 1)

            for c in range(2):
                new_values(TT - 1, c)
                latent_gains(2 * c)
                latent_gains(2 * c + 1)
                new_state(TT - 1, c)
            out_squares(TT - 1)
            out_norm(TT - 1)
            dve.drain().then_inc(s["gdn_over"], 1)
            dve.wait_ge(s["gdn_over"], 4)

            half_dim = ROPE // 2
            dve.wait_ge(s["trig_ready"], 2)
            def qk_squares(t):
                dve.wait_ge(s["mqsq_ready"], t + 1)
                link(V.reduce_sum(qms[:, t % 2, :], qsq[:, :, :], AX.X))
                ts(qms[:, t % 2, :], qms[:, t % 2, :], 1.0 / QK, EPS, ALU.mult, ALU.add).then_inc(s["mqms_ready"], 1)

            qk_squares(0)
            for t in range(TT):
                if t + 1 < TT:
                    qk_squares(t + 1)
                q = qk[:, t, :, :]
                dve.wait_ge(s["mqrs_ready"], t + 1)
                link(tt(q, q, bc(qrn[:, t % 2, :], QK, 2), ALU.mult))
                for g in range(2):
                    part = q[:, g * H:(g + 1) * H, :]
                    last = tt(part, part, bc(gqk[:, g, :], H, 1), ALU.mult)
                link(last)
                x1, x2r = q[:, :, NOPE:NOPE + half_dim], q[:, :, NOPE + half_dim:]
                ct, st = bc(cos[:, t, :], 2 * H, 1), bc(sin[:, t, :], 2 * H, 1)
                tt(rt[0][:, :, :], x1, ct, ALU.mult)
                tt(rt[1][:, :, :], x2r, st, ALU.mult)
                tt(rt[2][:, :, :], x2r, ct, ALU.mult)
                link(tt(rt[3][:, :, :], x1, st, ALU.mult))
                tt(x1, rt[0][:, :, :], rt[1][:, :, :], ALU.subtract)
                tt(x2r, rt[2][:, :, :], rt[3][:, :, :], ALU.add).then_inc(s["mrope_ready"], 1)
            NU = TT * H
            for i in range(NU + 1):
                if i < NU:
                    t = i // H
                    n = (t + 1) * P
                    dve.wait_ge(s["score_mm"], i + 1)
                    link(V.memset(ps[0:CH, 2 + i % 4, n - CH:n], NEG))
                    link(V.reduce_max(mx[:, i:i + 1], ps[:, 2 + i % 4, 0:n], AX.X))
                    ts(nmx[:, i:i + 1], mx[:, i:i + 1], -QK ** -0.5, None, ALU.mult).then_inc(s["negmax_ready"], 1)
                if i:
                    j = i - 1
                    n = (j // H + 1) * P
                    dve.wait_ge(s["prob_ready"], j + 1)
                    link(V.reciprocal(rinv[:, j:j + 1], rsum[:, j:j + 1]))
                    ts(prob[:, j % 4, 0:n], prob[:, j % 4, 0:n], rinv[:, j:j + 1], None, ALU.mult).then_inc(s["probn_ready"], 1)
            dve.drain().then_inc(s["mla_over"], 1)
            dve.wait_ge(s["mla_over"], 4)
            for u in range(2 * TT + 1):
                if u < 2 * TT:
                    n, t = divmod(u, TT)
                    dve.wait_ge(sig_loaded[t], 16 * (n + 1))
                    dve.wait_ge(s["y_mm"], u + 1)
                    for g in range(2):
                        last = tt(sig[:, g, t, :], sig[:, g, t, :], ps[:, 2 * (u % 2) + g, :], ALU.mult)
                    link(last)
                    tt(sig[:, 0, t, :], sig[:, 0, t, :], sig[:, 1, t, :], ALU.add).then_inc(s["merged_ready"], 1)
                if u:
                    n, t = divmod(u - 1, TT)
                    b = (slice(None), slice(4 * n, 4 * n + 4), slice(t * P, (t + 1) * P))
                    dve.wait_ge(s["m_hi"], u)
                    tt(merged_lo[b], ps[:, 4 + (u - 1) % 2, :].rearrange("p (a b) -> p a b", a=4), merged_hi[b].bitcast(F32), ALU.subtract)\
                        .then_inc(s["mT_taken"], 1)
            dve.wait_ge(x_loaded[0], 32)

            def residual(n):
                for t in range(TT):
                    dve.wait_ge(s["dense_mm"], 4 * (DENSE_O + n) + t + 1)
                    xs = x2[:, t, n * 512:(n + 1) * 512]
                    tt(xs, xs, ps[:, t, :], ALU.add).then_inc(s["dense_taken"], 1)

            for i in range(KD * DENSE_O, KD * DENSE_PQ):
                split_lo(i)
                if i == KD * (DENSE_O + 1) + 2:
                    residual(0)
            residual(1)
            for t in range(TT):
                dve.wait_ge(s["ss2_ready"], t + 1)
                ts(ss[:, t:t + 1], ss[:, t:t + 1], 1.0 / D, EPS, ALU.mult, ALU.add).then_inc(s["ms2_ready"], 1)
            for t in range(TT):
                dve.wait_ge(s["rs2_ready"], t + 1)
                ts(x2n[:, t, :], x2[:, t, :], rs[:, t:t + 1], None, ALU.mult).then_inc(s["h2n_ready"], 1)
            for i in range(NS):
                split_lo(KD * DENSE_PQ + i)
            for u in range(2 * TT):
                h_gain(2 * TT + u, s["h2T_mm"], s["h2T_taken"], g2)
            dve.wait_ge(x2_stored, 16)
            def best_of_set(m):
                dve.wait_ge(s["sc_taken"], m + 1)
                for t in range(TT):
                    last = V.max(tops[:, t, m, 0:8], sc[:, t, m, :])
                link(last)
                for t in range(TT):
                    V.max_index(topi[:, t, m, 0:8], tops[:, t, m, 0:8], sc[:, t, m, :])
                    last = V.match_replace(sc2[:, t, :], tops[:, t, m, 0:8], sc[:, t, m, :], -BIG)
                link(last)
                for t in range(TT):
                    last = V.max(tops[:, t, m, 8:16], sc2[:, t, :])
                link(last)
                for t in range(TT):
                    last = V.max_index(topi[:, t, m, 8:16], tops[:, t, m, 8:16], sc2[:, t, :])
                link(last)

            for j in range(KD * 4):
                if j >= NS:
                    split_lo(KD * DENSE_PQ + j)
                for m in range(SETS - LATE):
                    if j == KD * (m // 4 + 1) + 4 + 2 * (m % 4):
                        best_of_set(m)
            best_of_set(SETS - LATE - 2)
            best_of_set(SETS - LATE - 1)
            dve.drain().then_inc(s["early_over"], 1)
            dve.wait_ge(s["early_over"], 4)
            side = lambda ap, t, p: ap[:, t, :, :].rearrange("p (h s) k -> p h s k", s=2)[:, :, p, :]
            b4 = lambda ap, at: bc(ap, PK, at)
            wide = lambda sl: ps[:, 2 * sl:2 * sl + 2, :].rearrange("p a b -> p (a b)")

            def u_lo(sl, n):
                dve.wait_ge(s["u_hi"], n)
                tt(opr_lo[:, sl, :], wide(sl), opr_hi[:, sl, :].bitcast(F32), ALU.subtract).then_inc(s["u_lo"], 1)

            def choose(t, part):
                if part == 0:
                    first, second = side(tops, t, 0), side(tops, t, 1)
                    link(tt(cand[:, :, 0:64].rearrange("p h (a b) -> p h a b", a=4), b4(first[:, :, 0:4], 3),
                            bc(second, 4, 2), ALU.add))
                    link(tt(cand[:, :, 64:].rearrange("p h (a b) -> p h a b", b=4), bc(first[:, :, 4:], 4, 3),
                            bc(second[:, :, 0:4], PK - 4, 2), ALU.add))
                    for h in range(H):
                        last = V.max(best[:, h, 0:8], cand[:, h, :])
                    link(last)
                    for h in range(H):
                        V.max_index(bpos[:, h, 0:8], best[:, h, 0:8], cand[:, h, :])
                        last = V.match_replace(cand2[:, h, :], best[:, h, 0:8], cand[:, h, :], -BIG)
                    link(last)
                elif part == 1:
                    for h in range(H):
                        last = V.max(best[:, h, 8:16], cand2[:, h, :])
                    link(last)
                    for h in range(H):
                        last = V.max_index(bpos[:, h, 8:16], best[:, h, 8:16], cand2[:, h, :])
                    link(last)
                elif part == 2:
                    link(V.tensor_copy(gsm[:, 0, :], best[:, :, 0]))
                    tt(best[:, :, :], best[:, :, :], bc(gsm[:, 0, :], PK, 2), ALU.subtract).then_inc(s["best_ready"], 1)
                    pos = bpos[:, :, :]
                    ts(apos[:, 0, :, :], pos, 4, None, ALU.logical_shift_right)
                    ts(apos[:, 1, :, :], pos, 15, None, ALU.bitwise_and)
                    ts(apos[:, 2, :, :], pos, 2, None, ALU.logical_shift_right)
                    ts(apos[:, 3, :, :], pos, 3, None, ALU.bitwise_and)
                    link(V.tensor_copy(low[:, :, :], pos))
                    V.tensor_copy(afl[:, :, :, :], apos[:, :, :, :])
                    link(ts(low[:, :, :], low[:, :, :], 64.0, None, ALU.is_lt))
                    link(ts(afl[:, 2, :, :], afl[:, 2, :, :], PK - 4.0, None, ALU.subtract))
                    link(tt(afl[:, 0:2, :, :], afl[:, 0:2, :, :], afl[:, 2:4, :, :], ALU.subtract))
                    link(tt(afl[:, 0:2, :, :], afl[:, 0:2, :, :], bc(low[:, :, :], 2, 1), ALU.mult))
                    link(tt(afl[:, 0:2, :, :], afl[:, 0:2, :, :], afl[:, 2:4, :, :], ALU.add))
                else:
                    p, place = ((0, 1), (1, 0))[part - 3]
                    if p == 0 and t:
                        dve.wait_ge(s["selT_mm"], t)
                    io4 = bc(bc(iota[:, 0:PK], PK, 1), H, 1)
                    link(tt(pick[:, :, :, :], io4, b4(afl[:, p, :, :], 3), ALU.is_equal))
                    link(tt(pick[:, :, :, :], pick[:, :, :, :], b4(side(topf, t, p), 2), ALU.mult))
                    link(V.reduce_sum(sel[:, place, :, :], pick[:, :, :, :], AX.X))
                    if p:
                        dve.wait_ge(s["gexp2_ready"], t + 1)
                        link(V.reduce_sum(gsm[:, 1, :], best[:, :, :], AX.X))
                        link(V.reciprocal(gsm[:, 1, :], gsm[:, 1, :]))
                        tt(sel[:, 2, :, :], best[:, :, :], bc(gsm[:, 1, :], PK, 2), ALU.mult).then_inc(s["sel_ready"], 1)

            def take_choice(t):
                dve.wait_ge(s["selT_mm"], t + 1)
                cols = slice(t * P, (t + 1) * P)
                V.tensor_copy(jT[:, cols], ps[:, 6, 0:P])
                V.tensor_copy(iT[:, cols], ps[:, 6, P:2 * P])
                gates = ps[:, 6, 2 * P:3 * P]
                link(ts(gate_hi[:, cols], gates, GSCALE, None, ALU.mult))
                stt(gate_lo[:, cols], gates, GSCALE, gate_hi[:, cols], ALU.mult, ALU.subtract).then_inc(s["selT_taken"], 1)

            def onehots(g, slot, first=False, used=True):
                tok = lambda ap: bc(ap[:, bass.ds(g * GT, GT)], NK, 1)
                if used:
                    dve.wait_ge(s["spread_mm"], g - 1)
                if not first:
                    dve.wait_ge(s["onehot_ready"], g)
                tt(rowhot[:, :, :], iota8[:, :, :], tok(iT), ALU.is_equal).then_inc(s["rowhot_ready"], 1)
                tt(colhot[:, slot, :, :], iota8[:, :, :], tok(jT), ALU.is_equal)
                dve.wait_ge(s["rowhot_ready"], g + 1)
                tt(rowhi[:, slot, :, :], rowhot[:, :, :], tok(gate_hi), ALU.mult)
                tt(rowlo[:, slot, :, :], rowhot[:, :, :], tok(gate_lo), ALU.mult).then_inc(s["onehot_ready"], 1)

            def u_onehots(i, sl, used=True):
                j = i - LEAD
                onehots(2 * j + 1, 1, used=used)
                u_lo(1 - sl, i + 2)
                onehots(2 * j + 2, 0)

            def weigh(n, sl, slot, k, piece):
                dve.wait_ge(gate_loaded[slot], piece)
                a = act[:, bass.ds(n - 1 - base, 1), :].rearrange("p a b -> p (a b)")
                a3 = a.rearrange("p (g t) -> p g t", t=ST)
                tt(a3, a3, gring[:, slot, :, k, :], ALU.mult).then_inc(s["w_prod"], 1)
                dve.wait_ge(s["v_hi"], n)
                tt(opr_lo[:, sl, :], raw[:, sl, :], opr_hi[:, sl, :].bitcast(F32), ALU.subtract).then_inc(s["v_lo"], 1)
                dve.wait_ge(s["w_hi_ready"], n)
                tt(w_lo[:, sl, :], a, w_hi[:, sl, :].bitcast(F32), ALU.subtract).then_inc(s["w_ready"], 1)

            V.tensor_copy(iota8[:, :, :], bc(iota[:, :], GT, 2))
            base = pieces = 0
            for g, size in enumerate(GROUPS):
                u_lo(0, base + 1)
                if g == 0:
                    for i in range(LEAD):
                        u_lo(1 - i % 2, i + 2)
                        if i < LATE:
                            best_of_set(SETS - LATE + i)
                            continue
                        t, part = divmod(i - LATE, PARTS)
                        if (t, part) == (0, 0):
                            link(V.tensor_copy(topf[:, :, :, :].rearrange("p a b c -> p (a b c)"),
                                               topi[:, :, :, :].rearrange("p a b c -> p (a b c)")))
                        choose(t, part)
                        if t and part == 2:
                            take_choice(t - 1)
                        if t == 1 and part == 3:
                            link(V.nop())
                            onehots(0, 0, first=True, used=False)
                    take_choice(TT - 1)
                    dve.wait_ge(s["selT_taken"], TT)
                    u_onehots(LEAD, 0, used=False)
                    u_onehots(LEAD + 1, 1)
                    with dve.Fori(LEAD // 2 + 1, size // 2 - 1) as it:
                        for sl in range(2):
                            u_onehots(2 * it + sl, sl)
                    u_onehots(size - 2, 0)
                    onehots(NG - 1, 1)
                else:
                    u_lo(1, base + 2)
                    with dve.Fori(0, size // 2 - 1) as it:
                        for sl in range(2):
                            u_lo(sl, 2 * it + (base + 3 + sl))
                dve.wait_ge(s["act_ready"], base + size)
                for k in range(2 * CB):
                    if k >= 2:
                        dve.wait_ge(s["v_mm"], base + k - 1)
                    weigh(base + k + 1, k % 2, k // CB, k % CB, 16 * (pieces + 1))
                with dve.Fori(1, size // (2 * CB)) as it:
                    for k in range(2 * CB):
                        b = it * (2 * CB) + (base + k)
                        dve.wait_ge(s["v_mm"], b - 1)
                        weigh(b + 1, k % 2, k // CB, k % CB, 16 * it + 16 * (pieces + 1))
                base += size
                pieces += size // (2 * CB)
            dve.wait_ge(y_loaded, 48)
            for k in range(KD):
                tt(y0T[:, k, :], y0T[:, k, :], y1T[:, k, :], ALU.add).then_inc(s["ypre_ready"], 1)
            for k in range(KD):
                wait_y_bank(dve, 2, k)
                dve.wait_ge(s["ypre_ready"], k + 1)
                tt(y0T[:, k, :], y0T[:, k, :], ps[:, k, :], ALU.add).then_inc(s["y_copied"], 1)
            for u in range(2 * TT):
                hf, t = divmod(u, TT)
                dve.wait_ge(s["yT_mm"], u + 1)
                xs = xb[:, t, hf * 512:(hf + 1) * 512]
                tt(xs, xs, ps[:, u % 2, :], ALU.add).then_inc(s["y_added"], 1)

        @block.gpsimd
        def _(pool):
            link = linker(pool, s["pool_step"])
            G = nc.gpsimd
            ge, sel_ = ALU.is_ge, G.affine_select
            link(G.memset(ones[:, :], 1.0))
            link(G.memset(half_neg[:, :], -0.5))
            link(sel_(out=ident[:, :], in_=ones[:, :], pattern=[[-1, P]], base=0, channel_multiplier=1, compare_op=ALU.is_equal, fill=0.0))
            for t in range(TT):
                pool.wait_ge(s["meansq_ready"], t + 1)
                G.tensor_tensor(rs[:, t:t + 1], ss[:, t:t + 1], half_neg[:, 0:1], ALU.pow).then_inc(s["rstd_ready"], 1)
                if not t:
                    pool.wait_ge(s["pool_step"], 3)
                    G.nop().then_inc(s["consts_ready"], 1)
            for b in (2, 4, 8, 16, 32, 64):
                m = same[b][:, :].rearrange("p (n i) -> p n i", i=b)
                link(sel_(out=m, in_=ones[:, :].rearrange("p (n i) -> p n i", i=b), pattern=[[-b, P // b], [0, b]], base=0,
                          channel_multiplier=1, compare_op=ge, fill=0.0))
                link(sel_(out=m, in_=m, pattern=[[b, P // b], [0, b]], base=b - 1, channel_multiplier=-1, compare_op=ge, fill=0.0))
            link(sel_(out=causal[:, :], in_=same[64][:, :], pattern=[[1, P]], base=0, channel_multiplier=-1, compare_op=ge, fill=0.0))
            link(sel_(out=strict[:, :], in_=same[64][:, :], pattern=[[1, P]], base=-1, channel_multiplier=-1, compare_op=ge, fill=0.0))
            link(G.tensor_scalar(negmask[:, :], causal[:, :], -NEG, NEG, ALU.mult, ALU.add))
            for b in (1, 2, 4, 8, 16, 32):
                inner = ident if b == 1 else same[b]
                link(G.tensor_tensor(level[b][:, :], same[2 * b][:, :], inner[:, :], ALU.subtract))
                link(G.tensor_tensor(level[b][:, :], level[b][:, :], strict[:, :], ALU.mult))
            link(sel_(out=chunk_ones[:, 0, :], in_=ones[:, :], pattern=[[0, P]], base=CH - 1, channel_multiplier=-1, compare_op=ge, fill=0.0))
            link(sel_(out=chunk_ones[:, 1, :], in_=ones[:, :], pattern=[[0, P]], base=-CH, channel_multiplier=1, compare_op=ge, fill=0.0))
            link(G.iota(iota_i[:, :], pattern=[[1, P]], base=0, channel_multiplier=0))
            link(G.tensor_copy(iota[:, :], iota_i[:, :]))
            G.nop().then_inc(s["consts_ready"], 1)
            pool.wait_ge(s["gates_ready"], 1)
            def decay_mask(t):
                gt = gdec[:, t, :].rearrange("p (a b) -> p b a", b=2)
                for par in range(2):
                    last = G.tensor_tensor(gm[:, par, :, :], bc(causal[:, :], HP, 1), bc(gt[:, par, :], P, 2), ALU.mult)
                last.then_inc(s["gmask_ready"], 1)

            def norm_power(t):
                pool.wait_ge(s["gms_ready"], t + 1)
                G.tensor_tensor(rn[:, :], ms[:, :], half_neg[:, :], ALU.pow).then_inc(s["grn_ready"], 1)

            def out_power(t):
                pool.wait_ge(s["onsq_ready"], t + 1)
                G.tensor_tensor(orn[:, :], oms[:, :], half_neg[:, 0:H], ALU.pow).then_inc(s["onrs_ready"], 1)

            decay_mask(0)
            norm_power(0)
            pool.wait_ge(s["mms_ready"], 1)
            fl = lambda ap: ap[:, :, :].rearrange("p a b -> p (a b)")
            G.tensor_tensor(fl(rrs), fl(rss), half_neg[:, 0:2 * TT], ALU.pow).then_inc(s["mrs_ready"], 1)
            for t in range(TT):
                if t + 1 < TT:
                    pool.wait_ge(s["grow_mm"], t + 1)
                    decay_mask(t + 1)
                    norm_power(t + 1)
                if t:
                    out_power(t - 1)
            out_power(TT - 1)
            pool.drain().then_inc(s["gdn_over"], 1)
            pool.wait_ge(s["gdn_over"], 4)
            for t in range(TT):
                pool.wait_ge(s["mqms_ready"], t + 1)
                G.tensor_tensor(qrn[:, t % 2, :], qms[:, t % 2, :], half_neg[:, :], ALU.pow).then_inc(s["mqrs_ready"], 1)
            pool.drain().then_inc(s["mla_over"], 1)
            for t in range(TT):
                pool.wait_ge(s["ms2_ready"], t + 1)
                G.tensor_tensor(rs[:, t:t + 1], ss[:, t:t + 1], half_neg[:, 0:1], ALU.pow).then_inc(s["rs2_ready"], 1)
            pool.drain().then_inc(s["early_over"], 1)


_INS = ["x", "positions", "norm1_g", "w_in", "conv_w", "a_log", "dt_bias", "gdn_norm_g", "w_gdn_out", "cq_norm_g",
        "w_uq", "ckv_norm_g", "w_ukv", "q_norm_g", "k_norm_g", "w_mla_out", "w_o", "norm2_g", "w_pq", "sub_keys",
        "u_tab", "v_tab"]


def kernel(**inputs):
    import concourse.bacc as _bacc
    from concourse.bass_utils import run_bass_kernel_spmd as _run

    nc = _bacc.Bacc("TRN2", target_bir_lowering=False, num_devices=1)
    arrays, args = {}, []
    for name in _INS:
        a = np.ascontiguousarray(inputs[name])
        arrays[f"in_{name}_dram"] = a
        args.append(nc.dram_tensor(f"in_{name}_dram", a.shape, mybir.dt.from_np(a.dtype), kind="ExternalInput").ap())
    args.append(nc.dram_tensor("out_0_dram", (1, S, D), F32, kind="ExternalOutput").ap())
    build(nc, *args)
    r = _run(nc, [arrays], core_ids=[0])
    return r.results[0]["out_0_dram"]
```
